# Optimizing a Trainium2 kernel written in Bass

```python
import math
import jax, jax.numpy as jnp
from jax import lax
import numpy as np
import jax
import jax.numpy as jnp

D_MODEL = 1024
BATCH = 1
SEQ = 256
DEPTH = 2

EPS = 1e-6
D_FF = -(-8 * D_MODEL // (3 * 256)) * 256

POOL_WINDOWS = (2, 4, 8, 16)
POOL_WIDTH = D_MODEL // 2
POOL_GROUP = POOL_WIDTH // len(POOL_WINDOWS)

HGRN_HEADS = 4
HGRN_DK = 128
HGRN_DV = (D_MODEL // 2) // HGRN_HEADS
HGRN_CHUNK = 64
HGRN_KW = HGRN_HEADS * HGRN_DK
HGRN_VW = HGRN_HEADS * HGRN_DV

HYB_IN = POOL_WIDTH + 2 * HGRN_KW + 2 * HGRN_VW
HYB_OUT = POOL_WIDTH + HGRN_VW

DIL_GROUPS = ((128, 1), (512, 4), (2048, 16))
ATT_HEADS_PER_GROUP = 8
ATT_HEAD_DIM = 64
ATT_GROUP_WIDTH = ATT_HEADS_PER_GROUP * ATT_HEAD_DIM
N_ATT_HEADS = len(DIL_GROUPS) * ATT_HEADS_PER_GROUP
ATT_QKV = 3 * len(DIL_GROUPS) * ATT_GROUP_WIDTH
ATT_OUT = ATT_GROUP_WIDTH
REL_BUCKETS = 32
REL_MAX_DIST = 2048

N_HYB = (DEPTH + 1) // 2
N_ATT = DEPTH // 2


def rms_norm(x, gain):
    xf = x.astype(jnp.float32)
    y = xf * lax.rsqrt(jnp.mean(xf * xf, axis=-1, keepdims=True) + EPS)
    return (y * gain.astype(jnp.float32)).astype(x.dtype)

def t5_bucket(dist):
    max_exact = REL_BUCKETS // 2
    df = jnp.maximum(dist, 1).astype(jnp.float32)
    large = max_exact + (jnp.log(df / max_exact) / math.log(REL_MAX_DIST / max_exact)
                         * (REL_BUCKETS - max_exact)).astype(jnp.int32)
    large = jnp.minimum(large, REL_BUCKETS - 1)
    return jnp.where(dist < max_exact, dist, large)

def pool_mixer(u, w, scale):
    B, S, _ = u.shape
    uf = u.astype(jnp.float32)
    wmax = max(POOL_WINDOWS)
    cs = jnp.cumsum(uf, axis=1)
    cs_pad = jnp.pad(cs, ((0, 0), (wmax, 0), (0, 0)))
    pos = jnp.arange(S)
    diffs = []
    for gi, win in enumerate(POOL_WINDOWS):
        sl = slice(gi * POOL_GROUP, (gi + 1) * POOL_GROUP)
        window_sum = cs[:, :, sl] - cs_pad[:, wmax - win: wmax - win + S, sl]
        count = jnp.minimum(pos + 1, win).astype(jnp.float32)[None, :, None]
        diffs.append(window_sum / count - uf[:, :, sl])
    d = jnp.stack(diffs, axis=2)
    y = jnp.einsum('bsgc,gcd->bsgd', d, w.astype(jnp.float32)).reshape(B, S, POOL_WIDTH)
    return (y * scale.astype(jnp.float32)).astype(u.dtype)

def hgrn2_mixer(q_raw, f_raw, v_raw, g_raw, lb, out_gain):
    B, S, _ = q_raw.shape
    H, K, V, C = HGRN_HEADS, HGRN_DK, HGRN_DV, HGRN_CHUNK
    n = S // C
    q = jax.nn.silu(q_raw.astype(jnp.float32)).reshape(B, S, H, K)
    z = f_raw.astype(jnp.float32).reshape(B, S, H, K)
    lb = lb.astype(jnp.float32).reshape(H, K)
    log_f = jnp.logaddexp(jnp.log(lb), jnp.log1p(-lb) + jax.nn.log_sigmoid(z))
    k = (1.0 - lb) * jax.nn.sigmoid(-z)
    v = v_raw.astype(jnp.float32).reshape(B, S, H, V)

    def chunks(t):
        return t.reshape(B, n, C, H, t.shape[-1]).transpose(1, 0, 3, 2, 4)

    qc, kc, vc, lfc = chunks(q), chunks(k), chunks(v), chunks(log_f)
    bc = jnp.cumsum(lfc, axis=3)
    causal = jnp.tril(jnp.ones((C, C), dtype=bool))

    def step(state, inp):
        qt, kt, vt, bt = inp
        b_last = bt[:, :, -1:, :]
        o_inter = jnp.einsum('bhtk,bhkv->bhtv', qt * jnp.exp(bt), state)
        rel = jnp.where(causal[:, :, None], bt[:, :, :, None, :] - bt[:, :, None, :, :], -jnp.inf)
        a = jnp.einsum('bhtsk,bhsk->bhts', qt[:, :, :, None, :] * jnp.exp(rel), kt)
        o_intra = jnp.einsum('bhts,bhsv->bhtv', a, vt)
        k_dec = kt * jnp.exp(b_last - bt)
        state = (jnp.exp(b_last[:, :, 0, :, None]) * state
                 + jnp.einsum('bhsk,bhsv->bhkv', k_dec, vt))
        return state, o_inter + o_intra

    state0 = jnp.zeros((B, H, K, V), jnp.float32)
    _, o = lax.scan(step, state0, (qc, kc, vc, bc))
    o = o.transpose(1, 0, 3, 2, 4).reshape(B, S, H, V)
    o = rms_norm(o, out_gain) * jax.nn.silu(g_raw.astype(jnp.float32).reshape(B, S, H, V))
    return o.reshape(B, S, HGRN_VW).astype(q_raw.dtype)

def _to_strided(t, dil, blk):
    B, S, H, E = t.shape
    L = S // dil
    nb = -(-L // blk)
    t = t.reshape(B, L, dil, H, E).transpose(0, 2, 1, 3, 4)
    t = jnp.pad(t, ((0, 0), (0, 0), (0, nb * blk - L), (0, 0), (0, 0)))
    return t.reshape(B, dil, nb, blk, H, E)

def _from_strided(t, S):
    B, dil, nb, blk = t.shape[:4]
    tail = t.shape[4:]
    L = S // dil
    t = t.reshape(B, dil, nb * blk, *tail)[:, :, :L]
    return jnp.moveaxis(t, 1, 2).reshape(B, S, *tail)

def dilated_group_attention(q, k, v, win, dil, bias_table):
    S = q.shape[1]
    blk = win // dil
    qs = _to_strided(q * ATT_HEAD_DIM ** -0.5, dil, blk)
    ks = _to_strided(k, dil, blk)
    vs = _to_strided(v, dil, blk)
    nb = qs.shape[2]

    def with_prev(t):
        prev = jnp.pad(t[:, :, :-1], ((0, 0), (0, 0), (1, 0), (0, 0), (0, 0), (0, 0)))
        return jnp.concatenate([prev, t], axis=3)

    kk, vv = with_prev(ks), with_prev(vs)
    qi = jnp.arange(blk)[:, None]
    ki = jnp.arange(2 * blk)[None, :]
    dist = blk + qi - ki
    band = (dist >= 0) & (dist <= blk)
    bias = bias_table[t5_bucket(jnp.maximum(dist, 0) * dil)].astype(jnp.float32).transpose(2, 0, 1)
    has_prev = (jnp.arange(nb) > 0)[:, None, None] | (ki >= blk)[None]
    mask = band[None] & has_prev
    s = jnp.einsum('brnqhe,brnkhe->brnhqk', qs, kk) + bias
    s = jnp.where(mask[None, None, :, None], s, -jnp.inf)
    m = jnp.max(s, axis=-1, keepdims=True)
    p = jnp.exp(s - m)
    l = jnp.sum(p, axis=-1, keepdims=True)
    mt = jnp.moveaxis(m, 3, 4)
    lt = jnp.moveaxis(l, 3, 4)
    o = jnp.einsum('brnhqk,brnkhe->brnqhe', p, vv) / lt
    return _from_strided(o, S), _from_strided(mt, S), _from_strided(lt, S)

def dilated_attention_mixer(qkv, rel_bias):
    B, S, _ = qkv.shape
    G, Hg = len(DIL_GROUPS), ATT_HEADS_PER_GROUP
    t = qkv.astype(jnp.float32).reshape(B, S, 3, G, Hg, ATT_HEAD_DIM)
    outs, maxes, dens = [], [], []
    for gi, (win, dil) in enumerate(DIL_GROUPS):
        o, m, l = dilated_group_attention(t[:, :, 0, gi], t[:, :, 1, gi], t[:, :, 2, gi], win, dil,
                                          rel_bias[:, gi * Hg:(gi + 1) * Hg])
        outs.append(o)
        maxes.append(m)
        dens.append(l)
    o_all = jnp.stack(outs)
    m_all = jnp.stack(maxes)
    l_all = jnp.stack(dens)
    w = l_all * jnp.exp(m_all - jnp.max(m_all, axis=0, keepdims=True))
    o = jnp.sum(w * o_all, axis=0) / jnp.sum(w, axis=0)
    return o.reshape(B, S, ATT_OUT).astype(qkv.dtype)

def swiglu(h, w_in, w_out):
    a, b = jnp.split(h @ w_in, 2, axis=-1)
    return (jax.nn.silu(a) * b) @ w_out

def modulation(c, w, b):
    return jnp.split(jax.nn.silu(c) @ w + b, 3, axis=-1)

def sandwich(x, mod, g_pre, g_post, fn):
    shift, scale, gate = mod
    h = rms_norm(x, g_pre) * (1.0 + scale[:, None]) + shift[:, None]
    return x + gate[:, None] * rms_norm(fn(h), g_post)

def first_inputs(seed: int = 0) -> dict:
    key = jax.random.key(seed)
    ks = jax.random.split(key, 17)

    def nrm(k, shape, scale):
        return jax.random.normal(k, shape, jnp.float32) * scale

    D = D_MODEL
    return {
        'x': nrm(ks[0], (BATCH, SEQ, D), 1.0),
        'c': nrm(ks[1], (BATCH, D), 1.0),
        'ada_w': nrm(ks[2], (DEPTH, 2, D, 3 * D), D ** -0.5),
        'ada_b': nrm(ks[3], (DEPTH, 2, 3 * D), 0.01),
        'norm_pre': 1.0 + nrm(ks[4], (DEPTH, 2, D), 0.1),
        'norm_post': 1.0 + nrm(ks[5], (DEPTH, 2, D), 0.1),
        'ffn_w_in': nrm(ks[6], (DEPTH, D, 2 * D_FF), D ** -0.5),
        'ffn_w_out': nrm(ks[7], (DEPTH, D_FF, D), D_FF ** -0.5),
        'hyb_w_in': nrm(ks[8], (N_HYB, D, HYB_IN), D ** -0.5),
        'hyb_w_out': nrm(ks[9], (N_HYB, HYB_OUT, D), HYB_OUT ** -0.5),
        'pool_w': nrm(ks[10], (N_HYB, len(POOL_WINDOWS), POOL_GROUP, POOL_GROUP), POOL_GROUP ** -0.5),
        'pool_scale': 1.0 + nrm(ks[11], (N_HYB, POOL_WIDTH), 0.1),
        'hgrn_lb_logits': nrm(ks[12], (N_HYB, HGRN_KW), 1.0),
        'hgrn_out_norm': 1.0 + nrm(ks[13], (N_HYB, HGRN_DV), 0.1),
        'att_w_qkv': nrm(ks[14], (N_ATT, D, ATT_QKV), D ** -0.5),
        'att_w_out': nrm(ks[15], (N_ATT, ATT_OUT, D), ATT_OUT ** -0.5),
        'rel_bias': nrm(ks[16], (REL_BUCKETS, N_ATT_HEADS), 0.5),
    }

def first_block(x, c, ada_w, ada_b, norm_pre, norm_post, ffn_w_in, ffn_w_out, hyb_w_in, hyb_w_out,
              pool_w, pool_scale, hgrn_lb_logits, hgrn_out_norm, att_w_qkv, att_w_out, rel_bias):
    lb_cum = jnp.cumsum(jax.nn.softmax(hgrn_lb_logits.astype(jnp.float32), axis=0), axis=0)
    lower_bounds = jnp.maximum(lb_cum - lb_cum[:1], 0.0)
    split_at = [POOL_WIDTH, POOL_WIDTH + HGRN_KW, POOL_WIDTH + 2 * HGRN_KW, POOL_WIDTH + 2 * HGRN_KW + HGRN_VW]

    for layer in range(DEPTH):
        j = layer // 2
        if layer % 2 == 0:
            def mixer(h, j=j):
                u, qr, fr, vr, gr = jnp.split(h @ hyb_w_in[j], split_at, axis=-1)
                y = jnp.concatenate([pool_mixer(u, pool_w[j], pool_scale[j]),
                                     hgrn2_mixer(qr, fr, vr, gr, lower_bounds[j], hgrn_out_norm[j])], axis=-1)
                return y @ hyb_w_out[j]
        else:
            def mixer(h, j=j):
                return dilated_attention_mixer(h @ att_w_qkv[j], rel_bias) @ att_w_out[j]

        def ffn(h, l=layer):
            return swiglu(h, ffn_w_in[l], ffn_w_out[l])

        x = sandwich(x, modulation(c, ada_w[layer, 0], ada_b[layer, 0]), norm_pre[layer, 0], norm_post[layer, 0], mixer)
        x = sandwich(x, modulation(c, ada_w[layer, 1], ada_b[layer, 1]), norm_pre[layer, 1], norm_post[layer, 1], ffn)
    return x


D_MIX = D_MODEL
FOX_HEADS = 8
FOX_HEAD_DIM = 64
FOX_WIDTH = FOX_HEADS * FOX_HEAD_DIM
Q_BLOCK = 128
S5_WIDTH = D_MIX - FOX_WIDTH
S5_GROUP = 16
S5_GROUPS = S5_WIDTH // S5_GROUP
S5_STATE = 64
EVEN_IN = 3 * FOX_WIDTH + FOX_HEADS + S5_WIDTH
MLSTM_HEADS = 8
MLSTM_HEAD_DIM = D_MIX // MLSTM_HEADS
MLSTM_CHUNK = 64
CONV_WIDTH = 4
ODD_IN = 4 * D_MIX + 2 * MLSTM_HEADS
N_GROUPS = 4
EXPERTS_PER_GROUP = 4
N_EXPERTS = N_GROUPS * EXPERTS_PER_GROUP
EXPERT_TOP_K = 2
D_EXPERT = 256
DN_ALPHA = (2 * DEPTH) ** 0.25
DN_BETA = (8 * DEPTH) ** -0.25
N_EVEN = (DEPTH + 1) // 2
N_ODD = DEPTH // 2
LN_EPS = 1e-5


def layer_norm(x, g, b):
    xf = x.astype(jnp.float32)
    mu = jnp.mean(xf, axis=-1, keepdims=True)
    var = jnp.mean(jnp.square(xf - mu), axis=-1, keepdims=True)
    y = (xf - mu) * lax.rsqrt(var + LN_EPS) * g.astype(jnp.float32) + b.astype(jnp.float32)
    return y.astype(x.dtype)

def forgetting_attention(q, k, v, f_logit):
    B, S, H, Dh = q.shape
    nb = S // Q_BLOCK
    c = jnp.cumsum(jax.nn.log_sigmoid(f_logit.astype(jnp.float32)), axis=1).transpose(0, 2, 1)
    qh = q.transpose(0, 2, 1, 3)
    kh = k.transpose(0, 2, 1, 3)
    vh = v.transpose(0, 2, 1, 3)
    q_blocks = qh.reshape(B, H, nb, Q_BLOCK, Dh).transpose(2, 0, 1, 3, 4)
    c_blocks = c.reshape(B, H, nb, Q_BLOCK).transpose(2, 0, 1, 3)
    pos_k = jnp.arange(S)
    scale = Dh ** -0.5

    def one_block(args):
        qb, cb, i = args
        s = jnp.einsum('bhqd,bhkd->bhqk', qb, kh).astype(jnp.float32) * scale
        s = s + cb[..., :, None] - c[..., None, :]
        pos_q = i * Q_BLOCK + jnp.arange(Q_BLOCK)
        mask = pos_k[None, :] <= pos_q[:, None]
        s = jnp.where(mask, s, -jnp.inf)
        p = jax.nn.softmax(s, axis=-1).astype(vh.dtype)
        return jnp.einsum('bhqk,bhkd->bhqd', p, vh)

    out = lax.map(one_block, (q_blocks, c_blocks, jnp.arange(nb)))
    return out.transpose(1, 0, 3, 2, 4).reshape(B, S, H, Dh)

def s5_scan(u, a_re, a_im, log_dt, b_re, b_im, c_re, c_im, d_skip):
    dt = jnp.exp(log_dt)[:, None]
    mag = jnp.exp(a_re * dt)
    lb_re = mag * jnp.cos(a_im * dt)
    lb_im = mag * jnp.sin(a_im * dt)
    num_re = lb_re - 1.0
    num_im = lb_im
    den = a_re * a_re + a_im * a_im
    z_re = (num_re * a_re + num_im * a_im) / den
    z_im = (num_im * a_re - num_re * a_im) / den
    bb_re = z_re[..., None] * b_re - z_im[..., None] * b_im
    bb_im = z_re[..., None] * b_im + z_im[..., None] * b_re
    bu_re = jnp.einsum('bsgc,gpc->bsgp', u, bb_re)
    bu_im = jnp.einsum('bsgc,gpc->bsgp', u, bb_im)
    a_re_t = jnp.broadcast_to(lb_re, bu_re.shape)
    a_im_t = jnp.broadcast_to(lb_im, bu_im.shape)

    def combine(e1, e2):
        a1r, a1i, b1r, b1i = e1
        a2r, a2i, b2r, b2i = e2
        return (a2r * a1r - a2i * a1i,
                a2r * a1i + a2i * a1r,
                a2r * b1r - a2i * b1i + b2r,
                a2r * b1i + a2i * b1r + b2i)

    _, _, h_re, h_im = lax.associative_scan(combine, (a_re_t, a_im_t, bu_re, bu_im), axis=1)
    y = jnp.einsum('bsgp,gcp->bsgc', h_re, c_re) - jnp.einsum('bsgp,gcp->bsgc', h_im, c_im)
    return y + d_skip * u

def causal_dwconv(x, w, b):
    C = x.shape[-1]
    y = lax.conv_general_dilated(x, w[:, None, :], window_strides=(1,), padding=[(CONV_WIDTH - 1, 0)],
                                 dimension_numbers=('NWC', 'WIO', 'NWC'), feature_group_count=C)
    return y + b

def mlstm_chunkwise(q, k, v, i_pre, f_pre):
    B, S, H, Dh = q.shape
    L = MLSTM_CHUNK
    NC = S // L
    f32 = jnp.float32

    def to_chunks(t):
        return t.reshape(B, NC, L, H, Dh).transpose(0, 3, 1, 2, 4)

    qc = to_chunks(q)
    kc = to_chunks(k * (Dh ** -0.5))
    vc = to_chunks(v)
    log_i = i_pre.astype(f32).reshape(B, NC, L, H).transpose(0, 3, 1, 2)
    log_f = jax.nn.log_sigmoid(f_pre.astype(f32)).reshape(B, NC, L, H).transpose(0, 3, 1, 2)
    bcum = jnp.cumsum(log_f, axis=-1)
    b_last = bcum[..., -1]
    g = b_last[..., None] - bcum + log_i
    m_loc = jnp.max(g, axis=-1)

    def step(carry, inp):
        Cm, nv, m = carry
        k_n, v_n, g_n, bl_n, ml_n = inp
        m_new = jnp.maximum(bl_n + m, ml_n)
        decay = jnp.exp(bl_n + m - m_new)
        w = jnp.exp(g_n - m_new[..., None])
        C_new = decay[..., None, None] * Cm + jnp.einsum('bhld,bhle->bhde', v_n * w[..., None], k_n)
        n_new = decay[..., None] * nv + jnp.einsum('bhl,bhle->bhe', w, k_n)
        return (C_new, n_new, m_new), (Cm, nv, m)

    init = (jnp.zeros((B, H, Dh, Dh), f32), jnp.zeros((B, H, Dh), f32), jnp.zeros((B, H), f32))
    xs = (kc.transpose(2, 0, 1, 3, 4), vc.transpose(2, 0, 1, 3, 4), g.transpose(2, 0, 1, 3),
          b_last.transpose(2, 0, 1), m_loc.transpose(2, 0, 1))
    _, (C_prev, n_prev, m_prev) = lax.scan(step, init, xs)
    C_prev = C_prev.transpose(1, 2, 0, 3, 4)
    n_prev = n_prev.transpose(1, 2, 0, 3)
    m_prev = m_prev.transpose(1, 2, 0)

    causal = jnp.tril(jnp.ones((L, L), dtype=bool))
    log_D = bcum[..., :, None] - bcum[..., None, :] + log_i[..., None, :]
    log_D = jnp.where(causal, log_D, -jnp.inf)
    m_inter = bcum + m_prev[..., None]
    m_t = jnp.maximum(m_inter, jnp.max(log_D, axis=-1))
    Dmat = jnp.exp(log_D - m_t[..., None])
    s = jnp.einsum('bhnld,bhnjd->bhnlj', qc, kc) * Dmat
    inter_scale = jnp.exp(m_inter - m_t)
    num = jnp.einsum('bhnlj,bhnjd->bhnld', s, vc) + inter_scale[..., None] * jnp.einsum('bhnvk,bhnlk->bhnlv', C_prev, qc)
    den = jnp.sum(s, axis=-1) + inter_scale * jnp.einsum('bhnk,bhnlk->bhnl', n_prev, qc)
    h = num / jnp.maximum(jnp.abs(den), jnp.exp(-m_t))[..., None]
    return h.transpose(0, 2, 3, 1, 4).reshape(B, S, H, Dh).astype(v.dtype)

def fox_s5_mixer(x, w_in, f_bias, a_re, a_im, log_dt, b_re, b_im, c_re, c_im, d_skip, w_glu, b_glu, w_out):
    B, S, _ = x.shape
    z = x @ w_in
    q, k, v, f_logit, u = jnp.split(z, [FOX_WIDTH, 2 * FOX_WIDTH, 3 * FOX_WIDTH, 3 * FOX_WIDTH + FOX_HEADS], axis=-1)
    shp = (B, S, FOX_HEADS, FOX_HEAD_DIM)
    att = forgetting_attention(q.reshape(shp), k.reshape(shp), v.reshape(shp), f_logit + f_bias)
    att = att.reshape(B, S, FOX_WIDTH)
    y = s5_scan(u.reshape(B, S, S5_GROUPS, S5_GROUP), a_re, a_im, log_dt, b_re, b_im, c_re, c_im, d_skip)
    y = jax.nn.gelu(y.reshape(B, S, S5_WIDTH))
    y = y * jax.nn.sigmoid(y @ w_glu + b_glu)
    return jnp.concatenate([att, y], axis=-1) @ w_out

def mlstm_mixer(x, w_in, conv_w, conv_b, i_bias, f_bias, w_out):
    B, S, _ = x.shape
    z = x @ w_in
    qk, v, o, i_pre, f_pre = jnp.split(z, [2 * D_MIX, 3 * D_MIX, 4 * D_MIX, 4 * D_MIX + MLSTM_HEADS], axis=-1)
    qk = jax.nn.silu(causal_dwconv(qk, conv_w, conv_b))
    q, k = jnp.split(qk, 2, axis=-1)
    shp = (B, S, MLSTM_HEADS, MLSTM_HEAD_DIM)
    h = mlstm_chunkwise(q.reshape(shp), k.reshape(shp), v.reshape(shp), i_pre + i_bias, f_pre + f_bias)
    h = h.reshape(B, S, D_MIX) * jax.nn.sigmoid(o)
    return h @ w_out

def hier_moe(x, w_group, b_group, w_expert, b_expert, w_gate, w_up, w_down):
    B, S, D = x.shape
    t = x.reshape(B * S, D)
    g_prob = jax.nn.softmax((t @ w_group + b_group).astype(jnp.float32), axis=-1)
    g_val, g_idx = lax.top_k(g_prob, 1)
    e_all = jnp.einsum('td,gde->tge', t, w_expert) + b_expert
    e_logits = jnp.take_along_axis(e_all, g_idx[:, :, None], axis=1)[:, 0]
    e_prob = jax.nn.softmax(e_logits.astype(jnp.float32), axis=-1)
    e_val, e_idx = lax.top_k(e_prob, EXPERT_TOP_K)
    e_val = e_val / jnp.sum(e_val, axis=-1, keepdims=True)
    weights = g_val * e_val
    expert_id = g_idx * EXPERTS_PER_GROUP + e_idx
    combine = jnp.einsum('tk,tke->te', weights, jax.nn.one_hot(expert_id, N_EXPERTS, dtype=jnp.float32))
    hid = jax.nn.silu(jnp.einsum('td,edf->tef', t, w_gate)) * jnp.einsum('td,edf->tef', t, w_up)
    hid = hid * combine.astype(hid.dtype)[:, :, None]
    out = jnp.einsum('tef,efd->td', hid, w_down)
    return out.reshape(B, S, D)

def second_inputs(seed: int = 0) -> dict:
    key = jax.random.key(seed)
    ks = iter(jax.random.split(key, 48))
    f32 = jnp.float32

    def nrm(shape, scale):
        return jax.random.normal(next(ks), shape, f32) * scale

    x = nrm((BATCH, SEQ, D_MODEL), 1.0)
    ln_g = 1.0 + nrm((DEPTH, 2, D_MODEL), 0.01)
    ln_b = nrm((DEPTH, 2, D_MODEL), 0.01)
    even_w_in = nrm((N_EVEN, D_MODEL, EVEN_IN), D_MODEL ** -0.5)
    fox_f_bias = jnp.linspace(2.0, 5.0, FOX_HEADS, dtype=f32)[None, :] + nrm((N_EVEN, FOX_HEADS), 0.1)
    s5_a_re = -0.5 + nrm((N_EVEN, S5_GROUPS, S5_STATE), 0.01)
    s5_a_im = jnp.pi * jnp.arange(S5_STATE, dtype=f32)[None, None, :] + nrm((N_EVEN, S5_GROUPS, S5_STATE), 0.01)
    s5_log_dt = jax.random.uniform(next(ks), (N_EVEN, S5_GROUPS), f32, minval=math.log(1e-3), maxval=math.log(1e-1))
    s5_b_re = nrm((N_EVEN, S5_GROUPS, S5_STATE, S5_GROUP), (2 * S5_GROUP) ** -0.5)
    s5_b_im = nrm((N_EVEN, S5_GROUPS, S5_STATE, S5_GROUP), (2 * S5_GROUP) ** -0.5)
    s5_c_re = nrm((N_EVEN, S5_GROUPS, S5_GROUP, S5_STATE), S5_STATE ** -0.5)
    s5_c_im = nrm((N_EVEN, S5_GROUPS, S5_GROUP, S5_STATE), S5_STATE ** -0.5)
    s5_d = nrm((N_EVEN, S5_GROUPS, S5_GROUP), 1.0)
    s5_w_glu = nrm((N_EVEN, S5_WIDTH, S5_WIDTH), S5_WIDTH ** -0.5)
    s5_b_glu = nrm((N_EVEN, S5_WIDTH), 0.01)
    even_w_out = nrm((N_EVEN, D_MIX, D_MODEL), D_MIX ** -0.5 * DN_BETA)
    odd_w_in = nrm((N_ODD, D_MODEL, ODD_IN), D_MODEL ** -0.5)
    mlstm_conv_w = nrm((N_ODD, CONV_WIDTH, 2 * D_MIX), CONV_WIDTH ** -0.5)
    mlstm_conv_b = nrm((N_ODD, 2 * D_MIX), 0.01)
    mlstm_i_bias = nrm((N_ODD, MLSTM_HEADS), 0.1)
    mlstm_f_bias = jnp.linspace(3.0, 6.0, MLSTM_HEADS, dtype=f32)[None, :] + nrm((N_ODD, MLSTM_HEADS), 0.01)
    odd_w_out = nrm((N_ODD, D_MIX, D_MODEL), D_MIX ** -0.5 * DN_BETA)
    moe_w_group = nrm((DEPTH, D_MODEL, N_GROUPS), D_MODEL ** -0.5)
    moe_b_group = nrm((DEPTH, N_GROUPS), 0.01)
    moe_w_expert = nrm((DEPTH, N_GROUPS, D_MODEL, EXPERTS_PER_GROUP), D_MODEL ** -0.5)
    moe_b_expert = nrm((DEPTH, N_GROUPS, EXPERTS_PER_GROUP), 0.01)
    moe_w_gate = nrm((DEPTH, N_EXPERTS, D_MODEL, D_EXPERT), D_MODEL ** -0.5)
    moe_w_up = nrm((DEPTH, N_EXPERTS, D_MODEL, D_EXPERT), D_MODEL ** -0.5)
    moe_w_down = nrm((DEPTH, N_EXPERTS, D_EXPERT, D_MODEL), D_EXPERT ** -0.5 * DN_BETA)
    return {'x': x, 'ln_g': ln_g, 'ln_b': ln_b,
            'even_w_in': even_w_in, 'fox_f_bias': fox_f_bias,
            's5_a_re': s5_a_re, 's5_a_im': s5_a_im, 's5_log_dt': s5_log_dt,
            's5_b_re': s5_b_re, 's5_b_im': s5_b_im, 's5_c_re': s5_c_re, 's5_c_im': s5_c_im,
            's5_d': s5_d, 's5_w_glu': s5_w_glu, 's5_b_glu': s5_b_glu, 'even_w_out': even_w_out,
            'odd_w_in': odd_w_in, 'mlstm_conv_w': mlstm_conv_w, 'mlstm_conv_b': mlstm_conv_b,
            'mlstm_i_bias': mlstm_i_bias, 'mlstm_f_bias': mlstm_f_bias, 'odd_w_out': odd_w_out,
            'moe_w_group': moe_w_group, 'moe_b_group': moe_b_group,
            'moe_w_expert': moe_w_expert, 'moe_b_expert': moe_b_expert,
            'moe_w_gate': moe_w_gate, 'moe_w_up': moe_w_up, 'moe_w_down': moe_w_down}

def second_block(x, ln_g, ln_b, even_w_in, fox_f_bias, s5_a_re, s5_a_im, s5_log_dt, s5_b_re, s5_b_im,
              s5_c_re, s5_c_im, s5_d, s5_w_glu, s5_b_glu, even_w_out, odd_w_in, mlstm_conv_w,
              mlstm_conv_b, mlstm_i_bias, mlstm_f_bias, odd_w_out, moe_w_group, moe_b_group,
              moe_w_expert, moe_b_expert, moe_w_gate, moe_w_up, moe_w_down):
    h = x
    for layer in range(DEPTH):
        j = layer // 2
        if layer % 2 == 0:
            mix = fox_s5_mixer(h, even_w_in[j], fox_f_bias[j], s5_a_re[j], s5_a_im[j], s5_log_dt[j],
                               s5_b_re[j], s5_b_im[j], s5_c_re[j], s5_c_im[j], s5_d[j],
                               s5_w_glu[j], s5_b_glu[j], even_w_out[j])
        else:
            mix = mlstm_mixer(h, odd_w_in[j], mlstm_conv_w[j], mlstm_conv_b[j], mlstm_i_bias[j],
                              mlstm_f_bias[j], odd_w_out[j])
        h = layer_norm(DN_ALPHA * h + mix, ln_g[layer, 0], ln_b[layer, 0])
        ffn = hier_moe(h, moe_w_group[layer], moe_b_group[layer], moe_w_expert[layer], moe_b_expert[layer],
                       moe_w_gate[layer], moe_w_up[layer], moe_w_down[layer])
        h = layer_norm(DN_ALPHA * h + ffn, ln_g[layer, 1], ln_b[layer, 1])
    return h


def setup_inputs(seed=0):
    out = dict(first_inputs(seed))
    for name, value in second_inputs(seed + 1).items():
        if name != "x":
            out[name + "_2"] = value
    return out


def reference(
    x, c, ada_w, ada_b, norm_pre, norm_post, ffn_w_in, ffn_w_out, hyb_w_in, hyb_w_out, pool_w,
    pool_scale, hgrn_lb_logits, hgrn_out_norm, att_w_qkv, att_w_out, rel_bias, ln_g_2, ln_b_2,
    even_w_in_2, fox_f_bias_2, s5_a_re_2, s5_a_im_2, s5_log_dt_2, s5_b_re_2, s5_b_im_2,
    s5_c_re_2, s5_c_im_2, s5_d_2, s5_w_glu_2, s5_b_glu_2, even_w_out_2, odd_w_in_2,
    mlstm_conv_w_2, mlstm_conv_b_2, mlstm_i_bias_2, mlstm_f_bias_2, odd_w_out_2, moe_w_group_2,
    moe_b_group_2, moe_w_expert_2, moe_b_expert_2, moe_w_gate_2, moe_w_up_2, moe_w_down_2,
):
    x = first_block(
        x, c, ada_w, ada_b, norm_pre, norm_post, ffn_w_in, ffn_w_out, hyb_w_in, hyb_w_out,
        pool_w, pool_scale, hgrn_lb_logits, hgrn_out_norm, att_w_qkv, att_w_out, rel_bias,
    )
    return second_block(
        x, ln_g_2, ln_b_2, even_w_in_2, fox_f_bias_2, s5_a_re_2, s5_a_im_2, s5_log_dt_2,
        s5_b_re_2, s5_b_im_2, s5_c_re_2, s5_c_im_2, s5_d_2, s5_w_glu_2, s5_b_glu_2,
        even_w_out_2, odd_w_in_2, mlstm_conv_w_2, mlstm_conv_b_2, mlstm_i_bias_2,
        mlstm_f_bias_2, odd_w_out_2, moe_w_group_2, moe_b_group_2, moe_w_expert_2,
        moe_b_expert_2, moe_w_gate_2, moe_w_up_2, moe_w_down_2,
    )


_drawn_inputs = setup_inputs


def setup_inputs(seed=0):
    import zlib

    import numpy as np

    out = dict(_drawn_inputs(seed))
    spreads = {}
    factors = {'s5_a_re_2': 64.0,
     's5_a_im_2': 33.464,
     's5_log_dt_2': 41.136,
     's5_b_re_2': 40.496,
     's5_b_im_2': 38.424,
     's5_c_re_2': 51.176,
     's5_c_im_2': 43.112,
     's5_b_glu_2': 52.529,
     'mlstm_conv_b_2': 27.375,
     'mlstm_i_bias_2': 36.987,
     'moe_b_group_2': 22.079,
     'moe_b_expert_2': 26.955}
    for name, (base, spread) in spreads.items():
        noise = np.random.default_rng([zlib.crc32(name.encode()), seed]).standard_normal(out[name].shape)
        drawn = base * np.exp(spread * noise) if base else spread * noise
        out[name] = jnp.asarray(drawn.astype(out[name].dtype))
    for name, factor in factors.items():
        out[name] = (out[name] * factor).astype(out[name].dtype)
    return out
```

```python
import math
from contextlib import ExitStack

import numpy as np
import concourse.bass as bass
from concourse import mybir

ALU = mybir.AluOpType
ACTF = mybir.ActivationFunctionType
F32 = mybir.dt.float32
I32 = mybir.dt.int32
AX = mybir.AxisListType

P = 128
S = 256
D = 1024
NEG = -1.0e30
NF = 11
NSLOT = 8
ARENA = 22528
RSQRT_SEED = float(0x5F3759DF)
DN_ALPHA = 4.0 ** 0.25
TWO_PI = 2.0 * math.pi
ROUND = 1.5 * 2.0 ** 23

PARAM_COLS = [
    ("c", 8), ("npre", 32), ("npost", 32), ("adab", 96), ("pscale", 4), ("lbl", 4), ("onorm", 1),
    ("lng", 32), ("lnb", 32), ("are", 16), ("aim", 16), ("ldt", 16), ("s5d", 4), ("bglu", 4),
    ("convw", 64), ("convb", 16), ("rb", 40), ("fb", 3), ("bre", 256), ("bim", 256),
    ("cre", 256), ("cim", 256), ("wr", 320),
]
CONST_COLS = [("ident", 128), ("onesd", 128), ("causal", 128), ("hm", 896), ("hsel", 16), ("tt", 256),
              ("half", 2), ("firsts", 4)]
AUX_COLS = [("invc", 1024), ("onehot", 384), ("maskv", 384), ("relb", 24)]


def offsets(cols):
    out, at = {}, 0
    for name, n in cols:
        out[name] = (at, n)
        at += n
    return out, at


PO, PN = offsets(PARAM_COLS)
CO, CN = offsets(CONST_COLS)
AO, AN = offsets(AUX_COLS)


class Queue:

    def __init__(self, name, sem, link):
        self.name, self.sem, self.link = name, sem, link
        self.ops, self.n, self.seen, self.extra, self.open = [], 0, {}, [], False

    def last(self):
        assert not self.open
        return (self.name, self.sem, self.n)

    def do(self, fn, *waits, inc=True):
        todo = list(self.extra)
        self.extra = []
        if self.link and self.n:
            todo.append((self.name, self.sem, self.n))
        stack = list(waits)
        while stack:
            w = stack.pop()
            if w is None:
                continue
            if isinstance(w, list):
                stack.extend(w)
            else:
                todo.append(w)
        need = {}
        for name, sem, val in todo:
            if val > self.seen.get(name, 0):
                self.seen[name] = val
                need[name] = (sem, val)
        self.ops.append((list(need.values()), fn, inc))
        self.open = not inc
        if inc:
            self.n += 1
            return (self.name, self.sem, self.n)
        return None

    def emit(self, eng):
        for waits, fn, inc in self.ops:
            for sem, val in waits:
                eng.wait_ge(sem, val)
            ins = fn(eng)
            if inc:
                ins.then_inc(self.sem, 1)


class Slots:

    def __init__(self, n, base=0):
        self.n, self.base, self.i = n, base, 0
        self.free = [[] for _ in range(n)]

    def take(self, k=1):
        i = self.i
        if i % k:
            i += k - i % k
        i %= self.n
        self.i = (i + k) % self.n
        waits = []
        for j in range(i, i + k):
            assert self.free[j] is not None, "taken and not given back"
            waits += self.free[j]
            self.free[j] = None
        return self.base + i, waits

    def give(self, i, *toks, k=1):
        for j in range(i - self.base, i - self.base + k):
            assert self.free[j] is None
            self.free[j] = [t for t in toks if t is not None]


def build(nc, a, out):
    ctx = ExitStack()
    with ctx:
        def sb(name, cols):
            return ctx.enter_context(nc.sbuf_tensor(name, [P, cols], F32))

        def sem(name):
            return ctx.enter_context(nc.semaphore(name))

        PSA = ctx.enter_context(nc.psum_tensor("PSA", [P, 2048], F32))
        PSB = ctx.enter_context(nc.psum_tensor("PSB", [P, 2048], F32))
        XT = sb("XT", 2048)
        HT = sb("HT", 2048)
        T1 = sb("T1", 2048)
        T2 = sb("T2", 2048)
        RS = sb("RS", 1024)
        MC = sb("MC", 96)
        SM = sb("SM", 1024)
        CT = sb("CT", CN)
        PR = sb("PR", PN)
        WR = sb("WR", NSLOT * 2048)
        AR = sb("AR", ARENA)

        PE = Queue("pe", sem("s_pe"), False)
        ACT = Queue("act", sem("s_act"), True)
        DVE = Queue("dve", sem("s_dve"), True)
        POOL = Queue("pool", sem("s_pool"), True)
        SP = Queue("sp", sem("s_sp"), False)
        wsem = [sem(f"s_w{i}") for i in range(NSLOT)]
        wcnt = [0] * NSLOT
        s_in = sem("s_in")
        s_x = sem("s_x")
        s_bias = sem("s_bias")
        s_tp = sem("s_tp")
        s_out = sem("s_out")

        scratch = nc.dram_tensor("bias_rows", [24, 384], F32, kind="Internal")

        def par(name, a0=0, n=None, p=P):
            at, w = PO[name]
            n = w - a0 if n is None else n
            return PR[0:p, at + a0:at + a0 + n]

        def cst(name, a0=0, n=None, p=P):
            at, w = CO[name]
            n = w - a0 if n is None else n
            return CT[0:p, at + a0:at + a0 + n]

        ident = cst("ident")
        onesd = cst("onesd")

        W = Slots(NSLOT)
        PS = Slots(4)
        PT = Slots(2, base=6)

        def bank(b, lo=0, hi=512, p=P, p0=0):
            t = PSA if b < 4 else PSB
            o = (b % 4) * 512
            return t[p0:p0 + p, o + lo:o + hi]

        def wslot(i):
            return WR[:, i * 2048:(i + 1) * 2048]

        arena = [0]

        def take(n):
            at = arena[0]
            arena[0] += n
            assert arena[0] <= ARENA, arena[0]
            return AR[:, at:at + n]

        def fence():
            toks = [q.last() for q in (PE, ACT, DVE, POOL) if q.n]
            for q in (PE, ACT, DVE, POOL):
                q.extra = [t for t in toks if t[0] != q.name]
            arena[0] = 0

        def mm(o, l, r, start, stop, *waits, inc=False, skip=False):
            return PE.do(lambda e: e.matmul(o, l, r, start=start, stop=stop, skip_group_check=skip),
                         *waits, inc=inc)

        def tr(o, i, n, *waits, inc=False):
            return PE.do(lambda e: e.transpose(o, i, ident[0:n, 0:n]), *waits, inc=inc)

        def act(o, i, f, *waits, bias=0.0, scale=1.0, accum=None):
            if accum is None:
                return ACT.do(lambda e: e.activation(o, i, f, bias=bias, scale=scale), *waits)
            return ACT.do(lambda e: e.activation(o, i, f, bias=bias, scale=scale, accum_out=accum), *waits)

        def ts(o, i, s1, s2, op0, op1=None, *waits, q=None):
            q = q or DVE
            if op1 is None:
                return q.do(lambda e: e.tensor_scalar(o, i, s1, None, op0), *waits)
            return q.do(lambda e: e.tensor_scalar(o, i, s1, s2, op0, op1), *waits)

        def stt(o, i, s, j, op0, op1, *waits):
            return DVE.do(lambda e: e.scalar_tensor_tensor(out=o, in0=i, scalar=s, in1=j, op0=op0, op1=op1), *waits)

        def tt(o, i, j, op, *waits, q=None):
            q = q or DVE
            return q.do(lambda e: e.tensor_tensor(o, i, j, op), *waits)

        def cp(o, i, *waits, q=None):
            if q is ACT:
                return ACT.do(lambda e: e.copy(o, i), *waits)
            return (q or DVE).do(lambda e: e.tensor_copy(o, i), *waits)

        def scan(o, x, y, init, op0, op1, *waits):
            return DVE.do(lambda e: e.tensor_tensor_scan(o, x, y, init, op0, op1), *waits)

        def red(o, i, op, *waits):
            return DVE.do(lambda e: e.tensor_reduce(o, i, AX.X, op), *waits)

        def recip(o, i, *waits):
            return DVE.do(lambda e: e.reciprocal(o, i), *waits)

        def v3(ap, n):
            return ap.rearrange("p (a b) -> p a b", a=n)

        def v4(ap, n, m):
            return ap.rearrange("p (a b c) -> p a b c", a=n, b=m)

        def rep(ap, n):
            return ap.unsqueeze(1).to_broadcast([ap.shape[0], n, ap.shape[1]])

        def wide(ap, n):
            return ap.unsqueeze(2).to_broadcast([ap.shape[0], ap.shape[1], n])

        def row_of(e, k):
            return ident[0:k, e:e + 1].to_broadcast([k, P])

        def load(src, cols=2048, k=8, p=P):
            i, waits = W.take()
            dst = v3(wslot(i)[0:p, 0:cols], k) if k > 1 else wslot(i)[0:p, 0:cols]
            SP.do(lambda e: e.dma_start(dst, src).then_inc(wsem[i], 16), waits, inc=False)
            wcnt[i] += 16
            return i, dst, (f"w{i}", wsem[i], wcnt[i])

        def wk(m, c, n=256):
            return load(m[:, c:c + n].rearrange("(k p) n -> p k n", p=P), cols=8 * n)

        def wd(m, r):
            return load(m[r:r + 256, :].rearrange("(k p) n -> p k n", p=P), k=2)

        ht = v3(HT[:, :], 8)
        xt = v3(XT[:, :], 8)

        def fm(slot, htok, n=2, src=None):
            i, w, tok = slot
            x = ht if src is None else src
            nk = w.shape[1]
            b, waits = PS.take()
            for f in range(n):
                for k in range(nk):
                    t = mm(bank(b, f * 256, f * 256 + 256), w[:, k, f * P:(f + 1) * P], x[:, k, :],
                           k == 0, k == nk - 1, waits if f == k == 0 else None,
                           tok if f == k == 0 else None, htok[k] if f == 0 else None,
                           inc=(f == n - 1 and k == nk - 1))
            W.give(i, t)
            return b, t

        def tm(slot, htok):
            i, w, tok = slot
            b, waits = PS.take()
            for m in range(2):
                for k in range(8):
                    t = mm(bank(b, m * 256, m * 256 + 256), ht[:, k, m * P:(m + 1) * P], w[:, k, :],
                           k == 0, k == 7, waits, tok, htok[k], inc=(m == 1 and k == 7))
            W.give(i, t)
            return b, t

        acc_free = [[]]

        def down(slot, xs, first, last, *waits):
            i, w, tok = slot
            for k in range(2):
                for f in range(8):
                    o = bank(4 + f // 2, (f % 2) * 256, (f % 2) * 256 + 256)
                    st = first and k == 0 and f % 2 == 0
                    t = mm(o, w[:, k, f * P:(f + 1) * P], xs[k], st, last and k == 1, list(waits), tok,
                           acc_free[0] if first else None, inc=(k == 1 and f == 7), skip=True)
            W.give(i, t)
            return t

        yacc = v3(PSB[:, :], 8)

        V, Y, A_, B_ = (RS[:, i * 256:(i + 1) * 256] for i in range(4))

        def rsqrt(ps, eps, n, tok):
            v, y, t = V[0:n, :], Y[0:n, :], A_[0:n, :]
            done = ts(v, ps, eps, None, ALU.add, None, tok)
            ts(y.bitcast(I32), v.bitcast(I32), -0.5, RSQRT_SEED, ALU.mult, ALU.add)
            for _ in range(3):
                tt(t, y, y, ALU.mult)
                stt(t, t, -0.5, v, ALU.mult, ALU.mult)
                last = stt(y, t, 1.5, y, ALU.add, ALU.mult)
            return y, last, done

        def mean(src, toks):
            b, waits = PS.take()
            o = bank(b, 0, 256)
            for j in range(8):
                t = mm(o, onesd, src[:, j, :], j == 0, j == 7, waits, toks[j], inc=(j == 7))
            return b, o, t

        def square(src, toks):
            t1 = v3(T1[:, :], 8)
            res = []
            for j in range(0, 8, 2):
                t = act(t1[:, j:j + 2, :], src[:, j:j + 2, :], ACTF.Square, toks[j], toks[j + 1])
                res += [t, t]
            return t1, res

        def rms(src, toks):
            t1, sq = square(src, toks)
            b, ps, t = mean(t1, sq)
            r, rt, done = rsqrt(ps, 1e-6, P, t)
            PS.give(b, done)
            return r, rt

        SP.do(lambda e: e.dma_start(CT[:, :], a["consts"]).then_inc(s_in, 16), inc=False)
        SP.do(lambda e: e.dma_start(PR[:, :], a["params"]).then_inc(s_in, 16), inc=False)
        in_tok = ("in", s_in, 32)
        for m in range(2):
            SP.do(lambda e, m=m: e.dma_start(T2[:, m * 1024:(m + 1) * 1024], a["x"][m * P:(m + 1) * P, :])
                  .then_inc(s_x, 16), inc=False)
        for q in (PE, ACT, DVE, POOL):
            q.extra = [in_tok]
        x_tok = ("x", s_x, 32)

        xtok = [None] * 8
        for j in range(0, 8, 2):
            b, waits = PS.take()
            for jj in range(2):
                for m in range(2):
                    t = tr(bank(b, jj * 256 + m * P, jj * 256 + m * P + P),
                           T2[:, m * 1024 + (j + jj) * P:m * 1024 + (j + jj + 1) * P], P,
                           waits, x_tok, inc=(jj == m == 1))
            t = cp(XT[:, j * 256:(j + 2) * 256], bank(b), t, q=ACT)
            xtok[j] = xtok[j + 1] = t
            PS.give(b, t)

        csil = SM[:, 0:8]
        ct = act(csil, par("c"), ACTF.Silu)

        def modulation(l, i):
            n = 2 * l + i
            b, waits = PS.take()
            for s in range(12):
                si, w, tok = wk(a["ada_w"][l, i], s * 256)
                for f in range(2):
                    col = 2 * s + f
                    for k in range(8):
                        t = mm(bank(b, col, col + 1), w[:, k, f * P:(f + 1) * P], csil[:, k:k + 1],
                               k == 0, k == 7, waits, tok, ct, inc=(f == 1 and k == 7))
                W.give(si, t)
            m = MC[:, 0:24]
            t = tt(m, bank(b, 0, 24), par("adab", n * 24, 24), ALU.add, t)
            PS.give(b, t)
            sc = MC[:, 24:32]
            stt(sc, m[:, 8:16], 1.0, par("npre", n * 8, 8), ALU.add, ALU.mult)
            g = MC[:, 32:40]
            t = tt(g, m[:, 16:24], par("npost", n * 8, 8), ALU.mult)
            return m[:, 0:8], sc, g, t

        def pre(l, i, xtok):
            shift, sc, g, mt = modulation(l, i)
            r, rt = rms(xt, xtok)
            t2 = v3(T2[:, :], 8)
            htok = []
            for j in range(8):
                t = stt(t2[:, j, :], xt[:, j, :], sc[:, j:j + 1], r, ALU.mult, ALU.mult)
                htok.append(act(ht[:, j, :], t2[:, j, :], ACTF.Identity, t, bias=shift[:, j:j + 1]))
            return htok, g

        def post(g, ytok):
            r, rt = rms(yacc, [ytok] * 8)
            t2 = v3(T2[:, :], 8)
            res = []
            for j in range(8):
                t = stt(t2[:, j, :], yacc[:, j, :], g[:, j:j + 1], r, ALU.mult, ALU.mult)
                res.append(tt(xt[:, j, :], xt[:, j, :], t2[:, j, :], ALU.add))
            acc_free[0] = [t, ACT.last()]
            return res

        def layer_norm(n, ytok):
            t2 = v3(T2[:, :], 8)
            tk = []
            for j in range(0, 8, 2):
                t = stt(t2[:, j:j + 2, :], xt[:, j:j + 2, :], DN_ALPHA, yacc[:, j:j + 2, :], ALU.mult, ALU.add, ytok)
                tk += [t, t]
            acc_free[0] = [t]
            b, ps, t = mean(t2, tk)
            cen = []
            for j in range(0, 8, 2):
                t = tt(t2[:, j:j + 2, :], t2[:, j:j + 2, :], rep(ps, 2), ALU.subtract, t)
                cen += [t, t]
            PS.give(b, t)
            t1, sq = square(t2, cen)
            b, ps, t = mean(t1, sq)
            r, rt, done = rsqrt(ps, 1e-5, P, t)
            PS.give(b, done)
            res = []
            for j in range(8):
                t = stt(t2[:, j, :], t2[:, j, :], par("lng", n * 8 + j, 1), r, ALU.mult, ALU.mult)
                res.append(act(xt[:, j, :], t2[:, j, :], ACTF.Identity, t, bias=par("lnb", n * 8 + j, 1)))
            return res

        def gated(pairs, htok, x, spread=None, bt=None):
            hid = [v3(take(512), 2) for _ in range(2)]
            tmp = [v3(take(512), 2) for _ in range(2)]
            hfree = [None, None]
            pend = None
            n = len(pairs)

            def finish(p):
                i, hb, t = p
                return down(pairs[i][2](), [hid[hb][:, 0, :], hid[hb][:, 1, :]], i == 0, i == n - 1, t)

            for i, (g, u, _) in enumerate(pairs):
                hb = i % 2
                bg, tg = fm(g(), htok, src=x)
                ta = act(tmp[hb], v3(bank(bg), 2), ACTF.Silu, tg, hfree[hb])
                PS.give(bg, ta)
                if spread is not None:
                    ta = tt(tmp[hb], tmp[hb], rep(spread[:, i, :], 2), ALU.mult, ta, bt, q=POOL)
                bu, tu = fm(u(), htok, src=x)
                th = tt(hid[hb], tmp[hb], v3(bank(bu), 2), ALU.mult, ta, tu)
                PS.give(bu, th)
                if pend:
                    td = finish(pend)
                    hfree[pend[1]] = td
                pend = (i, hb, th)
            return finish(pend)

        def ffn(l, htok):
            wi, wo = a["ffn_w_in"][l], a["ffn_w_out"][l]
            return gated([(lambda i=i: wk(wi, i * 256), lambda i=i: wk(wi, 2816 + i * 256),
                           lambda i=i: wd(wo, i * 256)) for i in range(NF)], htok, ht)

        def hybrid(htok):
            wi = a["hyb_w_in"][0]
            ai, aux, atok = load(a["aux"], cols=AN, k=1)
            invc = take(1024)
            t = cp(invc, aux[:, 0:1024], atok, q=POOL)
            W.give(ai, t)
            inv_tok = t
            U = v3(take(4 * 272), 4)
            w2, w4, w8 = (v3(take(4 * 272), 4) for _ in range(3))
            z = [DVE.do(lambda e, x=x: e.memset(x, 0.0)) for x in
                 (U[:, :, 0:16],)]
            for s in range(2):
                b, t = fm(wk(wi, s * 256), htok)
                tu = cp(U[:, 2 * s:2 * s + 2, 16:272], v3(bank(b), 2), t, z)
                PS.give(b, tu)
            Qh = take(1024)
            Kh = take(1024)
            Fh = take(1024)
            Sg = take(1024)
            lb = SM[:, 16:20]
            om = SM[:, 20:24]
            e0 = SM[:, 24:28]
            tt(e0, par("lbl"), par("lbl"), ALU.subtract)
            te = act(e0, e0, ACTF.Exp, DVE.last())
            recip(lb, e0, te)
            tt(lb, lb, e0, ALU.mult)
            tt(lb, lb, lb, ALU.subtract)
            ts(lb, lb, 0.0, None, ALU.max)
            ts(om, lb, -1.0, 1.0, ALU.mult, ALU.add)
            for s in range(2):
                b, t = fm(wk(wi, 512 + s * 256), htok)
                tq = act(Qh[:, s * 512:(s + 1) * 512], bank(b), ACTF.Silu, t)
                PS.give(b, tq)
            for s in range(2):
                b, t = fm(wk(wi, 1024 + s * 256), htok)
                sl = slice(s * 512, (s + 1) * 512)
                t1 = act(Fh[:, sl], bank(b), ACTF.Sigmoid, t)
                t2 = act(Kh[:, sl], bank(b), ACTF.Sigmoid, scale=-1.0)
                PS.give(b, t2)
            for h in range(4):
                sl = slice(h * 256, (h + 1) * 256)
                ts(Fh[:, sl], Fh[:, sl], om[:, h:h + 1], lb[:, h:h + 1], ALU.mult, ALU.add, t2)
                tf = ts(Kh[:, sl], Kh[:, sl], om[:, h:h + 1], None, ALU.mult)
            Vt = v3(take(1024), 2)
            for s in range(2):
                b, t = tm(wk(wi, 1536 + s * 256), htok)
                tv = cp(Vt[:, :, s * 256:(s + 1) * 256], v3(bank(b), 2), t, q=ACT)
                PS.give(b, tv)
            for s in range(2):
                b, t = fm(wk(wi, 2048 + s * 256), htok)
                tg = act(Sg[:, s * 512:(s + 1) * 512], bank(b), ACTF.Silu, t)
                PS.give(b, tg)

            tt(w2[:, :, 1:272], U[:, :, 1:272], U[:, :, 0:271], ALU.add, tu)
            tt(w4[:, 1:4, 3:272], w2[:, 1:4, 3:272], w2[:, 1:4, 1:270], ALU.add)
            tt(w8[:, 2:4, 7:272], w4[:, 2:4, 7:272], w4[:, 2:4, 3:268], ALU.add)
            tt(w2[:, 3:4, 16:272], w8[:, 3:4, 16:272], w8[:, 3:4, 8:264], ALU.add)
            dif = v3(take(1024), 4)
            ic = v3(invc, 4)
            for g, wsrc in enumerate((w2, w4, w8, w2)):
                tt(dif[:, g, :], wsrc[:, g, 16:272], ic[:, g, :], ALU.mult, inv_tok)
            td = tt(dif, dif, U[:, :, 16:272], ALU.subtract)
            YP = v3(take(1024), 4)
            pi, pw, ptok = load(a["pool_w"][0].rearrange("g c d -> c g d"), cols=512, k=4)
            for s in range(2):
                b, waits = PS.take()
                for gg in range(2):
                    g = 2 * s + gg
                    t = mm(bank(b, gg * 256, gg * 256 + 256), pw[:, g, :], dif[:, g, :], True, True,
                           waits, ptok, td, inc=(gg == 1))
                for gg in range(2):
                    g = 2 * s + gg
                    ty = act(YP[:, g, :], bank(b, gg * 256, gg * 256 + 256), ACTF.Copy, t,
                             scale=par("pscale", g, 1))
                PS.give(b, ty)
            W.give(pi, t)

            Am = v3(take(1024), 8)
            A2 = v3(take(512), 4)
            q4, k4 = v3(Qh, 4), v3(Kh, 4)
            tot = Fh
            nxt = take(512)
            spare = take(256)
            ready = [tq, tf]
            levels = [0, 1, 2, 4, 8, 16, 32, 64]
            for li, h in enumerate(levels):
                if h == 1:
                    tq1 = tt(Qh, Qh, Fh, ALU.mult, t_mm)
                    ready = [tq1]
                if h > 1:
                    g = h // 2
                    n = 1024 // h
                    qv = Qh.rearrange("p (n b c) -> p n b c", n=n, b=2)
                    kv = Kh.rearrange("p (n b c) -> p n b c", n=n, b=2)
                    tv_ = tot[:, 0:2 * n].rearrange("p (n b) -> p n b", b=2)
                    tt(qv[:, :, 1, :], qv[:, :, 1, :], wide(tv_[:, :, 0], g), ALU.mult, t_mm)
                    tt(kv[:, :, 0, :], kv[:, :, 0, :], wide(tv_[:, :, 1], g), ALU.mult)
                    dst = nxt if tot is not nxt else spare
                    t = tt(dst[:, 0:n], tv_[:, :, 0], tv_[:, :, 1], ALU.mult)
                    tot = dst
                    ready = [t]
                for half in range(2):
                    b, waits = PS.take()
                    for x in range(4):
                        hd, m = 2 * half + x // 2, x % 2
                        t_mm = mm(bank(b, x * P, x * P + P), k4[:, hd, m * P:m * P + P],
                                  q4[:, hd, m * P:m * P + P], True, True, waits, ready, inc=(x == 3))
                    dst = Am[:, 4 * half:4 * half + 4, :]
                    if h == 0:
                        tm_ = tt(dst, v3(bank(b), 4), rep(ident, 4), ALU.mult, t_mm)
                    else:
                        mk = cst("hm", (li - 1) * P, P).bitcast(I32)
                        tm_ = DVE.do(lambda e, dst=dst, mk=mk, b=b: e.copy_predicated(
                            dst, rep(mk, 4), v3(bank(b), 4)), t_mm)
                    PS.give(b, tm_)
            n = 1024 // 128
            qv = Qh.rearrange("p (n b c) -> p n b c", n=n, b=2)
            kv = Kh.rearrange("p (n b c) -> p n b c", n=n, b=2)
            tv_ = tot[:, 0:2 * n].rearrange("p (n b) -> p n b", b=2)
            tt(qv[:, :, 1, :], qv[:, :, 1, :], wide(tv_[:, :, 0], 64), ALU.mult, t_mm)
            t = tt(kv[:, :, 0, :], kv[:, :, 0, :], wide(tv_[:, :, 1], 64), ALU.mult)
            b, waits = PS.take()
            for hd in range(4):
                t = mm(bank(b, hd * P, hd * P + P), k4[:, hd, 0:P], q4[:, hd, P:2 * P], True, True,
                       waits, t, inc=(hd == 3)) or t
            t2 = cp(A2, v3(bank(b), 4), t, q=ACT)
            PS.give(b, t2)
            b, waits = PS.take(2)
            o = PSA[:, b * 512:b * 512 + 1024]
            for hd in range(4):
                c = hd * 256
                vh = slice(hd * P, hd * P + P)
                mm(o[:, c:c + P], Vt[:, 0, vh], Am[:, 2 * hd, :], True, True, waits, t2, tm_, tv)
                mm(o[:, c + P:c + 256], Vt[:, 1, vh], Am[:, 2 * hd + 1, :], True, False)
                t = mm(o[:, c + P:c + 256], Vt[:, 0, vh], A2[:, hd, :], False, True, inc=True)
            sq = T1[:, 0:1024]
            t = act(sq, o, ACTF.Square, t)
            b2, waits = PS.take()
            st = bank(b2, 0, 256, p=4)
            for hd in range(4):
                ti = mm(st, cst("hsel", 4 * hd, 4), sq[:, hd * 256:hd * 256 + 256], hd == 0, hd == 3,
                        waits, t, inc=(hd == 3))
            r, rt, done = rsqrt(st, 1e-6, 4, ti)
            PS.give(b2, done)
            YH = take(1024)
            t1 = stt(YH, o, par("onorm"), Sg, ALU.mult, ALU.mult, tg)
            PS.give(b, t1, k=2)
            b, waits = PS.take(2)
            for hd in range(4):
                t = mm(PSA[:, b * 512 + hd * 256:b * 512 + hd * 256 + 256], row_of(hd, 4), r,
                       True, True, waits, rt, inc=(hd == 3))
            th = tt(YH, YH, PSA[:, b * 512:b * 512 + 1024], ALU.mult, t)
            PS.give(b, th, k=2)
            yh = v3(YH, 4)
            for s in range(4):
                src = YP if s < 2 else yh
                k0 = 2 * (s % 2)
                t = down(wd(a["hyb_w_out"][0], s * 256), [src[:, k0, :], src[:, k0 + 1, :]],
                         s == 0, s == 3, ty if s < 2 else th)
            return t

        def attend(units, scores, soft, blocks, value, width):
            NB = 2
            pts = [take(width) for _ in range(NB)]
            pfree = [None] * NB
            st = {}
            done = None

            def transposes(u):
                pr, tk = st[u]["p"]
                n = blocks(units[u])
                if n <= 4:
                    b, waits = PT.take()
                    kk = 1
                else:
                    b, waits = PT.take(2)
                    kk = 2
                for x in range(n):
                    t = tr(bank(b + x // 4, (x % 4) * P, (x % 4) * P + P), pr[:, x * P:(x + 1) * P], P,
                           waits, tk, inc=(x == n - 1))
                dst = pts[u % NB]
                o = (b - 4) * 512
                t2 = cp(dst[:, 0:n * P], PSB[:, o:o + n * P], t, pfree[u % NB], q=ACT)
                PT.give(b, t2, k=kk)
                st[u]["pt"] = (dst, t2)
                return t

            N = len(units)
            for u in range(N + 2):
                if u < N:
                    st[u] = {"s": scores(units[u])}
                    st[u]["p"] = soft(units[u], st[u]["s"])
                if 2 <= u:
                    done = value(units[u - 2], *st[u - 2]["pt"])
                    pfree[u % NB] = done
                if 1 <= u <= N:
                    st[u - 1]["tt"] = transposes(u - 1)
                    sfree[0][units[u - 1][2] % 3] = st[u - 1]["tt"]
            return done

        sfree = [[None] * 3]

        def dilated(htok):
            wq = a["att_w_qkv"][0]
            ai, aux, atok = load(a["aux"], cols=AN, k=1)
            b, waits = PS.take()
            oh = aux[0:32, 1024:1024 + 384]
            mv = aux[0:24, 1408:1408 + 384]
            rb = aux[0:32, 1792:1792 + 24]
            t = mm(bank(b, 0, 384, p=24), rb, oh, True, True, waits, atok, inc=True)
            brow = SM[0:24, 64:448]
            t = tt(brow, bank(b, 0, 384, p=24), mv, ALU.add, t, atok)
            W.give(ai, t)
            PS.give(b, t)
            ACT.do(lambda e: e.dma_start(scratch[:, :], brow).then_inc(s_bias, 16), t, inc=False)
            ACT.open = False
            bt = take(6144)
            src = bass.AP(scratch, 0, [[1, P], [384, 24], [1, 256]])
            ACT.do(lambda e: e.dma_start(v3(bt, 24), src).then_inc(s_tp, 16), ("bias", s_bias, 16), inc=False)
            ACT.open = False
            btok = ("tp", s_tp, 16)

            def bias_of(h, n):
                pp = [list(x) for x in bt.ap][0]
                return bass.AP(bt.tensor, bt.offset + h * 256 + n - 1, [pp, [8 * 256, 3], [-1, n]])

            qf = v3(take(3072), 12)
            kf = v3(take(3072), 12)
            vt = v3(take(3072), 2)
            for s in range(6):
                b, t = fm(wk(wq, s * 256), htok)
                tq = act(qf[:, 2 * s:2 * s + 2, :], v3(bank(b), 2), ACTF.Copy, t, scale=0.125)
                PS.give(b, tq)
            for s in range(6):
                b, t = fm(wk(wq, 1536 + s * 256), htok)
                tk = cp(kf[:, 2 * s:2 * s + 2, :], v3(bank(b), 2), t)
                PS.give(b, tk)
            for s in range(6):
                b, t = tm(wk(wq, 3072 + s * 256), htok)
                tv = cp(vt[:, :, s * 256:s * 256 + 256], v3(bank(b), 2), t)
                PS.give(b, tv)

            Sb = [take(768) for _ in range(3)]
            sfree[0] = [None] * 3
            mx = SM[:, 448:464]
            den = SM[:, 464:480]
            rd = SM[:, 480:496]
            units = [(qt, h, 8 * qt + h) for qt in range(2) for h in range(8)]

            def scores(u):
                qt, h, i = u
                n = (qt + 1) * P
                b, waits = PS.take(2)
                o = (h % 2) * 64
                for g in range(3):
                    tile = g * 4 + h // 2
                    t = mm(PSA[:, b * 512 + g * 256:b * 512 + g * 256 + n],
                           qf[o:o + 64, tile, qt * P:qt * P + P], kf[o:o + 64, tile, 0:n],
                           True, True, waits, tq, tk, inc=(g == 2))
                return b, t

            def soft(u, s):
                qt, h, i = u
                b, t = s
                n = (qt + 1) * P
                sbf = Sb[i % 3][:, 0:3 * n]
                ps = v3(PSA[:, b * 512:b * 512 + 768], 3)[:, :, 0:n]
                t = tt(v3(sbf, 3), ps, bias_of(h, n), ALU.add, t, btok, sfree[0][i % 3])
                PS.give(b, t, k=2)
                red(mx[:, i:i + 1], sbf, ALU.max)
                t = ts(mx[:, i:i + 1], mx[:, i:i + 1], -1.0, None, ALU.mult)
                t = act(sbf, sbf, ACTF.Exp, t, bias=mx[:, i:i + 1], accum=den[:, i:i + 1])
                return sbf, t

            def value(u, pt, tok):
                qt, h, i = u
                x = 0
                for g in range(3):
                    for kt in range(qt + 1):
                        c = g * 512 + h * 64
                        t = mm(bank(4 + qt, h * 64, h * 64 + 64), pt[:, x * P:(x + 1) * P],
                               vt[:, kt, c:c + 64], x == 0, x == 3 * (qt + 1) - 1, tok, tv,
                               acc_free[0], inc=(x == 3 * (qt + 1) - 1))
                        x += 1
                return t

            done = attend(units, scores, soft, lambda u: 3 * (u[0] + 1), value, 768)
            ot = take(1024)
            recip(rd, den, ACT.last())
            for qt in range(2):
                td = tt(v3(ot[:, qt * 512:(qt + 1) * 512], 8), v3(bank(4 + qt), 8),
                        wide(rd[:, 8 * qt:8 * qt + 8], 64), ALU.mult, done)
            return project_tokens(ot, td, a["att_w_out"][0], 0, 2, True, None)

        def to_features(ot, td, dst):
            res = []
            for f in range(0, 4, 2):
                b, waits = PS.take()
                for ff in range(2):
                    for m in range(2):
                        t = tr(bank(b, ff * 256 + m * P, ff * 256 + m * P + P),
                               ot[:, m * 512 + (f + ff) * P:m * 512 + (f + ff + 1) * P], P,
                               waits, td, inc=(ff == m == 1))
                t = cp(dst[:, f:f + 2, :], v3(bank(b), 2), t, q=ACT)
                PS.give(b, t)
                res.append(t)
            return res

        def project_tokens(ot, td, wout, s0, s1, last, extra):
            dst = v3(take(1024), 4)
            tf = to_features(ot, td, dst)
            acc_free[0] = acc_free[0] + [td]
            for s in range(s0, s1):
                t = down(wd(wout, s * 256), [dst[:, 2 * s, :], dst[:, 2 * s + 1, :]], s == s0,
                         last and s == s1 - 1, tf[s])
            return t

        def log_sigmoid(x, t0, t1, tok):
            stt(t0, x, -1.0, x, ALU.mult, ALU.min, tok)
            t = act(t0, t0, ACTF.Exp, DVE.last())
            t = act(t0, t0, ACTF.Ln, bias=1.0)
            return stt(x, x, 0.0, t0, ALU.min, ALU.subtract, t)

        def fox(xtok):
            wi = a["even_w_in_2"][0]
            src = xt
            qf, kf, uf = (v3(take(1024), 4) for _ in range(3))
            vt = v3(take(1024), 2)
            cf = take(256)[0:8, :]
            cw = take(256)[0:8, :]
            gi, gw, gtok = load(wi[:, 1536:1544].rearrange("(k p) n -> p k n", p=P), cols=64)
            b, waits = PS.take()
            for k in range(8):
                t = mm(bank(b, 0, 256, p=8), gw[:, k, :], src[:, k, :], k == 0, k == 7, waits, gtok,
                       xtok[k], inc=(k == 7))
            W.give(gi, t)
            t = ts(cf, bank(b, 0, 256, p=8), par("fb", 0, 1, p=8), None, ALU.add, None, t)
            PS.give(b, t)
            t = log_sigmoid(cf, cw, None, t)
            DVE.do(lambda e: e.memset(cw, 0.0))
            t = scan(cw, cf, cw, 0.0, ALU.add, ALU.add)
            tc_ = ts(cf, cw, -1.0, None, ALU.mult)
            cpos, cneg = cw, cf

            for s in range(2):
                b, t = fm(wk(wi, 1544 + s * 256), xtok, src=src)
                tu = cp(uf[:, 2 * s:2 * s + 2, :], v3(bank(b), 2), t)
                PS.give(b, tu)
            for s in range(2):
                b, t = fm(wk(wi, s * 256), xtok, src=src)
                tq = act(qf[:, 2 * s:2 * s + 2, :], v3(bank(b), 2), ACTF.Copy, t, scale=0.125)
                PS.give(b, tq)
            for s in range(2):
                b, t = fm(wk(wi, 512 + s * 256), xtok, src=src)
                tk = cp(kf[:, 2 * s:2 * s + 2, :], v3(bank(b), 2), t)
                PS.give(b, tk)
            for s in range(2):
                i, w, tok = wk(wi, 1024 + s * 256)
                b, waits = PS.take()
                for m in range(2):
                    for k in range(8):
                        t = mm(bank(b, m * 256, m * 256 + 256), src[:, k, m * P:(m + 1) * P], w[:, k, :],
                               k == 0, k == 7, waits, tok, inc=(m == 1 and k == 7))
                W.give(i, t)
                tv = cp(vt[:, :, s * 256:s * 256 + 256], v3(bank(b), 2), t)
                PS.give(b, tv)

            Sb = [take(256) for _ in range(3)]
            sfree[0] = [None] * 3
            mx, den, rd = SM[:, 448:464], SM[:, 464:480], SM[:, 480:496]
            units = [(qt, h, 8 * qt + h) for qt in range(2) for h in range(8)]

            def scores(u):
                qt, h, i = u
                n = (qt + 1) * P
                b, waits = PS.take()
                o = (h % 2) * 64
                r = bank(b, 0, n)
                mm(bank(b, n - P, n), ident, cst("causal"), True, False, waits, skip=True)
                mm(r, qf[o:o + 64, h // 2, qt * P:qt * P + P], kf[o:o + 64, h // 2, 0:n], False, False,
                   tq, tk, skip=True)
                mm(r, cpos[:, qt * P:qt * P + P], ident[0:8, h:h + 1].to_broadcast([8, n]), False, False, tc_,
                   skip=True)
                t = mm(r, row_of(h, 8), cneg[:, 0:n], False, True, inc=True, skip=True)
                return b, t

            def soft(u, s):
                qt, h, i = u
                b, t = s
                n = (qt + 1) * P
                sbf = Sb[i % 3][:, 0:n]
                red(mx[:, i:i + 1], bank(b, 0, n), ALU.max, t)
                t = ts(mx[:, i:i + 1], mx[:, i:i + 1], -1.0, None, ALU.mult)
                t = act(sbf, bank(b, 0, n), ACTF.Exp, t, sfree[0][i % 3], bias=mx[:, i:i + 1],
                        accum=den[:, i:i + 1])
                PS.give(b, t)
                return sbf, t

            def value(u, pt, tok):
                qt, h, i = u
                for kt in range(qt + 1):
                    t = mm(bank(4 + qt, h * 64, h * 64 + 64), pt[:, kt * P:(kt + 1) * P],
                           vt[:, kt, h * 64:h * 64 + 64], kt == 0, kt == qt, tok, tv, acc_free[0],
                           inc=(kt == qt))
                return t

            done = attend(units, scores, soft, lambda u: u[0] + 1, value, 256)
            ot = take(1024)
            recip(rd, den, ACT.last())
            for qt in range(2):
                td = tt(v3(ot[:, qt * 512:(qt + 1) * 512], 8), v3(bank(4 + qt), 8),
                        wide(rd[:, 8 * qt:8 * qt + 8], 64), ALU.mult, done)
            t = project_tokens(ot, td, a["even_w_out_2"][0], 0, 2, False, None)

            ys = s5(uf, tu)
            gi, gw, gtok = load(a["s5_w_glu_2"][0].rearrange("(k p) n -> p k n", p=P), k=4)
            y2 = qf
            for s in range(2):
                b, waits = PS.take()
                for f in range(2):
                    for k in range(4):
                        ff = 2 * s + f
                        t = mm(bank(b, f * 256, f * 256 + 256), gw[:, k, ff * P:ff * P + P], ys[0][:, k, :],
                               k == 0, k == 3, waits, gtok, ys[1], inc=(f == 1 and k == 3))
                for f in range(2):
                    ff = 2 * s + f
                    tg = act(y2[:, ff, :], bank(b, f * 256, f * 256 + 256), ACTF.Sigmoid, t,
                             bias=par("bglu", ff, 1))
                PS.give(b, tg)
            W.give(gi, t)
            ty = tt(y2, y2, ys[0], ALU.mult, tg)
            for s in range(2, 4):
                k0 = 2 * (s - 2)
                t = down(wd(a["even_w_out_2"][0], s * 256), [y2[:, k0, :], y2[:, k0 + 1, :]], False, s == 3, ty)
            return t

        def reduce_angle(x, n, *waits, q=None):
            c1 = 6.28125
            c2 = 0.0019350051879882812
            c3 = TWO_PI - c1 - c2
            ts(n, x, 1.0 / TWO_PI, ROUND, ALU.mult, ALU.add, *waits)
            ts(n, n, ROUND, None, ALU.subtract)
            stt(x, n, -c1, x, ALU.mult, ALU.add)
            stt(x, n, -c2, x, ALU.mult, ALU.add)
            stt(x, n, -c3, x, ALU.mult, ALU.add)
            return ts(x, x, 3.1415925, -3.1415925, ALU.min, ALU.max)

        def s5(uf, tu):
            sm = take(16 * 20)
            c = [sm[:, i * 16:(i + 1) * 16] for i in range(20)]
            dt, mag, th, nn, cs, sn, lre, lim, den, zre, zim, t0, t1 = c[:13]
            are, aim = par("are"), par("aim")
            half = cst("half", 0, 1)
            t = act(dt, par("ldt"), ACTF.Exp)
            tt(mag, are, dt, ALU.mult, t)
            t = act(mag, mag, ACTF.Exp, DVE.last())
            tt(th, aim, dt, ALU.mult)
            t2 = reduce_angle(th, nn)
            act(sn, th, ACTF.Sin, t2)
            act(cs, th, ACTF.Abs)
            t = act(cs, cs, ACTF.Sin, scale=-1.0, bias=half)
            tt(lre, mag, cs, ALU.mult, t)
            tt(lim, mag, sn, ALU.mult)
            ts(lre, lre, -1.0, None, ALU.add)
            tt(den, are, are, ALU.mult)
            tt(t0, aim, aim, ALU.mult)
            tt(den, den, t0, ALU.add)
            recip(den, den)
            tt(zre, lre, are, ALU.mult)
            tt(t0, lim, aim, ALU.mult)
            tt(zre, zre, t0, ALU.add)
            tt(zre, zre, den, ALU.mult)
            tt(zim, lim, are, ALU.mult)
            tt(t0, lre, aim, ALU.mult)
            tt(zim, zim, t0, ALU.subtract)
            tt(zim, zim, den, ALU.mult)
            bre, bim = v3(par("bre"), 16), v3(par("bim"), 16)
            bb = [v3(take(256), 16) for _ in range(2)]
            w0 = v3(take(256), 16)
            tt(bb[0], bre, wide(zre, 16), ALU.mult)
            tt(w0, bim, wide(zim, 16), ALU.mult)
            tt(bb[0], bb[0], w0, ALU.subtract)
            tt(bb[1], bim, wide(zre, 16), ALU.mult)
            tt(w0, bre, wide(zim, 16), ALU.mult)
            tt(bb[1], bb[1], w0, ALU.add)
            blk = take(1024)
            BT = [v3(take(512), 4) for _ in range(2)]
            CTt = [v3(take(512), 4) for _ in range(2)]
            DVE.do(lambda e: e.memset(blk, 0.0))
            for r in range(2):
                bv = blk[:, r * 512:(r + 1) * 512].rearrange("p (j e c) -> p j e c", j=16, e=2)
                for e_ in range(2):
                    t = cp(bv[e_ * 64:e_ * 64 + 64, :, e_, :], bb[r][e_ * 64:e_ * 64 + 64, :, :])
            for r in range(2):
                b, waits = PS.take()
                for i in range(4):
                    t2 = tr(bank(b, i * P, i * P + P), blk[:, r * 512 + i * P:r * 512 + i * P + P], P,
                            waits, t, inc=(i == 3))
                t3 = cp(BT[r], v3(bank(b), 4), t2, q=ACT)
                PS.give(b, t3)
            tbt = t3
            cblk = v4(take(1024), 2, 4)
            ev = cst("half", 1, 1)
            for r, nm in enumerate(("cre", "cim")):
                cv = v3(par(nm), 4)
                od = cst("firsts", 0, 1)
                ts(cblk[:, r, :, 0:64], cv, ev, 1.0 if r == 0 else -1.0, ALU.mult, ALU.mult)
                t = ts(cblk[:, r, :, 64:128], cv, od, 1.0 if r == 0 else -1.0, ALU.mult, ALU.mult)
            for r in range(2):
                b, waits = PS.take()
                for i in range(4):
                    t2 = tr(bank(b, i * P, i * P + P), cblk[:, r, i, :], P, waits, t, inc=(i == 3))
                t3 = cp(CTt[r], v3(bank(b), 4), t2, q=ACT)
                PS.give(b, t3)
            tct = t3

            YS = v3(take(1024), 4)
            C, Sn, An, Nn, Br, Bi, Gr, Gi = (v3(take(1024), 4) for _ in range(8))
            tvec = cst("tt")
            t_prev = None
            for i in range(4):
                for jj in range(4):
                    ts(An[:, jj, :], tvec, th[:, 4 * i + jj:4 * i + jj + 1], None, ALU.mult)
                t = reduce_angle(An, Nn)
                act(Sn, An, ACTF.Sin, t)
                act(C, An, ACTF.Abs)
                tsc = act(C, C, ACTF.Sin, scale=-1.0, bias=half)
                b, waits = PS.take(4)
                for jj in range(4):
                    for r in range(2):
                        t = mm(bank(b + jj, r * 256, r * 256 + 256), BT[r][32 * jj:32 * jj + 32, i, :],
                               uf[32 * jj:32 * jj + 32, i, :], True, True, waits, tbt, tu,
                               inc=(jj == 3 and r == 1))
                bu = PSA[:, :].rearrange("p (j r n) -> p j r n", j=4, r=2)
                cp(Br, bu[:, :, 0, :], t, q=ACT)
                t = cp(Bi, bu[:, :, 1, :], t, q=ACT)
                PS.give(b, t, k=4)
                tt(Gr, Br, C, ALU.mult, t, tsc)
                tt(Nn, Bi, Sn, ALU.mult)
                tt(Gr, Gr, Nn, ALU.add)
                tt(Gi, Bi, C, ALU.mult)
                tt(Nn, Br, Sn, ALU.mult)
                tt(Gi, Gi, Nn, ALU.subtract)
                for jj in range(4):
                    m = mag[:, 4 * i + jj:4 * i + jj + 1].to_broadcast([P, 256])
                    scan(Br[:, jj, :], m, Gr[:, jj, :], 0.0, ALU.mult, ALU.add)
                    scan(Bi[:, jj, :], m, Gi[:, jj, :], 0.0, ALU.mult, ALU.add)
                tt(Gr, Br, C, ALU.mult, t_prev)
                tt(Nn, Bi, Sn, ALU.mult)
                tt(Gr, Gr, Nn, ALU.subtract)
                tt(Gi, Bi, C, ALU.mult)
                tt(Nn, Br, Sn, ALU.mult)
                t = tt(Gi, Gi, Nn, ALU.add)
                b, waits = PS.take()
                for jj in range(4):
                    o = bank(b, 0, 256, p=32, p0=32 * jj)
                    mm(o, CTt[0][:, i, 32 * jj:32 * jj + 32], Gr[:, jj, :], True, False, waits, t, tct)
                    t_prev = mm(o, CTt[1][:, i, 32 * jj:32 * jj + 32], Gi[:, jj, :], False, True, inc=(jj == 3))
                t = stt(YS[:, i, :], uf[:, i, :], par("s5d", i, 1), bank(b, 0, 256), ALU.mult, ALU.add, t_prev)
                PS.give(b, t)
            tg = act(YS, YS, ACTF.Gelu_apprx_tanh, t)
            return YS, tg

        def mlstm(xtok):
            wi = a["odd_w_in_2"][0]
            src = xt
            qk = [v3(take(2048), 8) for _ in range(2)]
            vt = v3(take(2048), 2)
            og = v3(take(2048), 8)
            pad = [take(260) for _ in range(4)]
            acc = [take(256) for _ in range(2)]
            pfree = [None] * 4
            afree = [None] * 2
            gf = [take(256)[0:8, :] for _ in range(4)]
            lf, g, mr, wk_ = gf
            gi, gw, gtok = load(wi[:, 4096:4112].rearrange("(k p) n -> p k n", p=P), cols=128)
            b, waits = PS.take()
            for r in range(2):
                for k in range(8):
                    t = mm(bank(b, r * 256, r * 256 + 256, p=8), gw[:, k, 8 * r:8 * r + 8], src[:, k, :],
                           k == 0, k == 7, waits, gtok, xtok[k], inc=(r == 1 and k == 7))
            W.give(gi, t)
            ts(g, bank(b, 0, 256, p=8), par("fb", 1, 1, p=8), None, ALU.add, None, t)
            t = ts(lf, bank(b, 256, 512, p=8), par("fb", 2, 1, p=8), None, ALU.add)
            PS.give(b, t)
            log_sigmoid(lf, wk_, None, t)
            DVE.do(lambda e: e.memset(wk_, 0.0))
            scan(wk_, lf, wk_, 0.0, ALU.add, ALU.add)
            Fc = wk_
            tg_ = tt(g, g, Fc, ALU.subtract)
            scan(mr, g, g, 0.0, ALU.max, ALU.max)
            t = tt(lf, Fc, mr, ALU.add)
            b, waits = PS.take()
            for m in range(2):
                tr(bank(b, m * 16, m * 16 + 8), mr[:, m * P:(m + 1) * P], 8, waits, t)
                t2 = tr(bank(b, m * 16 + 8, m * 16 + 16), lf[:, m * P:(m + 1) * P], 8, inc=(m == 1))
            nm = SM[:, 500:532]
            t = ts(nm, bank(b, 0, 32), -1.0, None, ALU.mult, None, t2)
            PS.give(b, t)
            em = SM[:, 532:564]
            t_em = act(em, nm, ACTF.Exp, t)
            t_nm = t

            zt = [DVE.do(lambda e, x=x: e.memset(x[:, 0:3], 0.0)) for x in pad]
            for s in range(8):
                b, t = fm(wk(wi, s * 256), xtok, src=src)
                for f in range(2):
                    c = 2 * s + f
                    pb, ab = c % 4, c % 2
                    tp = cp(pad[pb][:, 3:259], bank(b, f * 256, f * 256 + 256), t, zt, pfree[pb], q=ACT)
                    ts(acc[ab], pad[pb][:, 0:256], par("convw", c, 1), par("convb", c, 1), ALU.mult, ALU.add,
                       tp, afree[ab])
                    for w in range(1, 4):
                        td = stt(acc[ab], pad[pb][:, w:w + 256], par("convw", w * 16 + c, 1), acc[ab],
                                 ALU.mult, ALU.add)
                    pfree[pb] = td
                    tqk = act(qk[c // 8][:, c % 8, :], acc[ab], ACTF.Silu, td)
                    afree[ab] = tqk
                PS.give(b, tp)
            for s in range(4):
                i, w, tok = wk(wi, 2048 + s * 256)
                b, waits = PS.take()
                for m in range(2):
                    for k in range(8):
                        t = mm(bank(b, m * 256, m * 256 + 256), src[:, k, m * P:(m + 1) * P], w[:, k, :],
                               k == 0, k == 7, waits, tok, inc=(m == 1 and k == 7))
                W.give(i, t)
                tv = cp(vt[:, :, s * 256:s * 256 + 256], v3(bank(b), 2), t)
                PS.give(b, tv)
            for s in range(4):
                b, t = fm(wk(wi, 3072 + s * 256), xtok, src=src)
                to = act(og[:, 2 * s:2 * s + 2, :], v3(bank(b), 2), ACTF.Sigmoid, t)
                PS.give(b, to)

            Sb = [take(256) for _ in range(3)]
            Db = [take(256) for _ in range(2)]
            sfree[0] = [None] * 3
            den = SM[:, 564:580]
            rd = SM[:, 580:596]
            units = [(qt, h, 2 * h + qt) for h in range(8) for qt in range(2)]
            hfree = [None] * 2
            hout = og
            st = {}
            INV = 128.0 ** -0.5

            def scores(u):
                qt, h, i = u
                n = (qt + 1) * P
                b, waits = PS.take()
                mm(bank(b, 0, n), qk[0][:, h, qt * P:qt * P + P], qk[1][:, h, 0:n], True, True, waits, tqk)
                mm(bank(b, 256 + n - P, 256 + n), ident, cst("causal"), True, False, skip=True)
                t = mm(bank(b, 256, 256 + n), row_of(h, 8), g[:, 0:n], False, True, tg_, inc=True, skip=True)
                return b, t

            def soft(u, s):
                qt, h, i = u
                b, t = s
                n = (qt + 1) * P
                sbf, dbf = Sb[i % 3][:, 0:n], Db[i % 2][:, 0:n]
                t = act(dbf, bank(b, 256, 256 + n), ACTF.Exp, t, st.get(("d", i % 2)), t_nm,
                        bias=nm[:, qt * 16 + h:qt * 16 + h + 1])
                t = DVE.do(lambda e: e.scalar_tensor_tensor(out=sbf, in0=bank(b, 0, n), scalar=INV, in1=dbf,
                                                            op0=ALU.mult, op1=ALU.mult,
                                                            accum_out=den[:, i:i + 1]), t, sfree[0][i % 3])
                PS.give(b, t)
                st[("d", i % 2)] = t
                stt(rd[:, i:i + 1], den[:, i:i + 1], -1.0, den[:, i:i + 1], ALU.mult, ALU.max)
                tt(rd[:, i:i + 1], rd[:, i:i + 1], em[:, qt * 16 + 8 + h:qt * 16 + 9 + h], ALU.max, t_em)
                recip(rd[:, i:i + 1], rd[:, i:i + 1])
                t = ts(sbf, sbf, rd[:, i:i + 1], None, ALU.mult)
                return sbf, t

            def value(u, pt, tok):
                qt, h, i = u
                bb = 4 + (h // 2) % 2
                lo = (h % 2) * 256 + qt * P
                for kt in range(qt + 1):
                    t = mm(bank(bb, lo, lo + P), vt[:, kt, h * P:(h + 1) * P], pt[:, kt * P:(kt + 1) * P],
                           kt == 0, kt == qt, tok, tv, acc_free[0], hfree[(h // 2) % 2], inc=(kt == qt))
                if h % 2 and qt:
                    hfree[(h // 2) % 2] = tt(hout[:, h - 1:h + 1, :], og[:, h - 1:h + 1, :], v3(bank(bb), 2),
                                             ALU.mult, t, to)
                return t

            attend(units, scores, soft, lambda u: u[0] + 1, value, 256)
            acc_free[0] = acc_free[0] + [DVE.last(), ACT.last()]
            for s in range(4):
                t = down(wd(a["odd_w_out_2"][0], s * 256), [hout[:, 2 * s, :], hout[:, 2 * s + 1, :]],
                         s == 0, s == 3, DVE.last())
            return t

        def moe(l, xtok):
            lg = v3(SM[:, 600:640], 2)
            b, waits = PS.take()
            wr = v3(par("wr", l * 160, 160), 8)
            for m in range(2):
                for k in range(8):
                    t = mm(bank(b, m * 20, m * 20 + 20), xt[:, k, m * P:(m + 1) * P], wr[:, k, :], k == 0, k == 7,
                           waits, xtok[k], inc=(m == 1 and k == 7))
            t = tt(lg, v3(bank(b, 0, 40), 2), rep(par("rb", l * 20, 20), 2), ALU.add, t)
            PS.give(b, t)
            at = [640]

            def s_(n):
                at[0] += n
                return SM[:, at[0] - n:at[0]]

            gl = lg[:, :, 0:4]
            el = lg[:, :, 4:20].rearrange("p m (g e) -> p m g e", g=4)
            m1, g4, ex, sm_, oh, gv = s_(2), v3(s_(8), 2), v3(s_(8), 2), s_(2), v3(s_(8), 2), s_(2)
            wt = cst("firsts", 0, 4)

            def onehot(o, x, mxv):
                tt(o, x, wide(mxv, 4), ALU.is_equal)
                tt(o, o, rep(order, 2), ALU.mult)
                red(m1, o, ALU.max)
                tt(o, o, wide(m1, 4), ALU.is_equal)

            order = s_(4)
            for x in range(4):
                DVE.do(lambda e, x=x: e.memset(order[:, x:x + 1], float(4 - x)))
            mg = s_(2)
            red(mg, gl, ALU.max)
            tt(g4, gl, wide(mg, 4), ALU.subtract)
            t = act(ex, g4, ACTF.Exp, DVE.last())
            red(sm_, ex, ALU.add, t)
            recip(gv, sm_)
            onehot(oh, gl, mg)
            sel = v4(s_(32), 2, 4)
            es = v3(s_(8), 2)
            for m in range(2):
                tt(sel[:, m], el[:, m], wide(oh[:, m, :], 4), ALU.mult)
                red(es[:, m, :], sel[:, m].rearrange("p g e -> p e g"), ALU.add)
            e1, o1, o2, l2, e2, p2, w1, w2 = s_(2), v3(s_(8), 2), v3(s_(8), 2), v3(s_(8), 2), s_(2), s_(2), s_(2), s_(2)
            red(e1, es, ALU.max)
            onehot(o1, es, e1)
            stt(l2, o1, -3.0e38, es, ALU.mult, ALU.add)
            red(e2, l2, ALU.max)
            onehot(o2, l2, e2)
            tt(p2, e2, e1, ALU.subtract)
            t = act(p2, p2, ACTF.Exp, DVE.last())
            ts(w1, p2, 1.0, None, ALU.add, None, t)
            recip(w1, w1)
            tt(w1, w1, gv, ALU.mult)
            tt(w2, w1, p2, ALU.mult)
            tt(o1, o1, wide(w1, 4), ALU.mult)
            tt(o2, o2, wide(w2, 4), ALU.mult)
            tt(o1, o1, o2, ALU.add)
            comb = v4(s_(32), 2, 4)
            for m in range(2):
                for g_ in range(4):
                    t = ts(comb[:, m, g_, :], o1[:, m, :], oh[:, m, g_:g_ + 1], None, ALU.mult)
            b, waits = PS.take()
            for m in range(2):
                t2 = tr(bank(b, m * P, m * P + P, p=16), comb[:, m].rearrange("p g e -> p (g e)"), P, waits, t,
                        inc=(m == 1))
            cT = take(256)[0:16, :]
            t = cp(cT, bank(b, 0, 256, p=16), t2, q=ACT)
            PS.give(b, t)
            spread = v3(take(4096), 16)
            for e_ in range(0, 16, 2):
                b, waits = PS.take()
                for x in range(2):
                    t2 = mm(bank(b, x * 256, x * 256 + 256), row_of(e_ + x, 16), cT, True, True, waits, t,
                            inc=(x == 1))
                tb = cp(spread[:, e_:e_ + 2, :], v3(bank(b), 2), t2, q=ACT)
                PS.give(b, tb)
            G, U_, Dn = a["moe_w_gate_2"][l], a["moe_w_up_2"][l], a["moe_w_down_2"][l]
            return gated([(lambda e=e: wk(G[e], 0), lambda e=e: wk(U_[e], 0), lambda e=e: wd(Dn[e], 0))
                          for e in range(16)], xtok, xt, spread, tb)

        for l in range(2):
            fence()
            htok, g = pre(l, 0, xtok)
            yt = hybrid(htok) if l == 0 else dilated(htok)
            xtok = post(g, yt)
            fence()
            htok, g = pre(l, 1, xtok)
            yt = ffn(l, htok)
            xtok = post(g, yt)
        for l in range(2):
            fence()
            yt = fox(xtok) if l == 0 else mlstm(xtok)
            xtok = layer_norm(2 * l, yt)
            fence()
            yt = moe(l, xtok)
            xtok = layer_norm(2 * l + 1, yt)

        fence()
        ov = take(2048)
        for m in range(2):
            for j in range(0, 8, 4):
                b, waits = PS.take()
                for jj in range(4):
                    t = tr(bank(b, jj * P, jj * P + P), xt[:, j + jj, m * P:(m + 1) * P], P, waits,
                           xtok[j + jj], inc=(jj == 3))
                t = cp(ov[:, m * 1024 + j * P:m * 1024 + (j + 4) * P], bank(b), t, q=(ACT if m else None))
                PS.give(b, t)
            SP.do(lambda e, m=m: e.dma_start(out[m * P:(m + 1) * P, :], ov[:, m * 1024:(m + 1) * 1024])
                  .then_inc(s_out, 16), t, inc=False)

        block = ctx.enter_context(nc.Block())

        @block.sync
        def _(eng):
            SP.emit(eng)
            eng.wait_ge(s_out, 32)

        @block.tensor
        def _(eng):
            PE.emit(eng)

        @block.scalar
        def _(eng):
            ACT.emit(eng)

        @block.vector
        def _(eng):
            DVE.emit(eng)

        @block.gpsimd
        def _(eng):
            POOL.emit(eng)


def shape_constants():
    c = np.zeros((P, CN), np.float32)
    i = np.arange(P)

    def put(name, v):
        at, n = CO[name]
        c[:, at:at + n] = v

    put("ident", np.eye(P))
    put("onesd", 1.0 / D)
    put("causal", np.where(i[None, :] <= i[:, None], 0.0, NEG))
    hm = []
    for h in (1, 2, 4, 8, 16, 32, 64):
        s, t = i[:, None], i[None, :]
        hm.append((s // (2 * h) == t // (2 * h)) & (s % (2 * h) < h) & (t % (2 * h) >= h))
    put("hm", np.concatenate(hm, 1))
    hs = np.zeros((P, 4, 4))
    for h in range(4):
        hs[:, h, h] = 1.0 / 128.0
    put("hsel", hs.reshape(P, 16))
    put("tt", np.arange(256)[None, :])
    put("half", np.stack([np.full(P, math.pi / 2), 1.0 - (i // 16) % 2], 1))
    put("firsts", np.stack([(i // 16) % 2] * 4, 1))

    x = np.zeros((P, AN), np.float32)
    inv = np.stack([1.0 / np.minimum(np.arange(256) + 1, w) for w in (2, 4, 8, 16)]).reshape(-1)
    x[:, 0:1024] = inv[None, :]
    d = np.arange(384) - 127
    dd = np.maximum(d, 0).astype(np.int64)
    df = np.maximum(dd, 1).astype(np.float32)
    large = 16 + (np.log(df / np.float32(16)).astype(np.float32) / np.float32(math.log(2048 / 16))
                  * np.float32(16)).astype(np.int32)
    bucket = np.where(dd < 16, dd, np.minimum(large, 31))
    x[0:32, 1024:1408] = (bucket[None, :] == np.arange(32)[:, None])
    ok = np.stack([(d >= 0) & (d <= 128), (d >= 0) & (d % 4 == 0), (d >= 0) & (d % 16 == 0)])
    x[0:24, 1408:1792] = np.where(np.repeat(ok, 8, 0), 0.0, NEG)
    return c, x


_BIG = ["ada_w", "ffn_w_in", "ffn_w_out", "hyb_w_in", "hyb_w_out", "pool_w", "att_w_qkv", "att_w_out",
        "even_w_in_2", "s5_w_glu_2", "even_w_out_2", "odd_w_in_2", "odd_w_out_2",
        "moe_w_gate_2", "moe_w_up_2", "moe_w_down_2"]


def kernel(**inputs):
    import concourse.bacc as bacc
    from concourse.bass_utils import run_bass_kernel_spmd

    f = {k: np.asarray(v) for k, v in inputs.items()}

    def cols(v):
        return np.asarray(v).reshape(-1, P).T

    def on8(v):
        r = np.zeros((P, 1), np.float32)
        r[0:8, 0] = v.reshape(-1)
        return r

    pr = np.zeros((P, PN), np.float32)

    def put(name, v):
        at, n = PO[name]
        pr[:, at:at + n] = v

    put("c", cols(f["c"]))
    put("npre", cols(f["norm_pre"]))
    put("npost", cols(f["norm_post"]))
    put("adab", cols(f["ada_b"]))
    put("pscale", cols(f["pool_scale"]))
    put("lbl", cols(f["hgrn_lb_logits"]))
    put("onorm", cols(f["hgrn_out_norm"]))
    put("lng", cols(f["ln_g_2"]))
    put("lnb", cols(f["ln_b_2"]))
    put("are", cols(f["s5_a_re_2"]))
    put("aim", cols(f["s5_a_im_2"]))
    put("ldt", cols(np.repeat(f["s5_log_dt_2"].reshape(-1), 64)))
    put("s5d", cols(f["s5_d_2"]))
    put("bglu", cols(f["s5_b_glu_2"]))
    put("convw", cols(f["mlstm_conv_w_2"]))
    put("convb", cols(f["mlstm_conv_b_2"]))
    rb = np.concatenate([f["moe_b_group_2"], f["moe_b_expert_2"].reshape(2, 16)], 1).reshape(1, 40)
    put("rb", np.broadcast_to(rb, (P, 40)))
    put("fb", np.concatenate([on8(f["fox_f_bias_2"]), on8(f["mlstm_i_bias_2"]), on8(f["mlstm_f_bias_2"])], 1))
    for n, s in (("bre", "s5_b_re_2"), ("bim", "s5_b_im_2")):
        put(n, f[s].reshape(16, P, 16).transpose(1, 0, 2).reshape(P, 256))
    for n, s in (("cre", "s5_c_re_2"), ("cim", "s5_c_im_2")):
        put(n, f[s].reshape(4, P, 64).transpose(1, 0, 2).reshape(P, 256))
    wr = np.concatenate([f["moe_w_group_2"].reshape(2, 8, P, 4),
                         f["moe_w_expert_2"].reshape(2, 4, 8, P, 4).transpose(0, 2, 3, 1, 4).reshape(2, 8, P, 16)], 3)
    put("wr", wr.transpose(2, 0, 1, 3).reshape(P, 320))
    ct, ax = shape_constants()
    at = AO["relb"][0]
    ax[0:32, at:at + 24] = f["rel_bias"]

    nc = bacc.Bacc("TRN2", target_bir_lowering=False, num_devices=1)
    arrays = {"params": pr, "consts": ct, "aux": ax, "x": np.ascontiguousarray(f["x"].reshape(S, D))}
    for n in _BIG:
        arrays[n] = np.ascontiguousarray(f[n])
    aps = {n: nc.dram_tensor(n, v.shape, mybir.dt.from_np(v.dtype), kind="ExternalInput").ap()
           for n, v in arrays.items()}
    out = nc.dram_tensor("out_x", (S, D), F32, kind="ExternalOutput").ap()
    build(nc, aps, out)
    r = run_bass_kernel_spmd(nc, [arrays], core_ids=[0])
    return r.results[0]["out_x"].reshape(1, S, D)
```

```python
import math
from contextlib import ExitStack

import numpy as np
import concourse.bass as bass
from concourse import mybir

ALU = mybir.AluOpType
ACTF = mybir.ActivationFunctionType
F32 = mybir.dt.float32
F32R = mybir.dt.float32r
I32 = mybir.dt.int32
AX = mybir.AxisListType

P = 128
S = 256
D = 1024
NEG = -1.0e30
NF = 11
NRAW = 4
NSPLIT = 5
ARENA = 16128
RSQRT_SEED = float(0x5F3759DF)
DN_ALPHA = 4.0 ** 0.25
TWO_PI = 2.0 * math.pi
BG = 1
ROUND = 1.5 * 2.0 ** 23

PARAM_COLS = [
    ("c", 8), ("npre", 32), ("npost", 32), ("adab", 96), ("pscale", 4), ("lbl", 4), ("onorm", 1),
    ("lng", 32), ("lnb", 32), ("are", 16), ("aim", 16), ("ldt", 16), ("s5d", 4), ("bglu", 4),
    ("convw", 64), ("convb", 16), ("rb", 40), ("fb", 3), ("bre", 256), ("bim", 256),
    ("cre", 256), ("cim", 256), ("wr", 320),
]
CONST_COLS = [("ident", 128), ("onesd", 128), ("causal", 128), ("hm", 896), ("hsel", 16), ("tt", 256),
              ("half", 2), ("firsts", 4)]
AUX_COLS = [("invc", 1024), ("onehot", 384), ("maskv", 384), ("relb", 24)]


def offsets(cols):
    out, at = {}, 0
    for name, n in cols:
        out[name] = (at, n)
        at += n
    return out, at


PO, PN = offsets(PARAM_COLS)
CO, CN = offsets(CONST_COLS)
AO, AN = offsets(AUX_COLS)


class Queue:

    def __init__(self, name, sem, link):
        self.name, self.sem, self.link = name, sem, link
        self.ops, self.n, self.seen, self.extra, self.open = [], 0, {}, [], False

    def last(self):
        assert not self.open
        return (self.name, self.sem, self.n)

    def do(self, fn, *waits, inc=True):
        todo = list(self.extra)
        self.extra = []
        if self.link and self.n:
            todo.append((self.name, self.sem, self.n))
        stack = list(waits)
        while stack:
            w = stack.pop()
            if w is None:
                continue
            if isinstance(w, list):
                stack.extend(w)
            else:
                todo.append(w)
        need = {}
        for name, sem, val in todo:
            if val > self.seen.get(name, 0):
                self.seen[name] = val
                need[name] = (sem, val)
        self.ops.append((list(need.values()), fn, inc))
        self.open = not inc
        if inc:
            self.n += 1
            return (self.name, self.sem, self.n)
        return None

    def emit(self, eng):
        for waits, fn, inc in self.ops:
            for sem, val in waits:
                eng.wait_ge(sem, val)
            ins = fn(eng)
            if inc:
                ins.then_inc(self.sem, 1)


def weight_plan():
    out = []

    def k(name, n, c):
        out.extend([(name, "k", n, c, 0), (name, "k", n, c, 1)])

    def d(name, n, r):
        out.append((name, "d", n, r, 0))

    def cols(name, *ranges):
        for at, count in ranges:
            for i in range(count):
                k(name, (0,), at + i * 256)

    def pairs(gate, up, down):
        n = len(gate)
        for i in range(n + 1):
            if i < n:
                k(*gate[i])
                k(*up[i])
            if i:
                d(*down[i - 1])
                d(down[i - 1][0], down[i - 1][1], down[i - 1][2] + P)

    def rows(name, count):
        for i in range(count):
            d(name, (0,), i * P)

    for l in range(2):
        if l == 0:
            cols("hyb_w_in", (0, 10))
            rows("hyb_w_out", 8)
        else:
            cols("att_w_qkv", (0, 18))
            rows("att_w_out", 4)
        pairs([("ffn_w_in", (l,), i * 256) for i in range(NF)],
              [("ffn_w_in", (l,), 2816 + i * 256) for i in range(NF)],
              [("ffn_w_out", (l,), i * 256) for i in range(NF)])
    for l in range(2):
        if l == 0:
            cols("even_w_in_2", (1544, 2), (0, 2), (512, 2), (1024, 2))
            rows("even_w_out_2", 8)
        else:
            cols("odd_w_in_2", (0, 16))
            rows("odd_w_out_2", 8)
        pairs([("moe_w_gate_2", (l, e), 0) for e in range(16)], [("moe_w_up_2", (l, e), 0) for e in range(16)],
              [("moe_w_down_2", (l, e), 0) for e in range(16)])
    return out


class Slots:

    def __init__(self, n, base=0):
        self.n, self.base, self.i = n, base, 0
        self.free = [[] for _ in range(n)]

    def take(self, k=1):
        i = self.i
        if i % k:
            i += k - i % k
        i %= self.n
        self.i = (i + k) % self.n
        waits = []
        for j in range(i, i + k):
            assert self.free[j] is not None, "taken and not given back"
            waits += self.free[j]
            self.free[j] = None
        return self.base + i, waits

    def give(self, i, *toks, k=1):
        for j in range(i - self.base, i - self.base + k):
            assert self.free[j] is None
            self.free[j] = [t for t in toks if t is not None]


def build(nc, a, out):
    ctx = ExitStack()
    with ctx:
        def sb(name, cols, dt=F32):
            return ctx.enter_context(nc.sbuf_tensor(name, [P, cols], dt))

        def sem(name):
            return ctx.enter_context(nc.semaphore(name))

        PSA = ctx.enter_context(nc.psum_tensor("PSA", [P, 2048], F32))
        PSB = ctx.enter_context(nc.psum_tensor("PSB", [P, 2048], F32))
        XT = sb("XT", 2048)
        XH = sb("XH", 2048, F32R)
        XL = sb("XL", 2048, F32R)
        GH = sb("GH", 2048, F32R)
        GL = sb("GL", 2048, F32R)
        ACC = sb("ACC", 1024)
        AD = sb("AD", 2048)
        T1 = sb("T1", 2048)
        T2 = sb("T2", 2048)
        RS = sb("RS", 1024)
        MC = sb("MC", 168)
        SM = sb("SM", 800)
        CT = sb("CT", CN)
        PR = sb("PR", PN)
        WR = sb("WR", NRAW * 1024)
        WH = sb("WH", NSPLIT * 1024, F32R)
        WL = sb("WL", NSPLIT * 1024, F32R)
        AR = sb("AR", ARENA)

        PE = Queue("pe", sem("s_pe"), False)
        ACT = Queue("act", sem("s_act"), True)
        DVE = Queue("dve", sem("s_dve"), True)
        POOL = Queue("pool", sem("s_pool"), True)
        SP = Queue("sp", sem("s_sp"), False)
        wsem = [sem(f"s_w{i}") for i in range(NRAW)]
        wcnt = [0] * NRAW
        asem = [sem(f"s_a{i}") for i in range(2)]
        acnt = [0] * 2
        s_in = sem("s_in")
        s_x = sem("s_x")
        s_aux = sem("s_aux")
        s_bias = sem("s_bias")
        s_tp = sem("s_tp")
        s_out = sem("s_out")

        scratch = nc.dram_tensor("bias_rows", [24, 384], F32, kind="Internal")

        def par(name, a0=0, n=None, p=P):
            at, w = PO[name]
            n = w - a0 if n is None else n
            return PR[0:p, at + a0:at + a0 + n]

        def cst(name, a0=0, n=None, p=P):
            at, w = CO[name]
            n = w - a0 if n is None else n
            return CT[0:p, at + a0:at + a0 + n]

        ident = cst("ident")
        onesd = cst("onesd")

        W = Slots(NRAW)
        WS = Slots(NSPLIT)
        WA = Slots(2)
        PS = Slots(4)
        PT = Slots(2, base=6)

        def bank(b, lo=0, hi=512, p=P, p0=0):
            t = PSA if b < 4 else PSB
            o = (b % 4) * 512
            return t[p0:p0 + p, o + lo:o + hi]

        def wslot(i):
            return WR[:, i * 1024:(i + 1) * 1024]

        arena = [0]

        def take(n):
            at = arena[0]
            arena[0] += n
            assert arena[0] <= ARENA, arena[0]
            return AR[:, at:at + n]

        def fence():
            toks = [q.last() for q in (PE, ACT, DVE, POOL) if q.n]
            for q in (PE, ACT, DVE, POOL):
                q.extra = [t for t in toks if t[0] != q.name]
            arena[0] = 0

        def mm(o, l, r, start, stop, *waits, inc=False, skip=False):
            return PE.do(lambda e: e.matmul(o, l, r, start=start, stop=stop, skip_group_check=skip),
                         *waits, inc=inc)

        def tr(o, i, n, *waits, inc=False):
            return PE.do(lambda e: e.transpose(o, i, ident[0:n, 0:n]), *waits, inc=inc)

        def act(o, i, f, *waits, bias=0.0, scale=1.0, accum=None):
            if accum is None:
                return ACT.do(lambda e: e.activation(o, i, f, bias=bias, scale=scale), *waits)
            return ACT.do(lambda e: e.activation(o, i, f, bias=bias, scale=scale, accum_out=accum), *waits)

        def ts(o, i, s1, s2, op0, op1=None, *waits, q=None):
            q = q or DVE
            if op1 is None:
                return q.do(lambda e: e.tensor_scalar(o, i, s1, None, op0), *waits)
            return q.do(lambda e: e.tensor_scalar(o, i, s1, s2, op0, op1), *waits)

        def stt(o, i, s, j, op0, op1, *waits):
            return DVE.do(lambda e: e.scalar_tensor_tensor(out=o, in0=i, scalar=s, in1=j, op0=op0, op1=op1), *waits)

        def tt(o, i, j, op, *waits, q=None):
            q = q or DVE
            return q.do(lambda e: e.tensor_tensor(o, i, j, op), *waits)

        def cp(o, i, *waits, q=None):
            if q is ACT:
                return ACT.do(lambda e: e.copy(o, i), *waits)
            return (q or DVE).do(lambda e: e.tensor_copy(o, i), *waits)

        def scan(o, x, y, init, op0, op1, *waits):
            return DVE.do(lambda e: e.tensor_tensor_scan(o, x, y, init, op0, op1), *waits)

        def red(o, i, op, *waits):
            return DVE.do(lambda e: e.tensor_reduce(o, i, AX.X, op), *waits)

        def recip(o, i, *waits):
            return DVE.do(lambda e: e.reciprocal(o, i), *waits)

        def v3(ap, n):
            return ap.rearrange("p (a b) -> p a b", a=n)

        def v4(ap, n, m):
            return ap.rearrange("p (a b c) -> p a b c", a=n, b=m)

        def rep(ap, n):
            return ap.unsqueeze(1).to_broadcast([ap.shape[0], n, ap.shape[1]])

        def wide(ap, n):
            return ap.unsqueeze(2).to_broadcast([ap.shape[0], ap.shape[1], n])

        def row_of(e, k):
            return ident[0:k, e:e + 1].to_broadcast([k, P])

        def load(src, cols=1024, k=4, p=P):
            i, waits = W.take()
            dst = v3(wslot(i)[0:p, 0:cols], k) if k > 1 else wslot(i)[0:p, 0:cols]
            SP.do(lambda e: e.dma_start(dst, src).then_inc(wsem[i], 16), waits, inc=False)
            wcnt[i] += 16
            return i, dst, (f"w{i}", wsem[i], wcnt[i])

        def source(key):
            name, kind, n, at, half = key
            m = a[name] if n is None else a[name][n[0]] if len(n) == 1 else a[name][n[0], n[1]]
            if kind == "k":
                return m[half * 512:half * 512 + 512, at:at + 256].rearrange("(k p) n -> p k n", p=P), 4
            return m[at:at + P, 0:1024], 1

        plan = weight_plan()
        raws, splits, popped = [], [], [0]

        def want_raw():
            if len(raws) < len(plan):
                src, k = source(plan[len(raws)])
                raws.append(load(src, k=k))

        def want_split():
            n = len(splits)
            if n >= len(plan):
                return
            while len(raws) <= n:
                want_raw()
            i, _, tok = raws[n]
            j, waits = WS.take()
            h, l = WH[:, j * 1024:(j + 1) * 1024], WL[:, j * 1024:(j + 1) * 1024]
            th = ACT.do(lambda e: e.copy(h, wslot(i)), tok, waits)
            tl = tt(l, wslot(i), h.bitcast(F32), ALU.subtract, th)
            W.give(i, tl)
            splits.append((j, h, l, tl))
            want_raw()

        def pop(name, kind, n, at, half):
            key = plan[popped[0]]
            assert key == (name, kind, n, at, half), (key, (name, kind, n, at, half))
            while len(splits) < min(len(plan), popped[0] + 5):
                want_split()
            res = splits[popped[0]]
            popped[0] += 1
            background()
            return res

        xh, xl = v3(XH[:, :], 8), v3(XL[:, :], 8)
        gh, gl = v3(GH[:, :], 8), v3(GL[:, :], 8)
        xt = v3(XT[:, :], 8)

        def mm3(o, lh, ll, rh, rl, start, stop, *waits, inc=False):
            mm(o, lh, rh, start, False, *waits, skip=True)
            mm(o, lh, rl, False, False, skip=True)
            return mm(o, ll, rh, False, stop, inc=inc, skip=True)

        def split(h, l, src, tok):
            t = ACT.do(lambda e: e.copy(h, src), tok)
            return tt(l, src, h.bitcast(F32), ALU.subtract, t)

        def fm(name, n, c, htok):
            b, waits = PS.take()
            for half in range(2):
                j, h, l, tok = pop(name, "k", n, c, half)
                h, l = v3(h, 4), v3(l, 4)
                for f in range(2):
                    for k in range(4):
                        kk = 4 * half + k
                        t = mm3(bank(b, f * 256, f * 256 + 256), h[:, k, f * P:(f + 1) * P],
                                l[:, k, f * P:(f + 1) * P], xh[:, kk, :], xl[:, kk, :],
                                half == f == k == 0, kk == 7, waits, tok, htok[kk], inc=(f == 1 and k == 3))
                WS.give(j, t)
            return b, t

        def tm(name, n, c, htok):
            b, waits = PS.take()
            for half in range(2):
                j, h, l, tok = pop(name, "k", n, c, half)
                h, l = v3(h, 4), v3(l, 4)
                for m in range(2):
                    for k in range(4):
                        kk = 4 * half + k
                        sl = slice(m * P, (m + 1) * P)
                        t = mm3(bank(b, m * 256, m * 256 + 256), xh[:, kk, sl], xl[:, kk, sl], h[:, k, :],
                                l[:, k, :], half == m == k == 0, kk == 7, waits, tok, htok[kk],
                                inc=(m == 1 and k == 3))
                WS.give(j, t)
            return b, t

        acc_free = [[]]

        def down(name, n, r, h_, l_, first, last, *waits):
            j, h, l, tok = pop(name, "d", n, r, 0)
            for f in range(8):
                o = bank(4 + f // 2, (f % 2) * 256, (f % 2) * 256 + 256)
                fs = slice(f * P, (f + 1) * P)
                t = mm3(o, h[:, fs], l[:, fs], h_, l_, first and f % 2 == 0, last, list(waits), tok,
                        acc_free[0] if first else None, inc=(f == 7))
            WS.give(j, t)
            return t

        yacc = v3(PSB[:, :], 8)

        V, Y, A_, B_ = (RS[:, i * 256:(i + 1) * 256] for i in range(4))

        def rsqrt(ps, eps, n, tok):
            v, y, t = V[0:n, :], Y[0:n, :], A_[0:n, :]
            done = ts(v, ps, eps, None, ALU.add, None, tok)
            ts(y.bitcast(I32), v.bitcast(I32), -0.5, RSQRT_SEED, ALU.mult, ALU.add)
            for _ in range(3):
                tt(t, y, y, ALU.mult)
                stt(t, t, -0.5, v, ALU.mult, ALU.mult)
                last = stt(y, t, 1.5, y, ALU.add, ALU.mult)
            return y, last, done

        def mean(src, toks):
            b, waits = PS.take()
            o = bank(b, 0, 256)
            for j in range(8):
                t = mm(o, onesd, src[:, j, :], j == 0, j == 7, waits, toks[j], inc=(j == 7))
            return b, o, t

        def square(src, toks):
            t1 = v3(T1[:, :], 8)
            res = []
            for j in range(0, 8, 2):
                t = act(t1[:, j:j + 2, :], src[:, j:j + 2, :], ACTF.Square, toks[j], toks[j + 1])
                res += [t, t]
            return t1, res

        def rms(src, toks):
            t1, sq = square(src, toks)
            b, ps, t = mean(t1, sq)
            r, rt, done = rsqrt(ps, 1e-6, P, t)
            PS.give(b, done)
            return r, rt

        SP.do(lambda e: e.dma_start(CT[:, :], a["consts"]).then_inc(s_in, 16), inc=False)
        SP.do(lambda e: e.dma_start(PR[:, :], a["params"]).then_inc(s_in, 16), inc=False)
        in_tok = ("in", s_in, 32)
        for m in range(2):
            SP.do(lambda e, m=m: e.dma_start(T2[:, m * 1024:(m + 1) * 1024], a["x"][m * P:(m + 1) * P, :])
                  .then_inc(s_x, 16), inc=False)
        for q in (PE, ACT, DVE, POOL):
            q.extra = [in_tok]
        x_tok = ("x", s_x, 32)

        xtok = [None] * 8
        for j in range(0, 8, 2):
            b, waits = PS.take()
            for jj in range(2):
                for m in range(2):
                    t = tr(bank(b, jj * 256 + m * P, jj * 256 + m * P + P),
                           T2[:, m * 1024 + (j + jj) * P:m * 1024 + (j + jj + 1) * P], P,
                           waits, x_tok, inc=(jj == m == 1))
            t = cp(XT[:, j * 256:(j + 2) * 256], bank(b), t, q=ACT)
            xtok[j] = xtok[j + 1] = t
            PS.give(b, t)

        csil = SM[:, 0:8]
        ct = act(csil, par("c"), ACTF.Silu)
        ct = ts(csil, csil, float(D), None, ALU.mult, None, ct)
        mod_tok = {}

        def ada_dma(n, part, k):
            i, waits = WA.take()
            dst = AD[:, i * 1024:(i + 1) * 1024]
            src = a["ada_w"][n // 2, n % 2][k * P:(k + 1) * P, part * 1024:(part + 1) * 1024]
            SP.do(lambda e: e.dma_start(dst, src).then_inc(asem[i], 16), waits, inc=False)
            acnt[i] += 16
            return i, dst, (f"a{i}", asem[i], acnt[i])

        def ada():
            steps = [(n, part, k) for n in range(4) for part in (1, 0, 2) for k in range(8)]
            got = [ada_dma(*steps[0])]
            acc_tok = None
            for x, (n, part, k) in enumerate(steps):
                if x + 1 < len(steps):
                    got.append(ada_dma(*steps[x + 1]))
                i, w, tok = got.pop(0)
                if k == 0:
                    t = ts(ACC[:, :], w, csil[:, 0:1], None, ALU.mult, None, tok, acc_tok)
                else:
                    t = stt(ACC[:, :], w, csil[:, k:k + 1], ACC[:, :], ALU.mult, ALU.add, tok)
                WA.give(i, t)
                if k == 7:
                    b, waits = PS.take()
                    for f in range(8):
                        t = mm(bank(b, f, f + 1), ACC[:, f * P:(f + 1) * P], onesd[:, 0:1], True, True, waits,
                               t if f == 0 else None, inc=(f == 7))
                    acc_tok = t
                    m = MC[:, n * 24 + part * 8:n * 24 + part * 8 + 8]
                    t = tt(m, bank(b, 0, 8), par("adab", n * 24 + part * 8, 8), ALU.add, t)
                    PS.give(b, t)
                    if part == 1:
                        t = stt(m, m, 1.0, par("npre", n * 8, 8), ALU.add, ALU.mult)
                    if part == 2:
                        t = tt(m, m, par("npost", n * 8, 8), ALU.mult)
                    mod_tok[n, part] = t
                yield
            while True:
                yield

        ada_run = ada()

        def background():
            for _ in range(BG):
                next(ada_run)

        def modulation(n, part):
            while (n, part) not in mod_tok:
                next(ada_run)
            return MC[:, n * 24 + part * 8:n * 24 + part * 8 + 8], mod_tok[n, part]

        def pre(n, xtok):
            r, rt = rms(xt, xtok)
            sc, t1 = modulation(n, 1)
            shift, t2_ = modulation(n, 0)
            t2 = v3(T2[:, :], 8)
            htok = []
            for j in range(8):
                t = stt(t2[:, j, :], xt[:, j, :], sc[:, j:j + 1], r, ALU.mult, ALU.mult)
                th = act(xh[:, j, :], t2[:, j, :], ACTF.Identity, t, t2_, bias=shift[:, j:j + 1])
                htok.append(stt(xl[:, j, :], t2[:, j, :], shift[:, j:j + 1], xh[:, j, :].bitcast(F32),
                                ALU.add, ALU.subtract, th))
            return htok

        def post(n, ytok):
            r, rt = rms(yacc, [ytok] * 8)
            g, _ = modulation(n, 2)
            t2 = v3(T2[:, :], 8)
            res = []
            for j in range(8):
                t = stt(t2[:, j, :], yacc[:, j, :], g[:, j:j + 1], r, ALU.mult, ALU.mult)
                last = tt(xt[:, j, :], xt[:, j, :], t2[:, j, :], ALU.add)
                res.append(last)
                if n == 3:
                    res[-1] = split(xh[:, j, :], xl[:, j, :], xt[:, j, :], last)
            acc_free[0] = [last, ACT.last()]
            return res

        def layer_norm(n, ytok):
            t2 = v3(T2[:, :], 8)
            tk = []
            for j in range(0, 8, 2):
                t = stt(t2[:, j:j + 2, :], xt[:, j:j + 2, :], DN_ALPHA, yacc[:, j:j + 2, :], ALU.mult, ALU.add, ytok)
                tk += [t, t]
            acc_free[0] = [t]
            b, ps, t = mean(t2, tk)
            cen = []
            for j in range(0, 8, 2):
                t = tt(t2[:, j:j + 2, :], t2[:, j:j + 2, :], rep(ps, 2), ALU.subtract, t)
                cen += [t, t]
            PS.give(b, t)
            t1, sq = square(t2, cen)
            b, ps, t = mean(t1, sq)
            r, rt, done = rsqrt(ps, 1e-5, P, t)
            PS.give(b, done)
            res = []
            for j in range(8):
                t = stt(t2[:, j, :], t2[:, j, :], par("lng", n * 8 + j, 1), r, ALU.mult, ALU.mult)
                lb = par("lnb", n * 8 + j, 1)
                th = act(xh[:, j, :], t2[:, j, :], ACTF.Identity, t, bias=lb)
                act(xt[:, j, :], t2[:, j, :], ACTF.Identity, bias=lb)
                res.append([stt(xl[:, j, :], t2[:, j, :], lb, xh[:, j, :].bitcast(F32), ALU.add, ALU.subtract, th),
                            ACT.last()])
            return res

        def gated(pairs, htok, spread=None, bt=None):
            tmp = [v3(take(512), 2) for _ in range(2)]
            hfree = [None, None]
            pend = None
            n = len(pairs)

            def finish(p):
                i, hb, t = p
                for k in range(2):
                    t = down(*pairs[i][2 + k], gh[:, 2 * hb + k, :], gl[:, 2 * hb + k, :], i == k == 0,
                             i == n - 1 and k == 1, t)
                return t

            for i, (g, u, _, _) in enumerate(pairs):
                hb = i % 2
                bg, tg = fm(*g, htok)
                ta = act(tmp[hb], v3(bank(bg), 2), ACTF.Silu, tg)
                PS.give(bg, ta)
                if spread is not None:
                    ta = tt(tmp[hb], tmp[hb], wide2(spread[:, i, :]), ALU.mult, ta, bt, q=POOL)
                bu, tu = fm(*u, htok)
                th = tt(tmp[hb], tmp[hb], v3(bank(bu), 2), ALU.mult, ta, tu)
                PS.give(bu, th)
                th = split(gh[:, 2 * hb:2 * hb + 2, :], gl[:, 2 * hb:2 * hb + 2, :], tmp[hb], [th, hfree[hb]])
                if pend:
                    td = finish(pend)
                    hfree[pend[1]] = td
                pend = (i, hb, th)
            return finish(pend)

        def wide2(ap):
            return rep(ap, 2)

        def ffn(l, htok):
            return gated([(("ffn_w_in", (l,), i * 256), ("ffn_w_in", (l,), 2816 + i * 256),
                           ("ffn_w_out", (l,), i * 256), ("ffn_w_out", (l,), i * 256 + P))
                          for i in range(NF)], htok)

        def hybrid(htok):
            H = "hyb_w_in"
            invc = take(1024)
            SP.do(lambda e: e.dma_start(invc, a["aux"][:, 0:1024]).then_inc(s_aux, 16), inc=False)
            inv_tok = ("aux", s_aux, 16)
            U = v3(take(4 * 272), 4)
            w2, w4, w8 = (v3(take(4 * 272), 4) for _ in range(3))
            z = [DVE.do(lambda e, x=x: e.memset(x, 0.0)) for x in
                 (U[:, :, 0:16],)]
            for s in range(2):
                b, t = fm(H, (0,), s * 256, htok)
                tu = cp(U[:, 2 * s:2 * s + 2, 16:272], v3(bank(b), 2), t, z)
                PS.give(b, tu)
            Qh = take(1024)
            Kh = take(1024)
            Fh = take(1024)
            Sg = take(1024)
            lb = SM[:, 16:20]
            om = SM[:, 20:24]
            e0 = SM[:, 24:28]
            tt(e0, par("lbl"), par("lbl"), ALU.subtract)
            te = act(e0, e0, ACTF.Exp, DVE.last())
            recip(lb, e0, te)
            tt(lb, lb, e0, ALU.mult)
            tt(lb, lb, lb, ALU.subtract)
            ts(lb, lb, 0.0, None, ALU.max)
            ts(om, lb, -1.0, 1.0, ALU.mult, ALU.add)
            for s in range(2):
                b, t = fm(H, (0,), 512 + s * 256, htok)
                tq = act(Qh[:, s * 512:(s + 1) * 512], bank(b), ACTF.Silu, t)
                PS.give(b, tq)
            for s in range(2):
                b, t = fm(H, (0,), 1024 + s * 256, htok)
                sl = slice(s * 512, (s + 1) * 512)
                t1 = act(Fh[:, sl], bank(b), ACTF.Sigmoid, t)
                t2 = act(Kh[:, sl], bank(b), ACTF.Sigmoid, scale=-1.0)
                PS.give(b, t2)
            for h in range(4):
                sl = slice(h * 256, (h + 1) * 256)
                ts(Fh[:, sl], Fh[:, sl], om[:, h:h + 1], lb[:, h:h + 1], ALU.mult, ALU.add, t2)
                tf = ts(Kh[:, sl], Kh[:, sl], om[:, h:h + 1], None, ALU.mult)
            Vt = v3(take(1024), 2)
            for s in range(2):
                b, t = tm(H, (0,), 1536 + s * 256, htok)
                tv = cp(Vt[:, :, s * 256:(s + 1) * 256], v3(bank(b), 2), t, q=ACT)
                PS.give(b, tv)
            for s in range(2):
                b, t = fm(H, (0,), 2048 + s * 256, htok)
                tg = act(Sg[:, s * 512:(s + 1) * 512], bank(b), ACTF.Silu, t)
                PS.give(b, tg)

            tt(w2[:, :, 1:272], U[:, :, 1:272], U[:, :, 0:271], ALU.add, tu)
            tt(w4[:, 1:4, 3:272], w2[:, 1:4, 3:272], w2[:, 1:4, 1:270], ALU.add)
            tt(w8[:, 2:4, 7:272], w4[:, 2:4, 7:272], w4[:, 2:4, 3:268], ALU.add)
            tt(w2[:, 3:4, 16:272], w8[:, 3:4, 16:272], w8[:, 3:4, 8:264], ALU.add)
            dif = v3(take(1024), 4)
            ic = v3(invc, 4)
            for g, wsrc in enumerate((w2, w4, w8, w2)):
                tt(dif[:, g, :], wsrc[:, g, 16:272], ic[:, g, :], ALU.mult, inv_tok)
            td = tt(dif, dif, U[:, :, 16:272], ALU.subtract)
            YP = v3(take(1024), 4)
            pi, pw, ptok = load(a["pool_w"][0].rearrange("g c d -> c g d"), cols=512, k=4)
            for s in range(2):
                b, waits = PS.take()
                for gg in range(2):
                    g = 2 * s + gg
                    t = mm(bank(b, gg * 256, gg * 256 + 256), pw[:, g, :], dif[:, g, :], True, True,
                           waits, ptok, td, inc=(gg == 1))
                for gg in range(2):
                    g = 2 * s + gg
                    ty = act(YP[:, g, :], bank(b, gg * 256, gg * 256 + 256), ACTF.Copy, t,
                             scale=par("pscale", g, 1))
                PS.give(b, ty)
            W.give(pi, t)
            typ = split(gh[:, 0:4, :], gl[:, 0:4, :], YP, ty)

            Am = v3(take(1024), 8)
            A2 = v3(take(512), 4)
            q4, k4 = v3(Qh, 4), v3(Kh, 4)
            tot = Fh
            nxt = take(512)
            spare = take(256)
            ready = [tq, tf]
            levels = [0, 1, 2, 4, 8, 16, 32, 64]
            for li, h in enumerate(levels):
                if h == 1:
                    tq1 = tt(Qh, Qh, Fh, ALU.mult, t_mm)
                    ready = [tq1]
                if h > 1:
                    g = h // 2
                    n = 1024 // h
                    qv = Qh.rearrange("p (n b c) -> p n b c", n=n, b=2)
                    kv = Kh.rearrange("p (n b c) -> p n b c", n=n, b=2)
                    tv_ = tot[:, 0:2 * n].rearrange("p (n b) -> p n b", b=2)
                    tt(qv[:, :, 1, :], qv[:, :, 1, :], wide(tv_[:, :, 0], g), ALU.mult, t_mm)
                    tt(kv[:, :, 0, :], kv[:, :, 0, :], wide(tv_[:, :, 1], g), ALU.mult)
                    dst = nxt if tot is not nxt else spare
                    t = tt(dst[:, 0:n], tv_[:, :, 0], tv_[:, :, 1], ALU.mult)
                    tot = dst
                    ready = [t]
                for half in range(2):
                    b, waits = PS.take()
                    for x in range(4):
                        hd, m = 2 * half + x // 2, x % 2
                        t_mm = mm(bank(b, x * P, x * P + P), k4[:, hd, m * P:m * P + P],
                                  q4[:, hd, m * P:m * P + P], True, True, waits, ready, inc=(x == 3))
                    dst = Am[:, 4 * half:4 * half + 4, :]
                    if h == 0:
                        tm_ = tt(dst, v3(bank(b), 4), rep(ident, 4), ALU.mult, t_mm)
                    else:
                        mk = cst("hm", (li - 1) * P, P).bitcast(I32)
                        tm_ = DVE.do(lambda e, dst=dst, mk=mk, b=b: e.copy_predicated(
                            dst, rep(mk, 4), v3(bank(b), 4)), t_mm)
                    PS.give(b, tm_)
            n = 1024 // 128
            qv = Qh.rearrange("p (n b c) -> p n b c", n=n, b=2)
            kv = Kh.rearrange("p (n b c) -> p n b c", n=n, b=2)
            tv_ = tot[:, 0:2 * n].rearrange("p (n b) -> p n b", b=2)
            tt(qv[:, :, 1, :], qv[:, :, 1, :], wide(tv_[:, :, 0], 64), ALU.mult, t_mm)
            t = tt(kv[:, :, 0, :], kv[:, :, 0, :], wide(tv_[:, :, 1], 64), ALU.mult)
            b, waits = PS.take()
            for hd in range(4):
                t = mm(bank(b, hd * P, hd * P + P), k4[:, hd, 0:P], q4[:, hd, P:2 * P], True, True,
                       waits, t, inc=(hd == 3)) or t
            t2 = cp(A2, v3(bank(b), 4), t, q=ACT)
            PS.give(b, t2)
            b, waits = PS.take(2)
            o = PSA[:, b * 512:b * 512 + 1024]
            for hd in range(4):
                c = hd * 256
                vh = slice(hd * P, hd * P + P)
                mm(o[:, c:c + P], Vt[:, 0, vh], Am[:, 2 * hd, :], True, True, waits, t2, tm_, tv)
                mm(o[:, c + P:c + 256], Vt[:, 1, vh], Am[:, 2 * hd + 1, :], True, False)
                t = mm(o[:, c + P:c + 256], Vt[:, 0, vh], A2[:, hd, :], False, True, inc=True)
            sq = T1[:, 0:1024]
            t = act(sq, o, ACTF.Square, t)
            b2, waits = PS.take()
            st = bank(b2, 0, 256, p=4)
            for hd in range(4):
                ti = mm(st, cst("hsel", 4 * hd, 4), sq[:, hd * 256:hd * 256 + 256], hd == 0, hd == 3,
                        waits, t, inc=(hd == 3))
            r, rt, done = rsqrt(st, 1e-6, 4, ti)
            PS.give(b2, done)
            YH = take(1024)
            t1 = stt(YH, o, par("onorm"), Sg, ALU.mult, ALU.mult, tg)
            PS.give(b, t1, k=2)
            b, waits = PS.take(2)
            for hd in range(4):
                t = mm(PSA[:, b * 512 + hd * 256:b * 512 + hd * 256 + 256], row_of(hd, 4), r,
                       True, True, waits, rt, inc=(hd == 3))
            th = tt(YH, YH, PSA[:, b * 512:b * 512 + 1024], ALU.mult, t)
            PS.give(b, th, k=2)
            th = split(gh[:, 4:8, :], gl[:, 4:8, :], v3(YH, 4), th)
            for s in range(8):
                t = down("hyb_w_out", (0,), s * P, gh[:, s, :], gl[:, s, :], s == 0, s == 7, typ if s < 4 else th)
            return t

        def attend(units, scores, soft, blocks, value, pts):
            NB = 2
            pfree = [None] * NB
            st = {}
            done = None

            def transposes(u):
                pr, tk = st[u]["p"]
                n = blocks(units[u])
                if n <= 4:
                    b, waits = PT.take()
                    kk = 1
                else:
                    b, waits = PT.take(2)
                    kk = 2
                for x in range(n):
                    t = tr(bank(b + x // 4, (x % 4) * P, (x % 4) * P + P), pr[:, x * P:(x + 1) * P], P,
                           waits, tk, inc=(x == n - 1))
                dst = pts[u % NB]
                o = (b - 4) * 512
                t2 = cp(dst[:, 0:n * P], PSB[:, o:o + n * P], t, pfree[u % NB], q=ACT)
                PT.give(b, t2, k=kk)
                st[u]["pt"] = (dst, t2)
                return t

            N = len(units)
            for u in range(N + 2):
                if u < N:
                    st[u] = {"s": scores(units[u])}
                    st[u]["p"] = soft(units[u], st[u]["s"])
                if 2 <= u:
                    done = value(units[u - 2], *st[u - 2]["pt"])
                    pfree[u % NB] = done
                if 1 <= u <= N:
                    st[u - 1]["tt"] = transposes(u - 1)
                    sfree[0][units[u - 1][2] % 3] = st[u - 1]["tt"]
            return done

        sfree = [[None] * 3]

        def dilated(htok):
            wq = "att_w_qkv"
            ai, aux, atok = load(a["aux"][:, 1024:AN], cols=AN - 1024, k=1)
            b, waits = PS.take()
            oh = aux[0:32, 0:384]
            mv = aux[0:24, 384:768]
            rb = aux[0:32, 768:792]
            t = mm(bank(b, 0, 384, p=24), rb, oh, True, True, waits, atok, inc=True)
            brow = SM[0:24, 64:448]
            t = tt(brow, bank(b, 0, 384, p=24), mv, ALU.add, t, atok)
            W.give(ai, t)
            PS.give(b, t)
            ACT.do(lambda e: e.dma_start(scratch[:, :], brow).then_inc(s_bias, 16), t, inc=False)
            ACT.open = False
            bt = take(6144)
            src = bass.AP(scratch, 0, [[1, P], [384, 24], [1, 256]])
            ACT.do(lambda e: e.dma_start(v3(bt, 24), src).then_inc(s_tp, 16), ("bias", s_bias, 16), inc=False)
            ACT.open = False
            btok = ("tp", s_tp, 16)

            def bias_of(h, n):
                pp = [list(x) for x in bt.ap][0]
                return bass.AP(bt.tensor, bt.offset + h * 256 + n - 1, [pp, [8 * 256, 3], [-1, n]])

            qf = v3(take(3072), 12)
            kf = v3(take(3072), 12)
            vt = v3(take(3072), 2)
            for s in range(6):
                b, t = fm(wq, (0,), s * 256, htok)
                tq = act(qf[:, 2 * s:2 * s + 2, :], v3(bank(b), 2), ACTF.Copy, t, scale=0.125)
                PS.give(b, tq)
            for s in range(6):
                b, t = fm(wq, (0,), 1536 + s * 256, htok)
                tk = cp(kf[:, 2 * s:2 * s + 2, :], v3(bank(b), 2), t)
                PS.give(b, tk)
            for s in range(6):
                b, t = tm(wq, (0,), 3072 + s * 256, htok)
                tv = cp(vt[:, :, s * 256:s * 256 + 256], v3(bank(b), 2), t)
                PS.give(b, tv)

            Sb = [T1[:, 0:768], T1[:, 768:1536], T2[:, 0:768]]
            pts = [T2[:, 768:1536], take(768)]
            sfree[0] = [None] * 3
            mx = SM[:, 448:464]
            den = SM[:, 464:480]
            rd = SM[:, 480:496]
            units = [(qt, h, 8 * qt + h) for qt in range(2) for h in range(8)]

            def scores(u):
                qt, h, i = u
                n = (qt + 1) * P
                b, waits = PS.take(2)
                o = (h % 2) * 64
                for g in range(3):
                    tile = g * 4 + h // 2
                    t = mm(PSA[:, b * 512 + g * 256:b * 512 + g * 256 + n],
                           qf[o:o + 64, tile, qt * P:qt * P + P], kf[o:o + 64, tile, 0:n],
                           True, True, waits, tq, tk, inc=(g == 2))
                return b, t

            def soft(u, s):
                qt, h, i = u
                b, t = s
                n = (qt + 1) * P
                sbf = Sb[i % 3][:, 0:3 * n]
                ps = v3(PSA[:, b * 512:b * 512 + 768], 3)[:, :, 0:n]
                t = tt(v3(sbf, 3), ps, bias_of(h, n), ALU.add, t, btok, sfree[0][i % 3])
                PS.give(b, t, k=2)
                red(mx[:, i:i + 1], sbf, ALU.max)
                t = ts(mx[:, i:i + 1], mx[:, i:i + 1], -1.0, None, ALU.mult)
                t = act(sbf, sbf, ACTF.Exp, t, bias=mx[:, i:i + 1], accum=den[:, i:i + 1])
                return sbf, t

            def value(u, pt, tok):
                qt, h, i = u
                x = 0
                for g in range(3):
                    for kt in range(qt + 1):
                        c = g * 512 + h * 64
                        t = mm(bank(4 + qt, h * 64, h * 64 + 64), pt[:, x * P:(x + 1) * P],
                               vt[:, kt, c:c + 64], x == 0, x == 3 * (qt + 1) - 1, tok, tv,
                               acc_free[0], inc=(x == 3 * (qt + 1) - 1))
                        x += 1
                return t

            done = attend(units, scores, soft, lambda u: 3 * (u[0] + 1), value, pts)
            ot = T1[:, 0:1024]
            recip(rd, den, ACT.last())
            for qt in range(2):
                td = tt(v3(ot[:, qt * 512:(qt + 1) * 512], 8), v3(bank(4 + qt), 8),
                        wide(rd[:, 8 * qt:8 * qt + 8], 64), ALU.mult, done)
            return project_tokens(ot, td, "att_w_out", True)

        def to_features(ot, td):
            res = []
            for f in range(0, 4, 2):
                b, waits = PS.take()
                for ff in range(2):
                    for m in range(2):
                        t = tr(bank(b, ff * 256 + m * P, ff * 256 + m * P + P),
                               ot[:, m * 512 + (f + ff) * P:m * 512 + (f + ff + 1) * P], P,
                               waits, td, inc=(ff == m == 1))
                t = split(gh[:, f:f + 2, :], gl[:, f:f + 2, :], v3(bank(b), 2), t)
                PS.give(b, t)
                res += [t, t]
            return res

        def project_tokens(ot, td, wout, last):
            tf = to_features(ot, td)
            acc_free[0] = acc_free[0] + [td]
            for s in range(4):
                t = down(wout, (0,), s * P, gh[:, s, :], gl[:, s, :], s == 0, last and s == 3, tf[s])
            return t

        def log_sigmoid(x, t0, t1, tok):
            stt(t0, x, -1.0, x, ALU.mult, ALU.min, tok)
            t = act(t0, t0, ACTF.Exp, DVE.last())
            t = act(t0, t0, ACTF.Ln, bias=1.0)
            return stt(x, x, 0.0, t0, ALU.min, ALU.subtract, t)

        def fox(xtok):
            wi = a["even_w_in_2"][0]
            src = xt
            qf, kf, uf = (v3(take(1024), 4) for _ in range(3))
            vt = v3(take(1024), 2)
            cf = take(256)[0:8, :]
            cw = take(256)[0:8, :]
            gi, gw, gtok = load(wi[:, 1536:1544].rearrange("(k p) n -> p k n", p=P), cols=64, k=8)
            b, waits = PS.take()
            for k in range(8):
                t = mm(bank(b, 0, 256, p=8), gw[:, k, :], src[:, k, :], k == 0, k == 7, waits, gtok,
                       xtok[k], inc=(k == 7))
            W.give(gi, t)
            t = ts(cf, bank(b, 0, 256, p=8), par("fb", 0, 1, p=8), None, ALU.add, None, t)
            PS.give(b, t)
            t = log_sigmoid(cf, cw, None, t)
            DVE.do(lambda e: e.memset(cw, 0.0))
            t = scan(cw, cf, cw, 0.0, ALU.add, ALU.add)
            tc_ = ts(cf, cw, -1.0, None, ALU.mult)
            cpos, cneg = cw, cf

            E = "even_w_in_2"
            for s in range(2):
                b, t = fm(E, (0,), 1544 + s * 256, xtok)
                tu = cp(uf[:, 2 * s:2 * s + 2, :], v3(bank(b), 2), t)
                PS.give(b, tu)
            for s in range(2):
                b, t = fm(E, (0,), s * 256, xtok)
                tq = act(qf[:, 2 * s:2 * s + 2, :], v3(bank(b), 2), ACTF.Copy, t, scale=0.125)
                PS.give(b, tq)
            for s in range(2):
                b, t = fm(E, (0,), 512 + s * 256, xtok)
                tk = cp(kf[:, 2 * s:2 * s + 2, :], v3(bank(b), 2), t)
                PS.give(b, tk)
            for s in range(2):
                b, t = tm(E, (0,), 1024 + s * 256, xtok)
                tv = cp(vt[:, :, s * 256:s * 256 + 256], v3(bank(b), 2), t)
                PS.give(b, tv)

            Sb = [take(256) for _ in range(3)]
            pts = [take(256) for _ in range(2)]
            sfree[0] = [None] * 3
            mx, den, rd = SM[:, 448:464], SM[:, 464:480], SM[:, 480:496]
            units = [(qt, h, 8 * qt + h) for qt in range(2) for h in range(8)]

            def scores(u):
                qt, h, i = u
                n = (qt + 1) * P
                b, waits = PS.take()
                o = (h % 2) * 64
                r = bank(b, 0, n)
                mm(bank(b, n - P, n), ident, cst("causal"), True, False, waits, skip=True)
                mm(r, qf[o:o + 64, h // 2, qt * P:qt * P + P], kf[o:o + 64, h // 2, 0:n], False, False,
                   tq, tk, skip=True)
                mm(r, cpos[:, qt * P:qt * P + P], ident[0:8, h:h + 1].to_broadcast([8, n]), False, False, tc_,
                   skip=True)
                t = mm(r, row_of(h, 8), cneg[:, 0:n], False, True, inc=True, skip=True)
                return b, t

            def soft(u, s):
                qt, h, i = u
                b, t = s
                n = (qt + 1) * P
                sbf = Sb[i % 3][:, 0:n]
                red(mx[:, i:i + 1], bank(b, 0, n), ALU.max, t)
                t = ts(mx[:, i:i + 1], mx[:, i:i + 1], -1.0, None, ALU.mult)
                t = act(sbf, bank(b, 0, n), ACTF.Exp, t, sfree[0][i % 3], bias=mx[:, i:i + 1],
                        accum=den[:, i:i + 1])
                PS.give(b, t)
                return sbf, t

            def value(u, pt, tok):
                qt, h, i = u
                for kt in range(qt + 1):
                    t = mm(bank(4 + qt, h * 64, h * 64 + 64), pt[:, kt * P:(kt + 1) * P],
                           vt[:, kt, h * 64:h * 64 + 64], kt == 0, kt == qt, tok, tv, acc_free[0],
                           inc=(kt == qt))
                return t

            done = attend(units, scores, soft, lambda u: u[0] + 1, value, pts)
            ot = take(1024)
            recip(rd, den, ACT.last())
            for qt in range(2):
                td = tt(v3(ot[:, qt * 512:(qt + 1) * 512], 8), v3(bank(4 + qt), 8),
                        wide(rd[:, 8 * qt:8 * qt + 8], 64), ALU.mult, done)
            t = project_tokens(ot, td, "even_w_out_2", False)

            ys = s5(uf, tu, kf)
            y2 = qf
            gws = [load(a["s5_w_glu_2"][0][256 * x:256 * x + 256, :].rearrange("(k p) n -> p k n", p=P), k=2)
                   for x in range(2)]
            for s in range(2):
                b, waits = PS.take()
                for f in range(2):
                    for k in range(4):
                        ff = 2 * s + f
                        gi, gw, gtok = gws[k // 2]
                        t = mm(bank(b, f * 256, f * 256 + 256), gw[:, k % 2, ff * P:ff * P + P], ys[0][:, k, :],
                               k == 0, k == 3, waits, gtok, ys[1], inc=(f == 1 and k == 3))
                for f in range(2):
                    ff = 2 * s + f
                    tg = act(y2[:, ff, :], bank(b, f * 256, f * 256 + 256), ACTF.Sigmoid, t,
                             bias=par("bglu", ff, 1))
                PS.give(b, tg)
            for x in range(2):
                W.give(gws[x][0], t)
            ty = tt(y2, y2, ys[0], ALU.mult, tg)
            ty = split(gh[:, 4:8, :], gl[:, 4:8, :], y2, ty)
            for s in range(4, 8):
                t = down("even_w_out_2", (0,), s * P, gh[:, s, :], gl[:, s, :], False, s == 7, ty)
            return t

        def reduce_angle(x, n, *waits, q=None):
            c1 = 6.28125
            c2 = 0.0019350051879882812
            c3 = TWO_PI - c1 - c2
            ts(n, x, 1.0 / TWO_PI, ROUND, ALU.mult, ALU.add, *waits)
            ts(n, n, ROUND, None, ALU.subtract)
            stt(x, n, -c1, x, ALU.mult, ALU.add)
            stt(x, n, -c2, x, ALU.mult, ALU.add)
            stt(x, n, -c3, x, ALU.mult, ALU.add)
            return ts(x, x, 3.1415925, -3.1415925, ALU.min, ALU.max)

        def s5(uf, tu, YS):
            sm = take(16 * 20)
            c = [sm[:, i * 16:(i + 1) * 16] for i in range(20)]
            dt, mag, th, nn, cs, sn, lre, lim, den, zre, zim, t0, t1 = c[:13]
            are, aim = par("are"), par("aim")
            half = cst("half", 0, 1)
            t = act(dt, par("ldt"), ACTF.Exp)
            tt(mag, are, dt, ALU.mult, t)
            t = act(mag, mag, ACTF.Exp, DVE.last())
            tt(th, aim, dt, ALU.mult)
            t2 = reduce_angle(th, nn)
            act(sn, th, ACTF.Sin, t2)
            act(cs, th, ACTF.Abs)
            t = act(cs, cs, ACTF.Sin, scale=-1.0, bias=half)
            tt(lre, mag, cs, ALU.mult, t)
            tt(lim, mag, sn, ALU.mult)
            ts(lre, lre, -1.0, None, ALU.add)
            tt(den, are, are, ALU.mult)
            tt(t0, aim, aim, ALU.mult)
            tt(den, den, t0, ALU.add)
            recip(den, den)
            tt(zre, lre, are, ALU.mult)
            tt(t0, lim, aim, ALU.mult)
            tt(zre, zre, t0, ALU.add)
            tt(zre, zre, den, ALU.mult)
            tt(zim, lim, are, ALU.mult)
            tt(t0, lre, aim, ALU.mult)
            tt(zim, zim, t0, ALU.subtract)
            tt(zim, zim, den, ALU.mult)
            bre, bim = v3(par("bre"), 16), v3(par("bim"), 16)
            bb = [v3(take(256), 16) for _ in range(2)]
            w0 = v3(take(256), 16)
            tt(bb[0], bre, wide(zre, 16), ALU.mult)
            tt(w0, bim, wide(zim, 16), ALU.mult)
            tt(bb[0], bb[0], w0, ALU.subtract)
            tt(bb[1], bim, wide(zre, 16), ALU.mult)
            tt(w0, bre, wide(zim, 16), ALU.mult)
            tt(bb[1], bb[1], w0, ALU.add)
            blk = take(1024)
            BT = [v3(take(512), 4) for _ in range(2)]
            CTt = [v3(take(512), 4) for _ in range(2)]
            DVE.do(lambda e: e.memset(blk, 0.0))
            for r in range(2):
                bv = blk[:, r * 512:(r + 1) * 512].rearrange("p (j e c) -> p j e c", j=16, e=2)
                for e_ in range(2):
                    t = cp(bv[e_ * 64:e_ * 64 + 64, :, e_, :], bb[r][e_ * 64:e_ * 64 + 64, :, :])
            for r in range(2):
                b, waits = PS.take()
                for i in range(4):
                    t2 = tr(bank(b, i * P, i * P + P), blk[:, r * 512 + i * P:r * 512 + i * P + P], P,
                            waits, t, inc=(i == 3))
                t3 = cp(BT[r], v3(bank(b), 4), t2, q=ACT)
                PS.give(b, t3)
            tbt = t3
            cblk = v4(blk, 2, 4)
            ev = cst("half", 1, 1)
            for r, nm in enumerate(("cre", "cim")):
                cv = v3(par(nm), 4)
                od = cst("firsts", 0, 1)
                ts(cblk[:, r, :, 0:64], cv, ev, 1.0 if r == 0 else -1.0, ALU.mult, ALU.mult, t2)
                t = ts(cblk[:, r, :, 64:128], cv, od, 1.0 if r == 0 else -1.0, ALU.mult, ALU.mult)
            for r in range(2):
                b, waits = PS.take()
                for i in range(4):
                    t2 = tr(bank(b, i * P, i * P + P), cblk[:, r, i, :], P, waits, t, inc=(i == 3))
                t3 = cp(CTt[r], v3(bank(b), 4), t2, q=ACT)
                PS.give(b, t3)
            tct = t3

            An, Nn, Br, Bi = (v3(take(1024), 4) for _ in range(4))
            C, Sn, Gr, Gi = (v3(x, 4) for x in (T1[:, 0:1024], T1[:, 1024:2048], T2[:, 0:1024], T2[:, 1024:2048]))
            tvec = cst("tt")
            t_prev = None
            for i in range(4):
                for jj in range(4):
                    ts(An[:, jj, :], tvec, th[:, 4 * i + jj:4 * i + jj + 1], None, ALU.mult)
                t = reduce_angle(An, Nn)
                act(Sn, An, ACTF.Sin, t)
                act(C, An, ACTF.Abs)
                tsc = act(C, C, ACTF.Sin, scale=-1.0, bias=half)
                b, waits = PS.take(4)
                for jj in range(4):
                    for r in range(2):
                        t = mm(bank(b + jj, r * 256, r * 256 + 256), BT[r][32 * jj:32 * jj + 32, i, :],
                               uf[32 * jj:32 * jj + 32, i, :], True, True, waits, tbt, tu,
                               inc=(jj == 3 and r == 1))
                bu = PSA[:, :].rearrange("p (j r n) -> p j r n", j=4, r=2)
                cp(Br, bu[:, :, 0, :], t, q=ACT)
                t = cp(Bi, bu[:, :, 1, :], t, q=ACT)
                PS.give(b, t, k=4)
                tt(Gr, Br, C, ALU.mult, t, tsc)
                tt(Nn, Bi, Sn, ALU.mult)
                tt(Gr, Gr, Nn, ALU.add)
                tt(Gi, Bi, C, ALU.mult)
                tt(Nn, Br, Sn, ALU.mult)
                tt(Gi, Gi, Nn, ALU.subtract)
                for jj in range(4):
                    m = mag[:, 4 * i + jj:4 * i + jj + 1].to_broadcast([P, 256])
                    scan(Br[:, jj, :], m, Gr[:, jj, :], 0.0, ALU.mult, ALU.add)
                    scan(Bi[:, jj, :], m, Gi[:, jj, :], 0.0, ALU.mult, ALU.add)
                tt(Gr, Br, C, ALU.mult, t_prev)
                tt(Nn, Bi, Sn, ALU.mult)
                tt(Gr, Gr, Nn, ALU.subtract)
                tt(Gi, Bi, C, ALU.mult)
                tt(Nn, Br, Sn, ALU.mult)
                t = tt(Gi, Gi, Nn, ALU.add)
                b, waits = PS.take()
                for jj in range(4):
                    o = bank(b, 0, 256, p=32, p0=32 * jj)
                    mm(o, CTt[0][:, i, 32 * jj:32 * jj + 32], Gr[:, jj, :], True, False, waits, t, tct)
                    t_prev = mm(o, CTt[1][:, i, 32 * jj:32 * jj + 32], Gi[:, jj, :], False, True, inc=(jj == 3))
                t = stt(YS[:, i, :], uf[:, i, :], par("s5d", i, 1), bank(b, 0, 256), ALU.mult, ALU.add, t_prev)
                PS.give(b, t)
            tg = act(YS, YS, ACTF.Gelu_apprx_tanh, t)
            return YS, tg

        def mlstm(xtok):
            wi = a["odd_w_in_2"][0]
            src = xt
            qk = [v3(take(2048), 8) for _ in range(2)]
            vt = v3(take(2048), 2)
            og = v3(take(2048), 8)
            pad = [take(260) for _ in range(4)]
            acc = [take(256) for _ in range(2)]
            pfree = [None] * 4
            afree = [None] * 2
            gf = [take(256)[0:8, :] for _ in range(4)]
            lf, g, mr, wk_ = gf
            gi, gw, gtok = load(wi[:, 4096:4112].rearrange("(k p) n -> p k n", p=P), cols=128, k=8)
            b, waits = PS.take()
            for r in range(2):
                for k in range(8):
                    t = mm(bank(b, r * 256, r * 256 + 256, p=8), gw[:, k, 8 * r:8 * r + 8], src[:, k, :],
                           k == 0, k == 7, waits, gtok, xtok[k], inc=(r == 1 and k == 7))
            W.give(gi, t)
            ts(g, bank(b, 0, 256, p=8), par("fb", 1, 1, p=8), None, ALU.add, None, t)
            t = ts(lf, bank(b, 256, 512, p=8), par("fb", 2, 1, p=8), None, ALU.add)
            PS.give(b, t)
            log_sigmoid(lf, wk_, None, t)
            DVE.do(lambda e: e.memset(wk_, 0.0))
            scan(wk_, lf, wk_, 0.0, ALU.add, ALU.add)
            Fc = wk_
            tg_ = tt(g, g, Fc, ALU.subtract)
            scan(mr, g, g, 0.0, ALU.max, ALU.max)
            t = tt(lf, Fc, mr, ALU.add)
            b, waits = PS.take()
            for m in range(2):
                tr(bank(b, m * 16, m * 16 + 8), mr[:, m * P:(m + 1) * P], 8, waits, t)
                t2 = tr(bank(b, m * 16 + 8, m * 16 + 16), lf[:, m * P:(m + 1) * P], 8, inc=(m == 1))
            nm = SM[:, 500:532]
            t = ts(nm, bank(b, 0, 32), -1.0, None, ALU.mult, None, t2)
            PS.give(b, t)
            em = SM[:, 532:564]
            t_em = act(em, nm, ACTF.Exp, t)
            t_nm = t

            zt = [DVE.do(lambda e, x=x: e.memset(x[:, 0:3], 0.0)) for x in pad]
            O = "odd_w_in_2"
            for s in range(8):
                b, t = fm(O, (0,), s * 256, xtok)
                for f in range(2):
                    c = 2 * s + f
                    pb, ab = c % 4, c % 2
                    tp = cp(pad[pb][:, 3:259], bank(b, f * 256, f * 256 + 256), t, zt, pfree[pb], q=ACT)
                    ts(acc[ab], pad[pb][:, 0:256], par("convw", c, 1), par("convb", c, 1), ALU.mult, ALU.add,
                       tp, afree[ab])
                    for w in range(1, 4):
                        td = stt(acc[ab], pad[pb][:, w:w + 256], par("convw", w * 16 + c, 1), acc[ab],
                                 ALU.mult, ALU.add)
                    pfree[pb] = td
                    tqk = act(qk[c // 8][:, c % 8, :], acc[ab], ACTF.Silu, td)
                    afree[ab] = tqk
                PS.give(b, tp)
            for s in range(4):
                b, t = tm(O, (0,), 2048 + s * 256, xtok)
                tv = cp(vt[:, :, s * 256:s * 256 + 256], v3(bank(b), 2), t)
                PS.give(b, tv)
            for s in range(4):
                b, t = fm(O, (0,), 3072 + s * 256, xtok)
                to = act(og[:, 2 * s:2 * s + 2, :], v3(bank(b), 2), ACTF.Sigmoid, t)
                PS.give(b, to)

            Sb = [take(256) for _ in range(3)]
            Db = [take(256) for _ in range(2)]
            pts = [take(256) for _ in range(2)]
            sfree[0] = [None] * 3
            den = SM[:, 564:580]
            rd = SM[:, 580:596]
            units = [(qt, h, 2 * h + qt) for h in range(8) for qt in range(2)]
            hfree = [None] * 2
            hout = og
            st = {}
            INV = 128.0 ** -0.5

            def scores(u):
                qt, h, i = u
                n = (qt + 1) * P
                b, waits = PS.take()
                mm(bank(b, 0, n), qk[0][:, h, qt * P:qt * P + P], qk[1][:, h, 0:n], True, True, waits, tqk)
                mm(bank(b, 256 + n - P, 256 + n), ident, cst("causal"), True, False, skip=True)
                t = mm(bank(b, 256, 256 + n), row_of(h, 8), g[:, 0:n], False, True, tg_, inc=True, skip=True)
                return b, t

            def soft(u, s):
                qt, h, i = u
                b, t = s
                n = (qt + 1) * P
                sbf, dbf = Sb[i % 3][:, 0:n], Db[i % 2][:, 0:n]
                t = act(dbf, bank(b, 256, 256 + n), ACTF.Exp, t, st.get(("d", i % 2)), t_nm,
                        bias=nm[:, qt * 16 + h:qt * 16 + h + 1])
                t = DVE.do(lambda e: e.scalar_tensor_tensor(out=sbf, in0=bank(b, 0, n), scalar=INV, in1=dbf,
                                                            op0=ALU.mult, op1=ALU.mult,
                                                            accum_out=den[:, i:i + 1]), t, sfree[0][i % 3])
                PS.give(b, t)
                st[("d", i % 2)] = t
                stt(rd[:, i:i + 1], den[:, i:i + 1], -1.0, den[:, i:i + 1], ALU.mult, ALU.max)
                tt(rd[:, i:i + 1], rd[:, i:i + 1], em[:, qt * 16 + 8 + h:qt * 16 + 9 + h], ALU.max, t_em)
                recip(rd[:, i:i + 1], rd[:, i:i + 1])
                t = ts(sbf, sbf, rd[:, i:i + 1], None, ALU.mult)
                return sbf, t

            def value(u, pt, tok):
                qt, h, i = u
                bb = 4 + (h // 2) % 2
                lo = (h % 2) * 256 + qt * P
                for kt in range(qt + 1):
                    t = mm(bank(bb, lo, lo + P), vt[:, kt, h * P:(h + 1) * P], pt[:, kt * P:(kt + 1) * P],
                           kt == 0, kt == qt, tok, tv, acc_free[0], hfree[(h // 2) % 2], inc=(kt == qt))
                if h % 2 and qt:
                    hfree[(h // 2) % 2] = tt(hout[:, h - 1:h + 1, :], og[:, h - 1:h + 1, :], v3(bank(bb), 2),
                                             ALU.mult, t, to)
                return t

            attend(units, scores, soft, lambda u: u[0] + 1, value, pts)
            acc_free[0] = acc_free[0] + [DVE.last(), ACT.last()]
            tsp = []
            for x in range(0, 8, 4):
                tsp.append(split(gh[:, x:x + 4, :], gl[:, x:x + 4, :], hout[:, x:x + 4, :], DVE.last()))
            for s in range(8):
                t = down("odd_w_out_2", (0,), s * P, gh[:, s, :], gl[:, s, :], s == 0, s == 7, tsp[s // 4])
            return t

        def moe(l, xtok):
            lg = v3(SM[:, 600:640], 2)
            b, waits = PS.take()
            wr = v3(par("wr", l * 160, 160), 8)
            for m in range(2):
                for k in range(8):
                    t = mm(bank(b, m * 20, m * 20 + 20), xt[:, k, m * P:(m + 1) * P], wr[:, k, :], k == 0, k == 7,
                           waits, xtok[k], inc=(m == 1 and k == 7))
            t = tt(lg, v3(bank(b, 0, 40), 2), rep(par("rb", l * 20, 20), 2), ALU.add, t)
            PS.give(b, t)
            at = [640]

            def s_(n):
                at[0] += n
                return SM[:, at[0] - n:at[0]]

            gl = lg[:, :, 0:4]
            el = lg[:, :, 4:20].rearrange("p m (g e) -> p m g e", g=4)
            m1, g4, ex, sm_, oh, gv = s_(2), v3(s_(8), 2), v3(s_(8), 2), s_(2), v3(s_(8), 2), s_(2)
            wt = cst("firsts", 0, 4)

            def onehot(o, x, mxv):
                tt(o, x, wide(mxv, 4), ALU.is_equal)
                tt(o, o, rep(order, 2), ALU.mult)
                red(m1, o, ALU.max)
                tt(o, o, wide(m1, 4), ALU.is_equal)

            order = s_(4)
            for x in range(4):
                DVE.do(lambda e, x=x: e.memset(order[:, x:x + 1], float(4 - x)))
            mg = s_(2)
            red(mg, gl, ALU.max)
            tt(g4, gl, wide(mg, 4), ALU.subtract)
            t = act(ex, g4, ACTF.Exp, DVE.last())
            red(sm_, ex, ALU.add, t)
            recip(gv, sm_)
            onehot(oh, gl, mg)
            sel = v4(s_(32), 2, 4)
            es = v3(s_(8), 2)
            for m in range(2):
                tt(sel[:, m], el[:, m], wide(oh[:, m, :], 4), ALU.mult)
                red(es[:, m, :], sel[:, m].rearrange("p g e -> p e g"), ALU.add)
            e1, o1, o2, l2, e2, p2, w1, w2 = s_(2), v3(s_(8), 2), v3(s_(8), 2), v3(s_(8), 2), s_(2), s_(2), s_(2), s_(2)
            red(e1, es, ALU.max)
            onehot(o1, es, e1)
            stt(l2, o1, -3.0e38, es, ALU.mult, ALU.add)
            red(e2, l2, ALU.max)
            onehot(o2, l2, e2)
            tt(p2, e2, e1, ALU.subtract)
            t = act(p2, p2, ACTF.Exp, DVE.last())
            ts(w1, p2, 1.0, None, ALU.add, None, t)
            recip(w1, w1)
            tt(w1, w1, gv, ALU.mult)
            tt(w2, w1, p2, ALU.mult)
            tt(o1, o1, wide(w1, 4), ALU.mult)
            tt(o2, o2, wide(w2, 4), ALU.mult)
            tt(o1, o1, o2, ALU.add)
            comb = v4(s_(32), 2, 4)
            for m in range(2):
                for g_ in range(4):
                    t = ts(comb[:, m, g_, :], o1[:, m, :], oh[:, m, g_:g_ + 1], None, ALU.mult)
            b, waits = PS.take()
            for m in range(2):
                t2 = tr(bank(b, m * P, m * P + P, p=16), comb[:, m].rearrange("p g e -> p (g e)"), P, waits, t,
                        inc=(m == 1))
            cT = take(256)[0:16, :]
            t = cp(cT, bank(b, 0, 256, p=16), t2, q=ACT)
            PS.give(b, t)
            spread = v3(take(4096), 16)
            for e_ in range(0, 16, 2):
                b, waits = PS.take()
                for x in range(2):
                    t2 = mm(bank(b, x * 256, x * 256 + 256), row_of(e_ + x, 16), cT, True, True, waits, t,
                            inc=(x == 1))
                tb = cp(spread[:, e_:e_ + 2, :], v3(bank(b), 2), t2, q=ACT)
                PS.give(b, tb)
            return gated([(("moe_w_gate_2", (l, e), 0), ("moe_w_up_2", (l, e), 0),
                           ("moe_w_down_2", (l, e), 0), ("moe_w_down_2", (l, e), P))
                          for e in range(16)], xtok, spread, tb)

        mixers = [hybrid, dilated, fox, mlstm]
        for n in range(8):
            fence()
            l = n // 2 % 2
            if n < 4:
                htok = pre(n, xtok)
                yt = ffn(l, htok) if n % 2 else mixers[l](htok)
                xtok = post(n, yt)
            else:
                yt = moe(l, xtok) if n % 2 else mixers[2 + l](xtok)
                xtok = layer_norm(n - 4, yt)

        fence()
        ov = take(2048)
        for m in range(2):
            for j in range(0, 8, 4):
                b, waits = PS.take()
                for jj in range(4):
                    t = tr(bank(b, jj * P, jj * P + P), xt[:, j + jj, m * P:(m + 1) * P], P, waits,
                           xtok[j + jj], inc=(jj == 3))
                t = cp(ov[:, m * 1024 + j * P:m * 1024 + (j + 4) * P], bank(b), t, q=(ACT if m else None))
                PS.give(b, t)
            SP.do(lambda e, m=m: e.dma_start(out[m * P:(m + 1) * P, :], ov[:, m * 1024:(m + 1) * 1024])
                  .then_inc(s_out, 16), t, inc=False)

        block = ctx.enter_context(nc.Block())

        @block.sync
        def _(eng):
            SP.emit(eng)
            eng.wait_ge(s_out, 32)

        @block.tensor
        def _(eng):
            PE.emit(eng)

        @block.scalar
        def _(eng):
            ACT.emit(eng)

        @block.vector
        def _(eng):
            DVE.emit(eng)

        @block.gpsimd
        def _(eng):
            POOL.emit(eng)


def shape_constants():
    c = np.zeros((P, CN), np.float32)
    i = np.arange(P)

    def put(name, v):
        at, n = CO[name]
        c[:, at:at + n] = v

    put("ident", np.eye(P))
    put("onesd", 1.0 / D)
    put("causal", np.where(i[None, :] <= i[:, None], 0.0, NEG))
    hm = []
    for h in (1, 2, 4, 8, 16, 32, 64):
        s, t = i[:, None], i[None, :]
        hm.append((s // (2 * h) == t // (2 * h)) & (s % (2 * h) < h) & (t % (2 * h) >= h))
    put("hm", np.concatenate(hm, 1))
    hs = np.zeros((P, 4, 4))
    for h in range(4):
        hs[:, h, h] = 1.0 / 128.0
    put("hsel", hs.reshape(P, 16))
    put("tt", np.arange(256)[None, :])
    put("half", np.stack([np.full(P, math.pi / 2), 1.0 - (i // 16) % 2], 1))
    put("firsts", np.stack([(i // 16) % 2] * 4, 1))

    x = np.zeros((P, AN), np.float32)
    inv = np.stack([1.0 / np.minimum(np.arange(256) + 1, w) for w in (2, 4, 8, 16)]).reshape(-1)
    x[:, 0:1024] = inv[None, :]
    d = np.arange(384) - 127
    dd = np.maximum(d, 0).astype(np.int64)
    df = np.maximum(dd, 1).astype(np.float32)
    large = 16 + (np.log(df / np.float32(16)).astype(np.float32) / np.float32(math.log(2048 / 16))
                  * np.float32(16)).astype(np.int32)
    bucket = np.where(dd < 16, dd, np.minimum(large, 31))
    x[0:32, 1024:1408] = (bucket[None, :] == np.arange(32)[:, None])
    ok = np.stack([(d >= 0) & (d <= 128), (d >= 0) & (d % 4 == 0), (d >= 0) & (d % 16 == 0)])
    x[0:24, 1408:1792] = np.where(np.repeat(ok, 8, 0), 0.0, NEG)
    return c, x


_BIG = ["ada_w", "ffn_w_in", "ffn_w_out", "hyb_w_in", "hyb_w_out", "pool_w", "att_w_qkv", "att_w_out",
        "even_w_in_2", "s5_w_glu_2", "even_w_out_2", "odd_w_in_2", "odd_w_out_2",
        "moe_w_gate_2", "moe_w_up_2", "moe_w_down_2"]


def kernel(**inputs):
    import concourse.bacc as bacc
    from concourse.bass_utils import run_bass_kernel_spmd

    f = {k: np.asarray(v) for k, v in inputs.items()}

    def cols(v):
        return np.asarray(v).reshape(-1, P).T

    def on8(v):
        r = np.zeros((P, 1), np.float32)
        r[0:8, 0] = v.reshape(-1)
        return r

    pr = np.zeros((P, PN), np.float32)

    def put(name, v):
        at, n = PO[name]
        pr[:, at:at + n] = v

    put("c", cols(f["c"]))
    put("npre", cols(f["norm_pre"]))
    put("npost", cols(f["norm_post"]))
    put("adab", cols(f["ada_b"]))
    put("pscale", cols(f["pool_scale"]))
    put("lbl", cols(f["hgrn_lb_logits"]))
    put("onorm", cols(f["hgrn_out_norm"]))
    put("lng", cols(f["ln_g_2"]))
    put("lnb", cols(f["ln_b_2"]))
    put("are", cols(f["s5_a_re_2"]))
    put("aim", cols(f["s5_a_im_2"]))
    put("ldt", cols(np.repeat(f["s5_log_dt_2"].reshape(-1), 64)))
    put("s5d", cols(f["s5_d_2"]))
    put("bglu", cols(f["s5_b_glu_2"]))
    put("convw", cols(f["mlstm_conv_w_2"]))
    put("convb", cols(f["mlstm_conv_b_2"]))
    rb = np.concatenate([f["moe_b_group_2"], f["moe_b_expert_2"].reshape(2, 16)], 1).reshape(1, 40)
    put("rb", np.broadcast_to(rb, (P, 40)))
    put("fb", np.concatenate([on8(f["fox_f_bias_2"]), on8(f["mlstm_i_bias_2"]), on8(f["mlstm_f_bias_2"])], 1))
    for n, s in (("bre", "s5_b_re_2"), ("bim", "s5_b_im_2")):
        put(n, f[s].reshape(16, P, 16).transpose(1, 0, 2).reshape(P, 256))
    for n, s in (("cre", "s5_c_re_2"), ("cim", "s5_c_im_2")):
        put(n, f[s].reshape(4, P, 64).transpose(1, 0, 2).reshape(P, 256))
    wr = np.concatenate([f["moe_w_group_2"].reshape(2, 8, P, 4),
                         f["moe_w_expert_2"].reshape(2, 4, 8, P, 4).transpose(0, 2, 3, 1, 4).reshape(2, 8, P, 16)], 3)
    put("wr", wr.transpose(2, 0, 1, 3).reshape(P, 320))
    ct, ax = shape_constants()
    at = AO["relb"][0]
    ax[0:32, at:at + 24] = f["rel_bias"]

    nc = bacc.Bacc("TRN2", target_bir_lowering=False, num_devices=1)
    arrays = {"params": pr, "consts": ct, "aux": ax, "x": np.ascontiguousarray(f["x"].reshape(S, D))}
    for n in _BIG:
        arrays[n] = np.ascontiguousarray(f[n])
    aps = {n: nc.dram_tensor(n, v.shape, mybir.dt.from_np(v.dtype), kind="ExternalInput").ap()
           for n, v in arrays.items()}
    out = nc.dram_tensor("out_x", (S, D), F32, kind="ExternalOutput").ap()
    build(nc, aps, out)
    r = run_bass_kernel_spmd(nc, [arrays], core_ids=[0])
    return r.results[0]["out_x"].reshape(1, S, D)
```

```python
import math
from contextlib import ExitStack

import numpy as np
import concourse.bass as bass
from concourse import mybir

ALU = mybir.AluOpType
ACTF = mybir.ActivationFunctionType
F32 = mybir.dt.float32
F32R = mybir.dt.float32r
I32 = mybir.dt.int32
AX = mybir.AxisListType

P = 128
S = 256
D = 1024
NEG = -1.0e30
NF = 11
NRAW = 4
NSPLIT = 5
ARENA = 16128
RSQRT_SEED = float(0x5F3759DF)
DN_ALPHA = 4.0 ** 0.25
TWO_PI = 2.0 * math.pi
BG = 1
ROUND = 1.5 * 2.0 ** 23

PARAM_COLS = [
    ("c", 8), ("npre", 32), ("npost", 32), ("adab", 96), ("pscale", 4), ("lbl", 4), ("onorm", 1),
    ("lng", 32), ("lnb", 32), ("are", 16), ("aim", 16), ("ldt", 16), ("s5d", 4), ("bglu", 4),
    ("convw", 64), ("convb", 16), ("rb", 40), ("fb", 3), ("bre", 256), ("bim", 256),
    ("cre", 256), ("cim", 256), ("wr", 320),
]
CONST_COLS = [("ident", 128), ("onesd", 128), ("causal", 128), ("hm", 896), ("hsel", 16), ("tt", 256),
              ("half", 2), ("firsts", 4)]
AUX_COLS = [("invc", 1024), ("onehot", 384), ("maskv", 384), ("relb", 24)]


def offsets(cols):
    out, at = {}, 0
    for name, n in cols:
        out[name] = (at, n)
        at += n
    return out, at


PO, PN = offsets(PARAM_COLS)
CO, CN = offsets(CONST_COLS)
AO, AN = offsets(AUX_COLS)


class Queue:

    def __init__(self, name, sem, link):
        self.name, self.sem, self.link = name, sem, link
        self.ops, self.n, self.seen, self.extra, self.open = [], 0, {}, [], False

    def last(self):
        assert not self.open
        return (self.name, self.sem, self.n)

    def do(self, fn, *waits, inc=True):
        todo = list(self.extra)
        self.extra = []
        if self.link and self.n:
            todo.append((self.name, self.sem, self.n))
        stack = list(waits)
        while stack:
            w = stack.pop()
            if w is None:
                continue
            if isinstance(w, list):
                stack.extend(w)
            else:
                todo.append(w)
        need = {}
        for name, sem, val in todo:
            if val > self.seen.get(name, 0):
                self.seen[name] = val
                need[name] = (sem, val)
        self.ops.append((list(need.values()), fn, inc))
        self.open = not inc
        if inc:
            self.n += 1
            return (self.name, self.sem, self.n)
        return None

    def emit(self, eng):
        for waits, fn, inc in self.ops:
            for sem, val in waits:
                eng.wait_ge(sem, val)
            ins = fn(eng)
            if inc:
                ins.then_inc(self.sem, 1)


def weight_plan():
    out = []

    def k(name, n, c):
        out.extend([(name, "k", n, c, 0), (name, "k", n, c, 1)])

    def d(name, n, r):
        out.append((name, "d", n, r, 0))

    def cols(name, *ranges):
        for at, count in ranges:
            for i in range(count):
                k(name, (0,), at + i * 256)

    def pairs(gate, up, down):
        n = len(gate)
        for i in range(n + 1):
            if i < n:
                k(*gate[i])
                k(*up[i])
            if i:
                d(*down[i - 1])
                d(down[i - 1][0], down[i - 1][1], down[i - 1][2] + P)

    def rows(name, count):
        for i in range(count):
            d(name, (0,), i * P)

    for l in range(2):
        if l == 0:
            cols("hyb_w_in", (0, 10))
            rows("hyb_w_out", 8)
        else:
            cols("att_w_qkv", (0, 18))
            rows("att_w_out", 4)
        pairs([("ffn_w_in", (l,), i * 256) for i in range(NF)],
              [("ffn_w_in", (l,), 2816 + i * 256) for i in range(NF)],
              [("ffn_w_out", (l,), i * 256) for i in range(NF)])
    for l in range(2):
        if l == 0:
            cols("even_w_in_2", (1544, 2), (0, 2), (512, 2), (1024, 2))
            rows("even_w_out_2", 8)
        else:
            cols("odd_w_in_2", (0, 16))
            rows("odd_w_out_2", 8)
        pairs([("moe_w_gate_2", (l, e), 0) for e in range(16)], [("moe_w_up_2", (l, e), 0) for e in range(16)],
              [("moe_w_down_2", (l, e), 0) for e in range(16)])
    return out


AHEAD = 2


class Slots:

    def __init__(self, n, base=0):
        self.n, self.base, self.i = n, base, 0
        self.free = [[] for _ in range(n)]

    def take(self, k=1):
        i = self.i
        if i % k:
            i += k - i % k
        i %= self.n
        for _ in range(self.n):
            if all(self.free[j] is not None for j in range(i, i + k)):
                break
            i = (i + k) % self.n
        self.i = (i + k) % self.n
        waits = []
        for j in range(i, i + k):
            assert self.free[j] is not None, "taken and not given back"
            waits += self.free[j]
            self.free[j] = None
        return self.base + i, waits

    def give(self, i, *toks, k=1):
        for j in range(i - self.base, i - self.base + k):
            assert self.free[j] is None
            self.free[j] = [t for t in toks if t is not None]


def build(nc, a, out):
    ctx = ExitStack()
    with ctx:
        def sb(name, cols, dt=F32):
            return ctx.enter_context(nc.sbuf_tensor(name, [P, cols], dt))

        def sem(name):
            return ctx.enter_context(nc.semaphore(name))

        PSA = ctx.enter_context(nc.psum_tensor("PSA", [P, 2048], F32))
        PSB = ctx.enter_context(nc.psum_tensor("PSB", [P, 2048], F32))
        XT = sb("XT", 2048)
        XH = sb("XH", 2048, F32R)
        XL = sb("XL", 2048, F32R)
        GH = sb("GH", 2048, F32R)
        GL = sb("GL", 2048, F32R)
        ACC = sb("ACC", 1024)
        AD = sb("AD", 2048)
        T1 = sb("T1", 2048)
        T2 = sb("T2", 2048)
        RS = sb("RS", 1024)
        MC = sb("MC", 168)
        SM = sb("SM", 800)
        CT = sb("CT", CN)
        PR = sb("PR", PN)
        WR = sb("WR", NRAW * 1024)
        WH = sb("WH", NSPLIT * 1024, F32R)
        WL = sb("WL", NSPLIT * 1024, F32R)
        AR = sb("AR", ARENA)

        PE = Queue("pe", sem("s_pe"), False)
        ACT = Queue("act", sem("s_act"), True)
        DVE = Queue("dve", sem("s_dve"), True)
        POOL = Queue("pool", sem("s_pool"), True)
        SP = Queue("sp", sem("s_sp"), False)
        wsem = [sem(f"s_w{i}") for i in range(NRAW)]
        wcnt = [0] * NRAW
        asem = [sem(f"s_a{i}") for i in range(8)]
        acnt = [0] * 8
        s_in = sem("s_in")
        s_x = sem("s_x")
        s_aux = sem("s_aux")
        s_bias = sem("s_bias")
        s_tp = sem("s_tp")
        s_out = sem("s_out")

        scratch = nc.dram_tensor("bias_rows", [24, 384], F32, kind="Internal")

        def par(name, a0=0, n=None, p=P):
            at, w = PO[name]
            n = w - a0 if n is None else n
            return PR[0:p, at + a0:at + a0 + n]

        def cst(name, a0=0, n=None, p=P):
            at, w = CO[name]
            n = w - a0 if n is None else n
            return CT[0:p, at + a0:at + a0 + n]

        ident = cst("ident")
        onesd = cst("onesd")

        W = Slots(NRAW)
        WS = Slots(NSPLIT)
        PS = Slots(4)
        PT = Slots(2, base=6)

        def bank(b, lo=0, hi=512, p=P, p0=0):
            t = PSA if b < 4 else PSB
            o = (b % 4) * 512
            return t[p0:p0 + p, o + lo:o + hi]

        def wslot(i):
            return WR[:, i * 1024:(i + 1) * 1024]

        arena = [0]

        top = [ARENA]

        def take(n):
            at = arena[0]
            arena[0] += n
            assert arena[0] <= top[0], (arena[0], top[0])
            return AR[:, at:at + n]

        def keep(n):
            top[0] -= n
            assert arena[0] <= top[0]
            return AR[:, top[0]:top[0] + n]

        def fence():
            toks = [q.last() for q in (PE, ACT, DVE, POOL) if q.n]
            for q in (PE, ACT, DVE, POOL):
                q.extra = [t for t in toks if t[0] != q.name]
            arena[0] = 0

        def mm(o, l, r, start, stop, *waits, inc=False, skip=False):
            return PE.do(lambda e: e.matmul(o, l, r, start=start, stop=stop, skip_group_check=skip),
                         *waits, inc=inc)

        def tr(o, i, n, *waits, inc=False):
            return PE.do(lambda e: e.transpose(o, i, ident[0:n, 0:n]), *waits, inc=inc)

        def act(o, i, f, *waits, bias=0.0, scale=1.0, accum=None):
            if accum is None:
                return ACT.do(lambda e: e.activation(o, i, f, bias=bias, scale=scale), *waits)
            return ACT.do(lambda e: e.activation(o, i, f, bias=bias, scale=scale, accum_out=accum), *waits)

        def ts(o, i, s1, s2, op0, op1=None, *waits, q=None):
            q = q or DVE
            if op1 is None:
                return q.do(lambda e: e.tensor_scalar(o, i, s1, None, op0), *waits)
            return q.do(lambda e: e.tensor_scalar(o, i, s1, s2, op0, op1), *waits)

        def stt(o, i, s, j, op0, op1, *waits):
            return DVE.do(lambda e: e.scalar_tensor_tensor(out=o, in0=i, scalar=s, in1=j, op0=op0, op1=op1), *waits)

        def tt(o, i, j, op, *waits, q=None):
            q = q or DVE
            return q.do(lambda e: e.tensor_tensor(o, i, j, op), *waits)

        def cp(o, i, *waits, q=None):
            if q is ACT:
                return ACT.do(lambda e: e.copy(o, i), *waits)
            return (q or DVE).do(lambda e: e.tensor_copy(o, i), *waits)

        def scan(o, x, y, init, op0, op1, *waits):
            return DVE.do(lambda e: e.tensor_tensor_scan(o, x, y, init, op0, op1), *waits)

        def red(o, i, op, *waits):
            return DVE.do(lambda e: e.tensor_reduce(o, i, AX.X, op), *waits)

        def recip(o, i, *waits):
            return DVE.do(lambda e: e.reciprocal(o, i), *waits)

        def v3(ap, n):
            return ap.rearrange("p (a b) -> p a b", a=n)

        def v4(ap, n, m):
            return ap.rearrange("p (a b c) -> p a b c", a=n, b=m)

        def rep(ap, n):
            return ap.unsqueeze(1).to_broadcast([ap.shape[0], n, ap.shape[1]])

        def wide(ap, n):
            return ap.unsqueeze(2).to_broadcast([ap.shape[0], ap.shape[1], n])

        def row_of(e, k):
            return ident[0:k, e:e + 1].to_broadcast([k, P])

        def load(src, cols=1024, k=4, p=P):
            i, waits = W.take()
            dst = v3(wslot(i)[0:p, 0:cols], k) if k > 1 else wslot(i)[0:p, 0:cols]
            SP.do(lambda e: e.dma_start(dst, src).then_inc(wsem[i], 16), waits, inc=False)
            wcnt[i] += 16
            return i, dst, (f"w{i}", wsem[i], wcnt[i])

        def source(key):
            name, kind, n, at, half = key
            m = a[name] if n is None else a[name][n[0]] if len(n) == 1 else a[name][n[0], n[1]]
            if kind == "k":
                return m[half * 512:half * 512 + 512, at:at + 256].rearrange("(k p) n -> p k n", p=P), 4
            return m[at:at + P, 0:1024], 1

        plan = weight_plan()
        raws, splits, popped = [], [], [0]

        def want_raw():
            if len(raws) < len(plan):
                src, k = source(plan[len(raws)])
                raws.append(load(src, k=k))

        def want_split():
            n = len(splits)
            if n >= len(plan):
                return
            while len(raws) <= n:
                want_raw()
            i, _, tok = raws[n]
            j, waits = WS.take()
            h, l = WH[:, j * 1024:(j + 1) * 1024], WL[:, j * 1024:(j + 1) * 1024]
            th = ACT.do(lambda e: e.copy(h, wslot(i)), tok, waits)
            tl = tt(l, wslot(i), h.bitcast(F32), ALU.subtract, th)
            W.give(i, tl)
            splits.append((j, h, l, tl))
            while len(raws) < min(len(plan), n + 3):
                want_raw()

        def pop(name, kind, n, at, half):
            key = plan[popped[0]]
            assert key == (name, kind, n, at, half), (key, (name, kind, n, at, half))
            while len(splits) < min(len(plan), popped[0] + 5):
                want_split()
            res = splits[popped[0]]
            popped[0] += 1
            background()
            return res

        xh, xl = v3(XH[:, :], 8), v3(XL[:, :], 8)
        gh, gl = v3(GH[:, :], 8), v3(GL[:, :], 8)
        xt = v3(XT[:, :], 8)

        def mm3(o, lh, ll, rh, rl, start, stop, *waits, inc=False):
            mm(o, lh, rh, start, False, *waits, skip=True)
            mm(o, lh, rl, False, False, skip=True)
            return mm(o, ll, rh, False, stop, inc=inc, skip=True)

        def split(h, l, src, tok):
            t = ACT.do(lambda e: e.copy(h, src), tok)
            return tt(l, src, h.bitcast(F32), ALU.subtract, t)

        def fm(name, n, c, htok):
            b, waits = PS.take()
            for half in range(2):
                j, h, l, tok = pop(name, "k", n, c, half)
                h, l = v3(h, 4), v3(l, 4)
                for f in range(2):
                    for k in range(4):
                        kk = 4 * half + k
                        t = mm3(bank(b, f * 256, f * 256 + 256), h[:, k, f * P:(f + 1) * P],
                                l[:, k, f * P:(f + 1) * P], xh[:, kk, :], xl[:, kk, :],
                                half == f == k == 0, kk == 7, waits, tok, htok[kk], inc=(f == 1 and k == 3))
                    if f == 0:
                        sideways()
                WS.give(j, t)
            return b, t

        def tm(name, n, c, htok):
            b, waits = PS.take()
            for half in range(2):
                j, h, l, tok = pop(name, "k", n, c, half)
                h, l = v3(h, 4), v3(l, 4)
                for m in range(2):
                    for k in range(4):
                        kk = 4 * half + k
                        sl = slice(m * P, (m + 1) * P)
                        t = mm3(bank(b, m * 256, m * 256 + 256), xh[:, kk, sl], xl[:, kk, sl], h[:, k, :],
                                l[:, k, :], half == m == k == 0, kk == 7, waits, tok, htok[kk],
                                inc=(m == 1 and k == 3))
                    if m == 0:
                        sideways()
                WS.give(j, t)
            return b, t

        acc_free = [[]]

        def down(name, n, r, h_, l_, first, last, *waits):
            j, h, l, tok = pop(name, "d", n, r, 0)
            ends = []
            for f in range(8):
                o = bank(4 + f // 2, (f % 2) * 256, (f % 2) * 256 + 256)
                fs = slice(f * P, (f + 1) * P)
                t = mm3(o, h[:, fs], l[:, fs], h_, l_, first and f % 2 == 0, last, list(waits), tok,
                        acc_free[0] if first else None, inc=(f == 7 or last and f % 2 == 1))
                if last and f % 2:
                    ends += [t, t]
            WS.give(j, t)
            return ends if last else t

        yacc = v3(PSB[:, :], 8)

        V, Y, A_, B_ = (RS[:, i * 256:(i + 1) * 256] for i in range(4))

        def rsqrt(ps, eps, n, tok):
            v, y, t = V[0:n, :], Y[0:n, :], A_[0:n, :]
            done = ts(v, ps, eps, None, ALU.add, None, tok)
            ts(y.bitcast(I32), v.bitcast(I32), -0.5, RSQRT_SEED, ALU.mult, ALU.add)
            c = math.sqrt(0.375)
            tt(t, y, y, ALU.mult)
            stt(t, t, c, v, ALU.mult, ALU.mult)
            stt(t, t, -1.25 / c, t, ALU.add, ALU.mult)
            stt(y, t, 1.875, y, ALU.add, ALU.mult)
            tt(t, y, y, ALU.mult)
            stt(t, t, -0.5, v, ALU.mult, ALU.mult)
            last = stt(y, t, 1.5, y, ALU.add, ALU.mult)
            return y, last, done

        def mean(src, toks):
            b, waits = PS.take()
            o = bank(b, 0, 256)
            for j in range(8):
                t = mm(o, onesd, src[:, j, :], j == 0, j == 7, waits, toks[j], inc=(j == 7))
            return b, o, t

        def square(src, toks):
            t1 = v3(T1[:, :], 8)
            res = []
            for j in range(0, 8, 2):
                t = act(t1[:, j:j + 2, :], src[:, j:j + 2, :], ACTF.Square, toks[j], toks[j + 1])
                res += [t, t]
            return t1, res

        def rms(src, toks):
            t1, sq = square(src, toks)
            b, ps, t = mean(t1, sq)
            r, rt, done = rsqrt(ps, 1e-6, P, t)
            PS.give(b, done)
            return r, rt

        SP.do(lambda e: e.dma_start(CT[:, :], a["consts"]).then_inc(s_in, 16), inc=False)
        SP.do(lambda e: e.dma_start(PR[:, :], a["params"]).then_inc(s_in, 16), inc=False)
        in_tok = ("in", s_in, 32)
        for m in range(2):
            SP.do(lambda e, m=m: e.dma_start(T2[:, m * 1024:(m + 1) * 1024], a["x"][m * P:(m + 1) * P, :])
                  .then_inc(s_x, 16), inc=False)
        for q in (PE, ACT, DVE, POOL):
            q.extra = [in_tok]
        x_tok = ("x", s_x, 32)

        xtok = [None] * 8
        for j in range(0, 8, 2):
            b, waits = PS.take()
            for jj in range(2):
                for m in range(2):
                    t = tr(bank(b, jj * 256 + m * P, jj * 256 + m * P + P),
                           T2[:, m * 1024 + (j + jj) * P:m * 1024 + (j + jj + 1) * P], P,
                           waits, x_tok, inc=(jj == m == 1))
            t = cp(XT[:, j * 256:(j + 2) * 256], bank(b), t, q=ACT)
            xtok[j] = xtok[j + 1] = t
            PS.give(b, t)

        csil = SM[:, 0:8]
        ct = act(csil, par("c"), ACTF.Silu)
        ct = ts(csil, csil, float(D), None, ALU.mult, None, ct)
        mod_tok = {}

        steps = [(n, part, k) for n in range(4) for part in (1, 0, 2) for k in range(8)]
        deep = keep(6 * 1024)
        afree = [[]] * 8

        def ada_buffer(x):
            i = x % 8 if x < 16 else x % 2
            return i, AD[:, i * 1024:(i + 1) * 1024] if i < 2 else deep[:, (i - 2) * 1024:(i - 1) * 1024]

        def ada_dma(x):
            n, part, k = steps[x]
            i, dst = ada_buffer(x)
            waits = afree[i]
            assert waits is not None
            afree[i] = None
            src = a["ada_w"][n // 2, n % 2][k * P:(k + 1) * P, part * 1024:(part + 1) * 1024]
            SP.do(lambda e: e.dma_start(dst, src).then_inc(asem[i], 16), waits, inc=False)
            acnt[i] += 16
            return i, dst, (f"a{i}", asem[i], acnt[i])

        def ada():
            got, asked = [], 0
            acc_tok = None
            for x, (n, part, k) in enumerate(steps):
                while asked < len(steps) and asked < x + (8 if asked < 16 else 2):
                    got.append(ada_dma(asked))
                    asked += 1
                i, w, tok = got.pop(0)
                if k == 0:
                    t = ts(ACC[:, :], w, csil[:, 0:1], None, ALU.mult, None, tok, acc_tok)
                else:
                    t = stt(ACC[:, :], w, csil[:, k:k + 1], ACC[:, :], ALU.mult, ALU.add, tok)
                afree[i] = t
                if k == 7:
                    yield
                    b, waits = PS.take()
                    for f in range(8):
                        t = mm(bank(b, f, f + 1), ACC[:, f * P:(f + 1) * P], onesd[:, 0:1], True, True, waits,
                               t if f == 0 else None, inc=(f == 7))
                    acc_tok = t
                    yield
                    m = MC[:, n * 24 + part * 8:n * 24 + part * 8 + 8]
                    t = tt(m, bank(b, 0, 8), par("adab", n * 24 + part * 8, 8), ALU.add, t)
                    PS.give(b, t)
                    if part == 1:
                        t = stt(m, m, 1.0, par("npre", n * 8, 8), ALU.add, ALU.mult)
                    if part == 2:
                        t = tt(m, m, par("npost", n * 8, 8), ALU.mult)
                    mod_tok[n, part] = t
                yield
            while True:
                yield

        ada_run = ada()

        side, rate, due = [], [0.0], [0.0]

        def background():
            due[0] += rate[0]
            while due[0] >= 1.0:
                due[0] -= 1.0
                next(ada_run)
            sideways()

        def sideways():
            for g in list(side):
                if next(g, "end") == "end":
                    side.remove(g)

        def slowly(g, k):
            for _ in g:
                for _ in range(k):
                    yield

        def drain(g):
            while g in side:
                if next(g, "end") == "end":
                    side.remove(g)

        def modulation(n, part):
            while (n, part) not in mod_tok:
                next(ada_run)
            return MC[:, n * 24 + part * 8:n * 24 + part * 8 + 8], mod_tok[n, part]

        def pre(n, xtok):
            if n == 0:
                modulation(n, 1)
                modulation(n, 0)
            r, rt = rms(xt, xtok)
            sc, t1 = modulation(n, 1)
            shift, t2_ = modulation(n, 0)
            t2 = v3(T2[:, :], 8)
            htok, high = [], []
            for j in range(8 + AHEAD):
                if j < 8:
                    t = stt(t2[:, j, :], xt[:, j, :], sc[:, j:j + 1], r, ALU.mult, ALU.mult)
                    high.append(act(xh[:, j, :], t2[:, j, :], ACTF.Identity, t, t2_, bias=shift[:, j:j + 1]))
                i = j - AHEAD
                if i >= 0:
                    htok.append(stt(xl[:, i, :], t2[:, i, :], shift[:, i:i + 1], xh[:, i, :].bitcast(F32),
                                    ALU.add, ALU.subtract, high[i]))
            return htok

        def post(n, ytok):
            r, rt = rms(yacc, ytok)
            g, _ = modulation(n, 2)
            t2 = v3(T2[:, :], 8)
            res = []
            high = []
            for j in range(8 + AHEAD):
                if j < 8:
                    t = stt(t2[:, j, :], yacc[:, j, :], g[:, j:j + 1], r, ALU.mult, ALU.mult)
                    last = tt(xt[:, j, :], xt[:, j, :], t2[:, j, :], ALU.add)
                    res.append(last)
                    if n == 3:
                        high.append(ACT.do(lambda e, j=j: e.copy(xh[:, j, :], xt[:, j, :]), last))
                i = j - AHEAD
                if n == 3 and i >= 0:
                    res[i] = tt(xl[:, i, :], xt[:, i, :], xh[:, i, :].bitcast(F32), ALU.subtract, high[i])
            acc_free[0] = [last, ACT.last()]
            return res

        def layer_norm(n, ytok):
            t2 = v3(T2[:, :], 8)
            tk = []
            for j in range(0, 8, 2):
                t = stt(t2[:, j:j + 2, :], xt[:, j:j + 2, :], DN_ALPHA, yacc[:, j:j + 2, :], ALU.mult, ALU.add, ytok[j])
                tk += [t, t]
            acc_free[0] = [t]
            b, ps, t = mean(t2, tk)
            cen = []
            for j in range(0, 8, 2):
                t = tt(t2[:, j:j + 2, :], t2[:, j:j + 2, :], rep(ps, 2), ALU.subtract, t)
                cen += [t, t]
            PS.give(b, t)
            t1, sq = square(t2, cen)
            b, ps, t = mean(t1, sq)
            r, rt, done = rsqrt(ps, 1e-5, P, t)
            PS.give(b, done)
            res = []
            high, whole = [], []
            for j in range(8 + AHEAD):
                if j < 8:
                    lb = par("lnb", n * 8 + j, 1)
                    t = stt(t2[:, j, :], t2[:, j, :], par("lng", n * 8 + j, 1), r, ALU.mult, ALU.mult)
                    high.append(act(xh[:, j, :], t2[:, j, :], ACTF.Identity, t, bias=lb))
                i = j - AHEAD
                if i >= 0:
                    lb = par("lnb", n * 8 + i, 1)
                    whole.append(act(xt[:, i, :], t2[:, i, :], ACTF.Identity, bias=lb))
                    res.append([stt(xl[:, i, :], t2[:, i, :], lb, xh[:, i, :].bitcast(F32), ALU.add, ALU.subtract,
                                    high[i]), whole[i]])
            return res

        def gated(pairs, htok, spread=None, weigh=None, bt=None):
            tmp = [v3(take(512), 2) for _ in range(2)]
            hfree = [None, None]
            pend = None
            n = len(pairs)

            def finish(p):
                i, hb, t = p
                for k in range(2):
                    t = down(*pairs[i][2 + k], gh[:, 2 * hb + k, :], gl[:, 2 * hb + k, :], i == k == 0,
                             i == n - 1 and k == 1, t)
                return t

            def product(i, ta, bu, tu):
                hb = i % 2
                if spread is not None:
                    ta = tt(tmp[hb], tmp[hb], wide2(spread[:, i, :]), ALU.mult, ta, bt[0], q=POOL)
                th = tt(tmp[hb], tmp[hb], v3(bank(bu), 2), ALU.mult, ta, tu)
                PS.give(bu, th)
                return i, hb, split(gh[:, 2 * hb:2 * hb + 2, :], gl[:, 2 * hb:2 * hb + 2, :], tmp[hb],
                                    [th, hfree[hb]])

            held = []
            for i, (g, u, _, _) in enumerate(pairs):
                hb = i % 2
                bg, tg = fm(*g, htok)
                ta = act(tmp[hb], v3(bank(bg), 2), ACTF.Silu, tg)
                PS.give(bg, ta)
                bu, tu = fm(*u, htok)
                held.append((i, ta, bu, tu))
                if weigh is not None and i == 0:
                    continue
                if weigh is not None and i == 1:
                    drain(weigh)
                for h_ in held:
                    nxt = product(*h_)
                    if pend:
                        hfree[pend[1]] = finish(pend)
                    pend = nxt
                held = []
            return finish(pend)

        def wide2(ap):
            return rep(ap, 2)

        def ffn(l, htok):
            return gated([(("ffn_w_in", (l,), i * 256), ("ffn_w_in", (l,), 2816 + i * 256),
                           ("ffn_w_out", (l,), i * 256), ("ffn_w_out", (l,), i * 256 + P))
                          for i in range(NF)], htok)

        def hybrid(htok):
            H = "hyb_w_in"
            invc = take(1024)
            SP.do(lambda e: e.dma_start(invc, a["aux"][:, 0:1024]).then_inc(s_aux, 16), inc=False)
            inv_tok = ("aux", s_aux, 16)
            U = v3(take(4 * 272), 4)
            w2, w4, w8 = (v3(take(4 * 272), 4) for _ in range(3))
            z = [DVE.do(lambda e, x=x: e.memset(x, 0.0)) for x in
                 (U[:, :, 0:16],)]
            for s in range(2):
                b, t = fm(H, (0,), s * 256, htok)
                tu = cp(U[:, 2 * s:2 * s + 2, 16:272], v3(bank(b), 2), t, z)
                PS.give(b, tu)
            tt(w2[:, :, 1:272], U[:, :, 1:272], U[:, :, 0:271], ALU.add, tu)
            tt(w4[:, 1:4, 3:272], w2[:, 1:4, 3:272], w2[:, 1:4, 1:270], ALU.add)
            tt(w8[:, 2:4, 7:272], w4[:, 2:4, 7:272], w4[:, 2:4, 3:268], ALU.add)
            tt(w2[:, 3:4, 16:272], w8[:, 3:4, 16:272], w8[:, 3:4, 8:264], ALU.add)
            dif = v3(take(1024), 4)
            ic = v3(invc, 4)
            for g, wsrc in enumerate((w2, w4, w8, w2)):
                tt(dif[:, g, :], wsrc[:, g, 16:272], ic[:, g, :], ALU.mult, inv_tok)
            td = tt(dif, dif, U[:, :, 16:272], ALU.subtract)
            YP = v3(take(1024), 4)
            Qh = take(1024)
            Kh = take(1024)
            Fh = take(1024)
            Sg = take(1024)
            lb = SM[:, 16:20]
            om = SM[:, 20:24]
            e0 = SM[:, 24:28]
            tt(e0, par("lbl"), par("lbl"), ALU.subtract)
            te = act(e0, e0, ACTF.Exp, DVE.last())
            recip(lb, e0, te)
            tt(lb, lb, e0, ALU.mult)
            tt(lb, lb, lb, ALU.subtract)
            ts(lb, lb, 0.0, None, ALU.max)
            ts(om, lb, -1.0, 1.0, ALU.mult, ALU.add)
            for s in range(2):
                b, t = fm(H, (0,), 512 + s * 256, htok)
                tq = act(Qh[:, s * 512:(s + 1) * 512], bank(b), ACTF.Silu, t)
                PS.give(b, tq)
            pi, pw, ptok = load(a["pool_w"][0].rearrange("g c d -> c g d"), cols=512, k=4)
            for s in range(2):
                b, waits = PS.take()
                for gg in range(2):
                    g = 2 * s + gg
                    t = mm(bank(b, gg * 256, gg * 256 + 256), pw[:, g, :], dif[:, g, :], True, True,
                           waits, ptok, td, inc=(gg == 1))
                for gg in range(2):
                    g = 2 * s + gg
                    ty = act(YP[:, g, :], bank(b, gg * 256, gg * 256 + 256), ACTF.Copy, t,
                             scale=par("pscale", g, 1))
                PS.give(b, ty)
            W.give(pi, t)
            typ = split(gh[:, 0:4, :], gl[:, 0:4, :], YP, ty)
            for s in range(2):
                b, t = fm(H, (0,), 1024 + s * 256, htok)
                sl = slice(s * 512, (s + 1) * 512)
                t1 = act(Fh[:, sl], bank(b), ACTF.Sigmoid, t)
                t2 = act(Kh[:, sl], bank(b), ACTF.Sigmoid, scale=-1.0)
                PS.give(b, t2)
            for h in range(4):
                sl = slice(h * 256, (h + 1) * 256)
                ts(Fh[:, sl], Fh[:, sl], om[:, h:h + 1], lb[:, h:h + 1], ALU.mult, ALU.add, t2)
                tf = ts(Kh[:, sl], Kh[:, sl], om[:, h:h + 1], None, ALU.mult)
            res = {}
            Am = v3(take(1024), 8)
            A2 = v3(take(512), 4)

            def decays():
                q4, k4 = v3(Qh, 4), v3(Kh, 4)
                tot = Fh
                t_mm = None
                nxt = take(512)
                spare = take(256)
                ready = [tq, tf]
                levels = [0, 1, 2, 4, 8, 16, 32, 64]
                for li, h in enumerate(levels):
                    if h == 1:
                        tq1 = tt(Qh, Qh, Fh, ALU.mult, t_mm)
                        ready = [tq1]
                    if h > 1:
                        g = h // 2
                        n = 1024 // h
                        qv = Qh.rearrange("p (n b c) -> p n b c", n=n, b=2)
                        kv = Kh.rearrange("p (n b c) -> p n b c", n=n, b=2)
                        tv_ = tot[:, 0:2 * n].rearrange("p (n b) -> p n b", b=2)
                        tt(qv[:, :, 1, :], qv[:, :, 1, :], wide(tv_[:, :, 0], g), ALU.mult, t_mm)
                        tt(kv[:, :, 0, :], kv[:, :, 0, :], wide(tv_[:, :, 1], g), ALU.mult)
                        dst = nxt if tot is not nxt else spare
                        t = tt(dst[:, 0:n], tv_[:, :, 0], tv_[:, :, 1], ALU.mult)
                        tot = dst
                        ready = [t]
                        yield
                    got = []
                    for half in range(2):
                        b, waits = PS.take()
                        got.append(b)
                        for x in range(4):
                            hd, m = 2 * half + x // 2, x % 2
                            t_mm = mm(bank(b, x * P, x * P + P), k4[:, hd, m * P:m * P + P],
                                      q4[:, hd, m * P:m * P + P], True, True, waits, ready, inc=(x == 3))
                        got[-1] = (b, t_mm)
                        yield
                    for half, (b, t_b) in enumerate(got):
                        dst = Am[:, 4 * half:4 * half + 4, :]
                        if h == 0:
                            tm_ = tt(dst, v3(bank(b), 4), rep(ident, 4), ALU.mult, t_b)
                        else:
                            mk = cst("hm", (li - 1) * P, P).bitcast(I32)
                            tm_ = DVE.do(lambda e, dst=dst, mk=mk, b=b: e.copy_predicated(
                                dst, rep(mk, 4), v3(bank(b), 4)), t_b)
                        PS.give(b, tm_)
                    yield
                n = 1024 // 128
                qv = Qh.rearrange("p (n b c) -> p n b c", n=n, b=2)
                kv = Kh.rearrange("p (n b c) -> p n b c", n=n, b=2)
                tv_ = tot[:, 0:2 * n].rearrange("p (n b) -> p n b", b=2)
                tt(qv[:, :, 1, :], qv[:, :, 1, :], wide(tv_[:, :, 0], 64), ALU.mult, t_mm)
                t = tt(kv[:, :, 0, :], kv[:, :, 0, :], wide(tv_[:, :, 1], 64), ALU.mult)
                yield
                b, waits = PS.take()
                for hd in range(4):
                    t = mm(bank(b, hd * P, hd * P + P), k4[:, hd, 0:P], q4[:, hd, P:2 * P], True, True,
                           waits, t, inc=(hd == 3)) or t
                t2 = cp(A2, v3(bank(b), 4), t, q=ACT)
                PS.give(b, t2)
                res['t2'], res['tm'] = t2, tm_
                yield

            lv = decays()
            side.append(lv)
            Vt = v3(take(1024), 2)
            for s in range(2):
                b, t = tm(H, (0,), 1536 + s * 256, htok)
                tv = cp(Vt[:, :, s * 256:(s + 1) * 256], v3(bank(b), 2), t, q=ACT)
                PS.give(b, tv)
            for s in range(2):
                b, t = fm(H, (0,), 2048 + s * 256, htok)
                tg = act(Sg[:, s * 512:(s + 1) * 512], bank(b), ACTF.Silu, t)
                PS.give(b, tg)


            def out_rows(lo, hi, tok):
                for s in range(lo, hi):
                    t = down("hyb_w_out", (0,), s * P, gh[:, s, :], gl[:, s, :], s == 0, s == 7, tok)
                return t

            drain(lv)
            t2, tm_ = res['t2'], res['tm']
            b, waits = PS.take(2)
            o = PSA[:, b * 512:b * 512 + 1024]
            for hd in range(4):
                c = hd * 256
                vh = slice(hd * P, hd * P + P)
                mm(o[:, c:c + P], Vt[:, 0, vh], Am[:, 2 * hd, :], True, True, waits, t2, tm_, tv)
                mm(o[:, c + P:c + 256], Vt[:, 1, vh], Am[:, 2 * hd + 1, :], True, False)
                t = mm(o[:, c + P:c + 256], Vt[:, 0, vh], A2[:, hd, :], False, True, inc=True)
            sq = T1[:, 0:1024]
            t = act(sq, o, ACTF.Square, t)
            out_rows(0, 1, typ)
            b2, waits = PS.take()
            st = bank(b2, 0, 256, p=4)
            for hd in range(4):
                ti = mm(st, cst("hsel", 4 * hd, 4), sq[:, hd * 256:hd * 256 + 256], hd == 0, hd == 3,
                        waits, t, inc=(hd == 3))
            r, rt, done = rsqrt(st, 1e-6, 4, ti)
            PS.give(b2, done)
            YH = take(1024)
            t1 = stt(YH, o, par("onorm"), Sg, ALU.mult, ALU.mult, tg)
            PS.give(b, t1, k=2)
            out_rows(1, 3, typ)
            b, waits = PS.take(2)
            for hd in range(4):
                t = mm(PSA[:, b * 512 + hd * 256:b * 512 + hd * 256 + 256], row_of(hd, 4), r,
                       True, True, waits, rt, inc=(hd == 3))
            th = tt(YH, YH, PSA[:, b * 512:b * 512 + 1024], ALU.mult, t)
            PS.give(b, th, k=2)
            out_rows(3, 4, typ)
            th = [split(gh[:, x:x + 2, :], gl[:, x:x + 2, :], v3(YH, 4)[:, x - 4:x - 2, :], th) for x in (4, 6)]
            out_rows(4, 6, th[0])
            t = out_rows(6, 8, th[1])
            return t

        def attend(units, scores, soft, blocks, value, pts):
            NB = 2
            pfree = [None] * NB
            st = {}
            done = None

            def transposes(u):
                pr, tk = st[u]["p"]
                n = blocks(units[u])
                if n <= 4:
                    b, waits = PT.take()
                    kk = 1
                else:
                    b, waits = PT.take(2)
                    kk = 2
                for x in range(n):
                    t = tr(bank(b + x // 4, (x % 4) * P, (x % 4) * P + P), pr[:, x * P:(x + 1) * P], P,
                           waits, tk, inc=(x == n - 1))
                dst = pts[u % NB]
                o = (b - 4) * 512
                t2 = cp(dst[:, 0:n * P], PSB[:, o:o + n * P], t, pfree[u % NB], q=ACT)
                PT.give(b, t2, k=kk)
                st[u]["pt"] = (dst, t2)
                return t

            N = len(units)
            for u in range(N + 2):
                if u < N:
                    st[u] = {"s": scores(units[u])}
                    st[u]["p"] = soft(units[u], st[u]["s"])
                sideways()
                sideways()
                if 2 <= u:
                    done = value(units[u - 2], *st[u - 2]["pt"])
                    pfree[u % NB] = done
                sideways()
                if 1 <= u <= N:
                    st[u - 1]["tt"] = transposes(u - 1)
                    sfree[0][units[u - 1][2] % 3] = st[u - 1]["tt"]
                background()
                sideways()
            return done

        sfree = [[None] * 3]

        def dilated(htok):
            wq = "att_w_qkv"
            ai, aux, atok = load(a["aux"][:, 1024:AN], cols=AN - 1024, k=1)
            b, waits = PS.take()
            oh = aux[0:32, 0:384]
            mv = aux[0:24, 384:768]
            rb = aux[0:32, 768:792]
            t = mm(bank(b, 0, 384, p=24), rb, oh, True, True, waits, atok, inc=True)
            brow = SM[0:24, 64:448]
            t = tt(brow, bank(b, 0, 384, p=24), mv, ALU.add, t, atok)
            W.give(ai, t)
            PS.give(b, t)
            ACT.do(lambda e: e.dma_start(scratch[:, :], brow).then_inc(s_bias, 16), t, inc=False)
            ACT.open = False
            bt = take(6144)
            src = bass.AP(scratch, 0, [[1, P], [384, 24], [1, 256]])
            ACT.do(lambda e: e.dma_start(v3(bt, 24), src).then_inc(s_tp, 16), ("bias", s_bias, 16), inc=False)
            ACT.open = False
            btok = ("tp", s_tp, 16)

            def bias_of(h, n):
                pp = [list(x) for x in bt.ap][0]
                return bass.AP(bt.tensor, bt.offset + h * 256 + n - 1, [pp, [8 * 256, 3], [-1, n]])

            qf = v3(take(3072), 12)
            kf = v3(take(3072), 12)
            vt = v3(take(3072), 2)
            for s in range(6):
                b, t = fm(wq, (0,), s * 256, htok)
                tq = act(qf[:, 2 * s:2 * s + 2, :], v3(bank(b), 2), ACTF.Copy, t, scale=0.125)
                PS.give(b, tq)
            for s in range(6):
                b, t = fm(wq, (0,), 1536 + s * 256, htok)
                tk = cp(kf[:, 2 * s:2 * s + 2, :], v3(bank(b), 2), t)
                PS.give(b, tk)
            for s in range(6):
                b, t = tm(wq, (0,), 3072 + s * 256, htok)
                tv = cp(vt[:, :, s * 256:s * 256 + 256], v3(bank(b), 2), t)
                PS.give(b, tv)

            Sb = [T1[:, 0:768], T1[:, 768:1536], T2[:, 0:768]]
            pts = [T2[:, 768:1536], take(768)]
            sfree[0] = [None] * 3
            mx = SM[:, 448:464]
            den = SM[:, 464:480]
            rd = SM[:, 480:496]
            units = [(qt, h, 8 * qt + h) for qt in range(2) for h in range(8)]

            def scores(u):
                qt, h, i = u
                n = (qt + 1) * P
                b, waits = PS.take(2)
                o = (h % 2) * 64
                for g in range(3):
                    tile = g * 4 + h // 2
                    t = mm(PSA[:, b * 512 + g * 256:b * 512 + g * 256 + n],
                           qf[o:o + 64, tile, qt * P:qt * P + P], kf[o:o + 64, tile, 0:n],
                           True, True, waits, tq, tk, inc=(g == 2))
                return b, t

            def soft(u, s):
                qt, h, i = u
                b, t = s
                n = (qt + 1) * P
                sbf = Sb[i % 3][:, 0:3 * n]
                ps = v3(PSA[:, b * 512:b * 512 + 768], 3)[:, :, 0:n]
                t = tt(v3(sbf, 3), ps, bias_of(h, n), ALU.add, t, btok, sfree[0][i % 3])
                PS.give(b, t, k=2)
                red(mx[:, i:i + 1], sbf, ALU.max)
                t = ts(mx[:, i:i + 1], mx[:, i:i + 1], -1.0, None, ALU.mult)
                t = act(sbf, sbf, ACTF.Exp, t, bias=mx[:, i:i + 1], accum=den[:, i:i + 1])
                return sbf, t

            def value(u, pt, tok):
                qt, h, i = u
                x = 0
                for g in range(3):
                    for kt in range(qt + 1):
                        c = g * 512 + h * 64
                        t = mm(bank(4 + qt, h * 64, h * 64 + 64), pt[:, x * P:(x + 1) * P],
                               vt[:, kt, c:c + 64], x == 0, x == 3 * (qt + 1) - 1, tok, tv,
                               acc_free[0], inc=(x == 3 * (qt + 1) - 1))
                        x += 1
                return t

            done = attend(units, scores, soft, lambda u: 3 * (u[0] + 1), value, pts)
            ot = T1[:, 0:1024]
            recip(rd, den, ACT.last())
            for qt in range(2):
                td = tt(v3(ot[:, qt * 512:(qt + 1) * 512], 8), v3(bank(4 + qt), 8),
                        wide(rd[:, 8 * qt:8 * qt + 8], 64), ALU.mult, done)
            return project_tokens(ot, td, "att_w_out", True)

        def to_features(ot, td):
            res = []
            for f in range(0, 4, 2):
                b, waits = PS.take()
                for ff in range(2):
                    for m in range(2):
                        t = tr(bank(b, ff * 256 + m * P, ff * 256 + m * P + P),
                               ot[:, m * 512 + (f + ff) * P:m * 512 + (f + ff + 1) * P], P,
                               waits, td, inc=(ff == m == 1))
                t = split(gh[:, f:f + 2, :], gl[:, f:f + 2, :], v3(bank(b), 2), t)
                PS.give(b, t)
                res += [t, t]
            return res

        def project_tokens(ot, td, wout, last):
            tf = to_features(ot, td)
            acc_free[0] = acc_free[0] + [td]
            for s in range(4):
                t = down(wout, (0,), s * P, gh[:, s, :], gl[:, s, :], s == 0, last and s == 3, tf[s])
            return t

        def log_sigmoid(x, t0, t1, tok):
            stt(t0, x, -1.0, x, ALU.mult, ALU.min, tok)
            t = act(t0, t0, ACTF.Exp, DVE.last())
            t = act(t0, t0, ACTF.Ln, bias=1.0)
            return stt(x, x, 0.0, t0, ALU.min, ALU.subtract, t)

        def fox(xtok):
            wi = a["even_w_in_2"][0]
            src = xt
            ta = s5_angles(0, None, s5_state)
            qf, kf, uf = (v3(take(1024), 4) for _ in range(3))
            vt = v3(take(1024), 2)
            cf = take(256)[0:8, :]
            cw = take(256)[0:8, :]
            gi, gw, gtok = load(wi[:, 1536:1544].rearrange("(k p) n -> p k n", p=P), cols=64, k=8)
            b, waits = PS.take()
            for k in range(8):
                t = mm(bank(b, 0, 256, p=8), gw[:, k, :], src[:, k, :], k == 0, k == 7, waits, gtok,
                       xtok[k], inc=(k == 7))
            W.give(gi, t)
            t = ts(cf, bank(b, 0, 256, p=8), par("fb", 0, 1, p=8), None, ALU.add, None, t)
            PS.give(b, t)
            t = log_sigmoid(cf, cw, None, t)
            DVE.do(lambda e: e.memset(cw, 0.0))
            t = scan(cw, cf, cw, 0.0, ALU.add, ALU.add)
            tc_ = ts(cf, cw, -1.0, None, ALU.mult)
            cpos, cneg = cw, cf

            E = "even_w_in_2"
            for s in range(2):
                b, t = fm(E, (0,), 1544 + s * 256, xtok)
                tu = cp(uf[:, 2 * s:2 * s + 2, :], v3(bank(b), 2), t)
                PS.give(b, tu)
            YS = v3(take(1024), 4)
            ys5 = {}
            s5g = s5(uf, tu, YS, ys5, s5_state, ta)
            side.append(s5g)
            for s in range(2):
                b, t = fm(E, (0,), s * 256, xtok)
                tq = act(qf[:, 2 * s:2 * s + 2, :], v3(bank(b), 2), ACTF.Copy, t, scale=0.125)
                PS.give(b, tq)
            for s in range(2):
                b, t = fm(E, (0,), 512 + s * 256, xtok)
                tk = cp(kf[:, 2 * s:2 * s + 2, :], v3(bank(b), 2), t)
                PS.give(b, tk)
            for s in range(2):
                b, t = tm(E, (0,), 1024 + s * 256, xtok)
                tv = cp(vt[:, :, s * 256:s * 256 + 256], v3(bank(b), 2), t)
                PS.give(b, tv)

            Sb = [take(256) for _ in range(3)]
            pts = [take(256) for _ in range(2)]
            sfree[0] = [None] * 3
            mx, den, rd = SM[:, 448:464], SM[:, 464:480], SM[:, 480:496]
            units = [(qt, h, 8 * qt + h) for qt in range(2) for h in range(8)]

            def scores(u):
                qt, h, i = u
                n = (qt + 1) * P
                b, waits = PS.take()
                o = (h % 2) * 64
                r = bank(b, 0, n)
                mm(bank(b, n - P, n), ident, cst("causal"), True, False, waits, skip=True)
                mm(r, qf[o:o + 64, h // 2, qt * P:qt * P + P], kf[o:o + 64, h // 2, 0:n], False, False,
                   tq, tk, skip=True)
                mm(r, cpos[:, qt * P:qt * P + P], ident[0:8, h:h + 1].to_broadcast([8, n]), False, False, tc_,
                   skip=True)
                t = mm(r, row_of(h, 8), cneg[:, 0:n], False, True, inc=True, skip=True)
                return b, t

            def soft(u, s):
                qt, h, i = u
                b, t = s
                n = (qt + 1) * P
                sbf = Sb[i % 3][:, 0:n]
                red(mx[:, i:i + 1], bank(b, 0, n), ALU.max, t)
                t = ts(mx[:, i:i + 1], mx[:, i:i + 1], -1.0, None, ALU.mult)
                t = act(sbf, bank(b, 0, n), ACTF.Exp, t, sfree[0][i % 3], bias=mx[:, i:i + 1],
                        accum=den[:, i:i + 1])
                PS.give(b, t)
                return sbf, t

            def value(u, pt, tok):
                qt, h, i = u
                for kt in range(qt + 1):
                    t = mm(bank(4 + qt, h * 64, h * 64 + 64), pt[:, kt * P:(kt + 1) * P],
                           vt[:, kt, h * 64:h * 64 + 64], kt == 0, kt == qt, tok, tv, acc_free[0],
                           inc=(kt == qt))
                return t

            done = attend(units, scores, soft, lambda u: u[0] + 1, value, pts)
            ot = take(1024)
            recip(rd, den, ACT.last())
            for qt in range(2):
                td = tt(v3(ot[:, qt * 512:(qt + 1) * 512], 8), v3(bank(4 + qt), 8),
                        wide(rd[:, 8 * qt:8 * qt + 8], 64), ALU.mult, done)
            t = project_tokens(ot, td, "even_w_out_2", False)

            drain(s5g)
            ys = (YS, ys5['t'])
            y2 = qf
            gws = [load(a["s5_w_glu_2"][0][256 * x:256 * x + 256, :].rearrange("(k p) n -> p k n", p=P), k=2)
                   for x in range(2)]
            for s in range(2):
                b, waits = PS.take()
                for f in range(2):
                    for k in range(4):
                        ff = 2 * s + f
                        gi, gw, gtok = gws[k // 2]
                        t = mm(bank(b, f * 256, f * 256 + 256), gw[:, k % 2, ff * P:ff * P + P], ys[0][:, k, :],
                               k == 0, k == 3, waits, gtok, ys[1], inc=(f == 1 and k == 3))
                for f in range(2):
                    ff = 2 * s + f
                    tg = act(y2[:, ff, :], bank(b, f * 256, f * 256 + 256), ACTF.Sigmoid, t,
                             bias=par("bglu", ff, 1))
                PS.give(b, tg)
            for x in range(2):
                W.give(gws[x][0], t)
            ty = tt(y2, y2, ys[0], ALU.mult, tg)
            ty = split(gh[:, 4:8, :], gl[:, 4:8, :], y2, ty)
            for s in range(4, 8):
                t = down("even_w_out_2", (0,), s * P, gh[:, s, :], gl[:, s, :], False, s == 7, ty)
            return t

        def reduce_angle(x, n, *waits, q=None):
            c1 = 6.28125
            c2 = 0.0019350051879882812
            c3 = TWO_PI - c1 - c2
            ts(n, x, 1.0 / TWO_PI, ROUND, ALU.mult, ALU.add, *waits)
            ts(n, n, ROUND, None, ALU.subtract)
            stt(x, n, -c1, x, ALU.mult, ALU.add)
            stt(x, n, -c2, x, ALU.mult, ALU.add)
            stt(x, n, -c3, x, ALU.mult, ALU.add)
            return ts(x, x, 3.1415925, -3.1415925, ALU.min, ALU.max)

        XW = AD[:, 0:1024]

        def pool_angle(x, n, *waits):
            c1 = 6.28125
            c2 = 0.0019350051879882812
            c3 = TWO_PI - c1 - c2
            ts(n, x, 1.0 / TWO_PI, ROUND, ALU.mult, ALU.add, *waits, q=POOL)
            ts(n, n, -1.0, ROUND, ALU.mult, ALU.add, q=POOL)
            for c in (c1, c2, c3):
                ts(v3(XW, 4), n, c, 1.0, ALU.mult, ALU.mult, q=POOL)
                tt(x, x, v3(XW, 4), ALU.add, q=POOL)
            return ts(x, x, 3.1415925, -3.1415925, ALU.min, ALU.max, q=POOL)

        def s5_setup(st):
            sm = keep(16 * 13)
            c = [sm[:, i * 16:(i + 1) * 16] for i in range(13)]
            dt, mag, th, nn, cs, sn, lre, lim, den, zre, zim, t0, t1 = c
            are, aim = par("are"), par("aim")
            half = cst("half", 0, 1)
            blk = keep(1024)
            BT = [v3(keep(512), 4) for _ in range(2)]
            CTt = [v3(keep(512), 4) for _ in range(2)]
            before = ACT.last()
            t = act(dt, par("ldt"), ACTF.Exp)
            yield
            tt(mag, are, dt, ALU.mult, t)
            yield
            t = act(mag, mag, ACTF.Exp, DVE.last())
            tt(th, aim, dt, ALU.mult)
            t2 = reduce_angle(th, nn)
            yield
            act(sn, th, ACTF.Sin, t2)
            act(cs, th, ACTF.Abs)
            t = act(cs, cs, ACTF.Sin, scale=-1.0, bias=half)
            th_tok = t2
            yield
            tt(lre, mag, cs, ALU.mult, t)
            tt(lim, mag, sn, ALU.mult)
            ts(lre, lre, -1.0, None, ALU.add)
            tt(den, are, are, ALU.mult)
            tt(t0, aim, aim, ALU.mult)
            tt(den, den, t0, ALU.add)
            recip(den, den)
            yield
            tt(zre, lre, are, ALU.mult)
            tt(t0, lim, aim, ALU.mult)
            tt(zre, zre, t0, ALU.add)
            tt(zre, zre, den, ALU.mult)
            tt(zim, lim, are, ALU.mult)
            tt(t0, lre, aim, ALU.mult)
            tt(zim, zim, t0, ALU.subtract)
            tt(zim, zim, den, ALU.mult)
            yield
            bre, bim = v3(par("bre"), 16), v3(par("bim"), 16)
            bb = [v3(T2[:, 256 * x:256 * x + 256], 16) for x in range(2)]
            w0 = v3(T2[:, 512:768], 16)
            tt(bb[0], bre, wide(zre, 16), ALU.mult, before)
            tt(w0, bim, wide(zim, 16), ALU.mult)
            tt(bb[0], bb[0], w0, ALU.subtract)
            yield
            tt(bb[1], bim, wide(zre, 16), ALU.mult)
            tt(w0, bre, wide(zim, 16), ALU.mult)
            tt(bb[1], bb[1], w0, ALU.add)
            yield
            POOL.do(lambda e: e.memset(blk, 0.0))
            for r in range(2):
                bv = blk[:, r * 512:(r + 1) * 512].rearrange("p (j e c) -> p j e c", j=16, e=2)
                for e_ in range(2):
                    t = cp(bv[e_ * 64:e_ * 64 + 64, :, e_, :], bb[r][e_ * 64:e_ * 64 + 64, :, :], POOL.last())
            yield
            for r in range(2):
                b, waits = PS.take()
                for i in range(4):
                    t2 = tr(bank(b, i * P, i * P + P), blk[:, r * 512 + i * P:r * 512 + i * P + P], P,
                            waits, t, inc=(i == 3))
                yield
                t3 = cp(BT[r], v3(bank(b), 4), t2, q=ACT)
                PS.give(b, t3)
            tbt = t3
            yield
            cblk = v4(blk, 2, 4)
            ev, od = cst("half", 1, 1), cst("firsts", 0, 1)
            for r, nm in enumerate(("cre", "cim")):
                cv = v3(par(nm), 4)
                ts(cblk[:, r, :, 0:64], cv, ev, 1.0 if r == 0 else -1.0, ALU.mult, ALU.mult, t2)
                t = ts(cblk[:, r, :, 64:128], cv, od, 1.0 if r == 0 else -1.0, ALU.mult, ALU.mult)
                yield
            for r in range(2):
                b, waits = PS.take()
                for i in range(4):
                    t2 = tr(bank(b, i * P, i * P + P), cblk[:, r, i, :], P, waits, t, inc=(i == 3))
                yield
                t3 = cp(CTt[r], v3(bank(b), 4), t2, q=ACT)
                PS.give(b, t3)
            st.update(mag=mag, th=th, blk=blk, BT=BT, CTt=CTt, tbt=tbt, tct=t3, t_nn=t2, th_tok=th_tok,
                      An=v3(keep(1024), 4))

        def s5_angles(i, free, st):
            for jj in range(4):
                ts(st["An"][:, jj, :], cst("tt"), st["th"][:, 4 * i + jj:4 * i + jj + 1], 1.0, ALU.mult, ALU.mult,
                   st["th_tok"], free, q=POOL)
            return pool_angle(st["An"], v3(ACC[:, :], 4))

        def s5(uf, tu, YS, out_, st, ta):
            mag, blk, BT, CTt, tbt, tct, An = (st[x] for x in ("mag", "blk", "BT", "CTt", "tbt", "tct", "An"))
            half = cst("half", 0, 1)
            C, Sn, Gr, Gi = (v3(x, 4) for x in (T1[:, 0:1024], T1[:, 1024:2048], T2[:, 0:1024], T2[:, 1024:2048]))
            Br, Bi = (v3(take(1024), 4) for _ in range(2))
            Nn = v3(blk, 4)
            t_prev = t_free = None
            t_nn = st["t_nn"]
            for _ in range(5):
                yield
            for i in range(4):
                act(Sn, An, ACTF.Sin, ta, t_free)
                act(C, An, ACTF.Abs)
                tsc = act(C, C, ACTF.Sin, scale=-1.0, bias=half)
                if i < 3:
                    ta = s5_angles(i + 1, tsc, st)
                for _ in range(1):
                    yield
                for jj in range(4):
                    b, waits = PS.take()
                    for r in range(2):
                        t = mm(bank(b, r * 256, r * 256 + 256), BT[r][32 * jj:32 * jj + 32, i, :],
                               uf[32 * jj:32 * jj + 32, i, :], True, True, waits, tbt, tu, inc=(r == 1))
                    cp(Br[:, jj, :], bank(b, 0, 256), t, t_free, q=ACT)
                    t = cp(Bi[:, jj, :], bank(b, 256, 512), q=ACT)
                    PS.give(b, t)
                    if i < 2 or jj == 1:
                        yield
                yield
                tt(Gr, Br, C, ALU.mult, t, tsc, t_prev)
                yield
                tt(Nn, Bi, Sn, ALU.mult, t_nn)
                yield
                tt(Gr, Gr, Nn, ALU.add)
                yield
                tt(Gi, Bi, C, ALU.mult)
                yield
                tt(Nn, Br, Sn, ALU.mult)
                yield
                tt(Gi, Gi, Nn, ALU.subtract)
                yield
                for jj in range(4):
                    m = mag[:, 4 * i + jj:4 * i + jj + 1].to_broadcast([P, 256])
                    scan(Br[:, jj, :], m, Gr[:, jj, :], 0.0, ALU.mult, ALU.add)
                    scan(Bi[:, jj, :], m, Gi[:, jj, :], 0.0, ALU.mult, ALU.add)
                    yield
                tt(Gr, Br, C, ALU.mult)
                yield
                tt(Nn, Bi, Sn, ALU.mult)
                yield
                tt(Gr, Gr, Nn, ALU.subtract)
                yield
                tt(Gi, Bi, C, ALU.mult)
                yield
                tt(Nn, Br, Sn, ALU.mult)
                yield
                t = t_free = tt(Gi, Gi, Nn, ALU.add)
                yield
                b, waits = PS.take()
                for jj in range(4):
                    o = bank(b, 0, 256, p=32, p0=32 * jj)
                    mm(o, CTt[0][:, i, 32 * jj:32 * jj + 32], Gr[:, jj, :], True, False, waits, t, tct)
                    t_prev = mm(o, CTt[1][:, i, 32 * jj:32 * jj + 32], Gi[:, jj, :], False, True, inc=(jj == 3))
                yield
                t = stt(YS[:, i, :], uf[:, i, :], par("s5d", i, 1), bank(b, 0, 256), ALU.mult, ALU.add, t_prev)
                PS.give(b, t)
            out_["t"] = act(YS, YS, ACTF.Gelu_apprx_tanh, t)
            yield

        def mlstm(xtok):
            wi = a["odd_w_in_2"][0]
            src = xt
            qk = [v3(take(2048), 8) for _ in range(2)]
            vt = v3(take(2048), 2)
            og = v3(take(2048), 8)
            pad = [take(260) for _ in range(4)]
            acc = [take(256) for _ in range(4)]
            pfree = [None] * 4
            afree = [None] * 4
            late = []
            gf = [take(256)[0:8, :] for _ in range(4)]
            lf, g, mr, wk_ = gf
            gi, gw, gtok = load(wi[:, 4096:4112].rearrange("(k p) n -> p k n", p=P), cols=128, k=8)
            nm = SM[:, 500:532]
            em = SM[:, 532:564]
            got = {}

            def gates():
                b, waits = PS.take()
                for r in range(2):
                    for k in range(8):
                        t = mm(bank(b, r * 256, r * 256 + 256, p=8), gw[:, k, 8 * r:8 * r + 8], src[:, k, :],
                               k == 0, k == 7, waits, gtok, xtok[k], inc=(r == 1 and k == 7))
                W.give(gi, t)
                yield
                ts(g, bank(b, 0, 256, p=8), par("fb", 1, 1, p=8), None, ALU.add, None, t)
                t = ts(lf, bank(b, 256, 512, p=8), par("fb", 2, 1, p=8), None, ALU.add)
                PS.give(b, t)
                yield
                log_sigmoid(lf, wk_, None, t)
                yield
                DVE.do(lambda e: e.memset(wk_, 0.0))
                scan(wk_, lf, wk_, 0.0, ALU.add, ALU.add)
                Fc = wk_
                yield
                got["g"] = tt(g, g, Fc, ALU.subtract)
                scan(mr, g, g, 0.0, ALU.max, ALU.max)
                t = tt(lf, Fc, mr, ALU.add)
                yield
                b, waits = PS.take()
                for m in range(2):
                    tr(bank(b, m * 16, m * 16 + 8), mr[:, m * P:(m + 1) * P], 8, waits, t)
                    t2 = tr(bank(b, m * 16 + 8, m * 16 + 16), lf[:, m * P:(m + 1) * P], 8, inc=(m == 1))
                yield
                t = ts(nm, bank(b, 0, 32), -1.0, None, ALU.mult, None, t2)
                PS.give(b, t)
                yield
                got["em"] = act(em, nm, ACTF.Exp, t)
                got["nm"] = t

            gate_run = gates()
            next(gate_run)
            side.append(gate_run)
            zt = [DVE.do(lambda e, x=x: e.memset(x[:, 0:3], 0.0)) for x in pad]
            O = "odd_w_in_2"

            def silus(keep_=2):
                while len(late) > keep_:
                    c, td = late.pop(0)
                    afree[c % 4] = act(qk[c // 8][:, c % 8, :], acc[c % 4], ACTF.Silu, td)

            for s in range(8):
                b, t = fm(O, (0,), s * 256, xtok)
                for f in range(2):
                    c = 2 * s + f
                    pb, ab = c % 4, c % 4
                    tp = cp(pad[pb][:, 3:259], bank(b, f * 256, f * 256 + 256), t, zt, pfree[pb], q=ACT)
                    ts(acc[ab], pad[pb][:, 0:256], par("convw", c, 1), par("convb", c, 1), ALU.mult, ALU.add,
                       tp, afree[ab])
                    for w in range(1, 4):
                        td = stt(acc[ab], pad[pb][:, w:w + 256], par("convw", w * 16 + c, 1), acc[ab],
                                 ALU.mult, ALU.add)
                    pfree[pb] = td
                    late.append((c, td))
                PS.give(b, tp)
                if s:
                    silus()
            silus(0)
            tqk = ACT.last()
            for s in range(4):
                b, t = tm(O, (0,), 2048 + s * 256, xtok)
                tv = cp(vt[:, :, s * 256:s * 256 + 256], v3(bank(b), 2), t)
                PS.give(b, tv)
            for s in range(4):
                b, t = fm(O, (0,), 3072 + s * 256, xtok)
                to = act(og[:, 2 * s:2 * s + 2, :], v3(bank(b), 2), ACTF.Sigmoid, t)
                PS.give(b, to)
            drain(gate_run)
            tg_, t_em, t_nm = got["g"], got["em"], got["nm"]

            Sb = [take(256) for _ in range(3)]
            Db = [take(256) for _ in range(2)]
            pts = [take(256) for _ in range(2)]
            sfree[0] = [None] * 3
            den = SM[:, 564:580]
            rd = SM[:, 580:596]
            units = [(qt, h, 2 * h + qt) for h in range(8) for qt in range(2)]
            hfree = [None] * 2
            hout = og
            st = {}
            INV = 128.0 ** -0.5

            def scores(u):
                qt, h, i = u
                n = (qt + 1) * P
                b, waits = PS.take()
                mm(bank(b, 0, n), qk[0][:, h, qt * P:qt * P + P], qk[1][:, h, 0:n], True, True, waits, tqk)
                mm(bank(b, 256 + n - P, 256 + n), ident, cst("causal"), True, False, skip=True)
                t = mm(bank(b, 256, 256 + n), row_of(h, 8), g[:, 0:n], False, True, tg_, inc=True, skip=True)
                return b, t

            def soft(u, s):
                qt, h, i = u
                b, t = s
                n = (qt + 1) * P
                sbf, dbf = Sb[i % 3][:, 0:n], Db[i % 2][:, 0:n]
                t = act(dbf, bank(b, 256, 256 + n), ACTF.Exp, t, st.get(("d", i % 2)), t_nm,
                        bias=nm[:, qt * 16 + h:qt * 16 + h + 1])
                t = DVE.do(lambda e: e.scalar_tensor_tensor(out=sbf, in0=bank(b, 0, n), scalar=INV, in1=dbf,
                                                            op0=ALU.mult, op1=ALU.mult,
                                                            accum_out=den[:, i:i + 1]), t, sfree[0][i % 3])
                PS.give(b, t)
                st[("d", i % 2)] = t
                stt(rd[:, i:i + 1], den[:, i:i + 1], -1.0, den[:, i:i + 1], ALU.mult, ALU.max)
                tt(rd[:, i:i + 1], rd[:, i:i + 1], em[:, qt * 16 + 8 + h:qt * 16 + 9 + h], ALU.max, t_em)
                recip(rd[:, i:i + 1], rd[:, i:i + 1])
                t = ts(sbf, sbf, rd[:, i:i + 1], None, ALU.mult)
                return sbf, t

            def value(u, pt, tok):
                qt, h, i = u
                bb = 4 + (h // 2) % 2
                lo = (h % 2) * 256 + qt * P
                for kt in range(qt + 1):
                    t = mm(bank(bb, lo, lo + P), vt[:, kt, h * P:(h + 1) * P], pt[:, kt * P:(kt + 1) * P],
                           kt == 0, kt == qt, tok, tv, acc_free[0], hfree[(h // 2) % 2], inc=(kt == qt))
                if h % 2 and qt:
                    hfree[(h // 2) % 2] = tt(hout[:, h - 1:h + 1, :], og[:, h - 1:h + 1, :], v3(bank(bb), 2),
                                             ALU.mult, t, to)
                return t

            attend(units, scores, soft, lambda u: u[0] + 1, value, pts)
            acc_free[0] = acc_free[0] + [DVE.last(), ACT.last()]
            tsp = []
            for x in range(0, 8, 4):
                tsp.append(split(gh[:, x:x + 4, :], gl[:, x:x + 4, :], hout[:, x:x + 4, :], DVE.last()))
            for s in range(8):
                t = down("odd_w_out_2", (0,), s * P, gh[:, s, :], gl[:, s, :], s == 0, s == 7, tsp[s // 4])
            return t

        def moe(l, xtok):
            spread = v3(take(4096), 16)
            bt = [None]
            weigh = route(l, xtok, spread, bt)
            next(weigh)
            side.append(weigh)
            return gated([(("moe_w_gate_2", (l, e), 0), ("moe_w_up_2", (l, e), 0),
                           ("moe_w_down_2", (l, e), 0), ("moe_w_down_2", (l, e), P))
                          for e in range(16)], xtok, spread, weigh, bt)

        def route(l, xtok, spread, bt):
            lg = v3(SM[:, 600:640], 2)
            b, waits = PS.take()
            wr = v3(par("wr", l * 160, 160), 8)
            for m in range(2):
                for k in range(8):
                    t = mm(bank(b, m * 20, m * 20 + 20), xt[:, k, m * P:(m + 1) * P], wr[:, k, :], k == 0, k == 7,
                           waits, xtok[k], inc=(m == 1 and k == 7))
            yield
            t = tt(lg, v3(bank(b, 0, 40), 2), rep(par("rb", l * 20, 20), 2), ALU.add, t)
            PS.give(b, t)
            at = [640]

            def s_(n):
                at[0] += n
                return SM[:, at[0] - n:at[0]]

            gl = lg[:, :, 0:4]
            el = lg[:, :, 4:20].rearrange("p m (g e) -> p m g e", g=4)
            m1, g4, ex, sm_, oh, gv = s_(2), v3(s_(8), 2), v3(s_(8), 2), s_(2), v3(s_(8), 2), s_(2)
            wt = cst("firsts", 0, 4)

            def onehot(o, x, mxv):
                tt(o, x, wide(mxv, 4), ALU.is_equal)
                tt(o, o, rep(order, 2), ALU.mult)
                red(m1, o, ALU.max)
                tt(o, o, wide(m1, 4), ALU.is_equal)

            order = s_(4)
            for x in range(4):
                DVE.do(lambda e, x=x: e.memset(order[:, x:x + 1], float(4 - x)))
            mg = s_(2)
            red(mg, gl, ALU.max)
            tt(g4, gl, wide(mg, 4), ALU.subtract)
            yield
            t = act(ex, g4, ACTF.Exp, DVE.last())
            onehot(oh, gl, mg)
            yield
            red(sm_, ex, ALU.add, t)
            recip(gv, sm_)
            yield
            sel = v4(s_(32), 2, 4)
            es = v3(s_(8), 2)
            for m in range(2):
                tt(sel[:, m], el[:, m], wide(oh[:, m, :], 4), ALU.mult)
                red(es[:, m, :], sel[:, m].rearrange("p g e -> p e g"), ALU.add)
            e1, o1, o2, l2, e2, p2, w1, w2 = s_(2), v3(s_(8), 2), v3(s_(8), 2), v3(s_(8), 2), s_(2), s_(2), s_(2), s_(2)
            yield
            red(e1, es, ALU.max)
            onehot(o1, es, e1)
            yield
            stt(l2, o1, -3.0e38, es, ALU.mult, ALU.add)
            red(e2, l2, ALU.max)
            tt(p2, e2, e1, ALU.subtract)
            t3 = DVE.last()
            onehot(o2, l2, e2)
            yield
            t = act(p2, p2, ACTF.Exp, t3)
            yield
            ts(w1, p2, 1.0, None, ALU.add, None, t)
            recip(w1, w1)
            tt(w1, w1, gv, ALU.mult)
            tt(w2, w1, p2, ALU.mult)
            tt(o1, o1, wide(w1, 4), ALU.mult)
            tt(o2, o2, wide(w2, 4), ALU.mult)
            tt(o1, o1, o2, ALU.add)
            yield
            comb = v4(s_(32), 2, 4)
            for m in range(2):
                for g_ in range(4):
                    t = ts(comb[:, m, g_, :], o1[:, m, :], oh[:, m, g_:g_ + 1], None, ALU.mult)
            yield
            b, waits = PS.take()
            for m in range(2):
                t2 = tr(bank(b, m * P, m * P + P, p=16), comb[:, m].rearrange("p g e -> p (g e)"), P, waits, t,
                        inc=(m == 1))
            yield
            cT = take(256)[0:16, :]
            t = cp(cT, bank(b, 0, 256, p=16), t2, q=ACT)
            PS.give(b, t)
            yield
            for e_ in range(0, 16, 2):
                b, waits = PS.take()
                for x in range(2):
                    t2 = mm(bank(b, x * 256, x * 256 + 256), row_of(e_ + x, 16), cT, True, True, waits, t,
                            inc=(x == 1))
                tb = cp(spread[:, e_:e_ + 2, :], v3(bank(b), 2), t2, q=ACT)
                PS.give(b, tb)
                yield
            bt[0] = tb

        mixers = [hybrid, dilated, fox, mlstm]
        s5_state = {}
        for n in range(8):
            fence()
            l = n // 2 % 2
            rate[0] = (1.0, 0.5, 0.6, 0.2, 0.0, 0.0, 0.0, 0.0)[n]
            if n < 4:
                htok = pre(n, xtok)
                if n == 0:
                    top[0] = ARENA
                if n == 3:
                    setup = slowly(s5_setup(s5_state), 5)
                    side.append(setup)
                yt = ffn(l, htok) if n % 2 else mixers[l](htok)
                if n == 3:
                    drain(setup)
                xtok = post(n, yt)
            else:
                yt = moe(l, xtok) if n % 2 else mixers[2 + l](xtok)
                top[0] = ARENA
                xtok = layer_norm(n - 4, yt)

        fence()
        ov = take(2048)
        for m in range(2):
            for j in range(0, 8, 4):
                b, waits = PS.take()
                for jj in range(4):
                    t = tr(bank(b, jj * P, jj * P + P), xt[:, j + jj, m * P:(m + 1) * P], P, waits,
                           xtok[j + jj], inc=(jj == 3))
                t = cp(ov[:, m * 1024 + j * P:m * 1024 + (j + 4) * P], bank(b), t, q=(ACT if m else None))
                PS.give(b, t)
            SP.do(lambda e, m=m: e.dma_start(out[m * P:(m + 1) * P, :], ov[:, m * 1024:(m + 1) * 1024])
                  .then_inc(s_out, 16), t, inc=False)

        block = ctx.enter_context(nc.Block())

        @block.sync
        def _(eng):
            SP.emit(eng)
            eng.wait_ge(s_out, 32)

        @block.tensor
        def _(eng):
            PE.emit(eng)

        @block.scalar
        def _(eng):
            ACT.emit(eng)

        @block.vector
        def _(eng):
            DVE.emit(eng)

        @block.gpsimd
        def _(eng):
            POOL.emit(eng)


def shape_constants():
    c = np.zeros((P, CN), np.float32)
    i = np.arange(P)

    def put(name, v):
        at, n = CO[name]
        c[:, at:at + n] = v

    put("ident", np.eye(P))
    put("onesd", 1.0 / D)
    put("causal", np.where(i[None, :] <= i[:, None], 0.0, NEG))
    hm = []
    for h in (1, 2, 4, 8, 16, 32, 64):
        s, t = i[:, None], i[None, :]
        hm.append((s // (2 * h) == t // (2 * h)) & (s % (2 * h) < h) & (t % (2 * h) >= h))
    put("hm", np.concatenate(hm, 1))
    hs = np.zeros((P, 4, 4))
    for h in range(4):
        hs[:, h, h] = 1.0 / 128.0
    put("hsel", hs.reshape(P, 16))
    put("tt", np.arange(256)[None, :])
    put("half", np.stack([np.full(P, math.pi / 2), 1.0 - (i // 16) % 2], 1))
    put("firsts", np.stack([(i // 16) % 2] * 4, 1))

    x = np.zeros((P, AN), np.float32)
    inv = np.stack([1.0 / np.minimum(np.arange(256) + 1, w) for w in (2, 4, 8, 16)]).reshape(-1)
    x[:, 0:1024] = inv[None, :]
    d = np.arange(384) - 127
    dd = np.maximum(d, 0).astype(np.int64)
    df = np.maximum(dd, 1).astype(np.float32)
    large = 16 + (np.log(df / np.float32(16)).astype(np.float32) / np.float32(math.log(2048 / 16))
                  * np.float32(16)).astype(np.int32)
    bucket = np.where(dd < 16, dd, np.minimum(large, 31))
    x[0:32, 1024:1408] = (bucket[None, :] == np.arange(32)[:, None])
    ok = np.stack([(d >= 0) & (d <= 128), (d >= 0) & (d % 4 == 0), (d >= 0) & (d % 16 == 0)])
    x[0:24, 1408:1792] = np.where(np.repeat(ok, 8, 0), 0.0, NEG)
    return c, x


_BIG = ["ada_w", "ffn_w_in", "ffn_w_out", "hyb_w_in", "hyb_w_out", "pool_w", "att_w_qkv", "att_w_out",
        "even_w_in_2", "s5_w_glu_2", "even_w_out_2", "odd_w_in_2", "odd_w_out_2",
        "moe_w_gate_2", "moe_w_up_2", "moe_w_down_2"]


def kernel(**inputs):
    import concourse.bacc as bacc
    from concourse.bass_utils import run_bass_kernel_spmd

    f = {k: np.asarray(v) for k, v in inputs.items()}

    def cols(v):
        return np.asarray(v).reshape(-1, P).T

    def on8(v):
        r = np.zeros((P, 1), np.float32)
        r[0:8, 0] = v.reshape(-1)
        return r

    pr = np.zeros((P, PN), np.float32)

    def put(name, v):
        at, n = PO[name]
        pr[:, at:at + n] = v

    put("c", cols(f["c"]))
    put("npre", cols(f["norm_pre"]))
    put("npost", cols(f["norm_post"]))
    put("adab", cols(f["ada_b"]))
    put("pscale", cols(f["pool_scale"]))
    put("lbl", cols(f["hgrn_lb_logits"]))
    put("onorm", cols(f["hgrn_out_norm"]))
    put("lng", cols(f["ln_g_2"]))
    put("lnb", cols(f["ln_b_2"]))
    put("are", cols(f["s5_a_re_2"]))
    put("aim", cols(f["s5_a_im_2"]))
    put("ldt", cols(np.repeat(f["s5_log_dt_2"].reshape(-1), 64)))
    put("s5d", cols(f["s5_d_2"]))
    put("bglu", cols(f["s5_b_glu_2"]))
    put("convw", cols(f["mlstm_conv_w_2"]))
    put("convb", cols(f["mlstm_conv_b_2"]))
    rb = np.concatenate([f["moe_b_group_2"], f["moe_b_expert_2"].reshape(2, 16)], 1).reshape(1, 40)
    put("rb", np.broadcast_to(rb, (P, 40)))
    put("fb", np.concatenate([on8(f["fox_f_bias_2"]), on8(f["mlstm_i_bias_2"]), on8(f["mlstm_f_bias_2"])], 1))
    for n, s in (("bre", "s5_b_re_2"), ("bim", "s5_b_im_2")):
        put(n, f[s].reshape(16, P, 16).transpose(1, 0, 2).reshape(P, 256))
    for n, s in (("cre", "s5_c_re_2"), ("cim", "s5_c_im_2")):
        put(n, f[s].reshape(4, P, 64).transpose(1, 0, 2).reshape(P, 256))
    wr = np.concatenate([f["moe_w_group_2"].reshape(2, 8, P, 4),
                         f["moe_w_expert_2"].reshape(2, 4, 8, P, 4).transpose(0, 2, 3, 1, 4).reshape(2, 8, P, 16)], 3)
    put("wr", wr.transpose(2, 0, 1, 3).reshape(P, 320))
    ct, ax = shape_constants()
    at = AO["relb"][0]
    ax[0:32, at:at + 24] = f["rel_bias"]

    nc = bacc.Bacc("TRN2", target_bir_lowering=False, num_devices=1)
    arrays = {"params": pr, "consts": ct, "aux": ax, "x": np.ascontiguousarray(f["x"].reshape(S, D))}
    for n in _BIG:
        arrays[n] = np.ascontiguousarray(f[n])
    aps = {n: nc.dram_tensor(n, v.shape, mybir.dt.from_np(v.dtype), kind="ExternalInput").ap()
           for n, v in arrays.items()}
    out = nc.dram_tensor("out_x", (S, D), F32, kind="ExternalOutput").ap()
    build(nc, aps, out)
    r = run_bass_kernel_spmd(nc, [arrays], core_ids=[0])
    return r.results[0]["out_x"].reshape(1, S, D)
```
